# Optimizing a Trainium2 kernel written in Bass

```python
import math
import jax, jax.numpy as jnp
from jax import lax
import numpy as np

D_MODEL = 1024
BATCH = 1
SEQ = 512
DEPTH = 2

MEM_LEN = 256
Q_BLOCK = 128
NSA_Q_BLOCK = 32
N_BUCKETS = 32
MAX_DISTANCE = 128
RMS_EPS = 1e-6
ROPE_THETA = 10000.0
NEG_INF = -1e30
D_FF = 2816
A_HEADS = 8
A_KV = 2
A_GRP = A_HEADS // A_KV
A_DH = 64
CMP_LEN = 32
CMP_STRIDE = 16
SLC_LEN = 64
SLC_TOP = 16
WIN = 512
FORCE_BONUS = 1e3
B_HEADS = 8
B_DH = 64
IDX_HEADS = 8
IDX_DH = 32
IDX_TOPK_MAX = 256
C_HEADS = 8
C_Q_RANK = 256
C_KV_RANK = 128
C_DN = 64
C_DR = 32
C_DV = 64
D_HEADS = 4
D_DH = 64
D_DV = 128
X_HEADS = 4
X_DH = 128
N_BIAS_HEADS = A_HEADS + B_HEADS + D_HEADS

EV_SIZES = (A_HEADS * A_DH, 6 * A_KV * A_DH, 3 * A_HEADS,
            B_HEADS * B_DH, B_DH, B_DH, IDX_HEADS * IDX_DH, IDX_DH, IDX_HEADS)
EV_IN = sum(EV_SIZES)
EV_OUT = A_HEADS * A_DH + B_HEADS * B_DH
OD_SIZES = (C_Q_RANK, C_KV_RANK, C_DR, D_HEADS * 2 * D_DH, D_HEADS * 2 * D_DH, D_HEADS * D_DV)
OD_IN = sum(OD_SIZES)
OD_OUT = C_HEADS * C_DV + D_HEADS * D_DV

kernel_name = 'hybrid_nsa_dsa_mla_diff_macaron_block'

def rmsnorm(x, g):
    x32 = x.astype(jnp.float32)
    y = x32 * lax.rsqrt(jnp.mean(x32 * x32, axis=-1, keepdims=True) + RMS_EPS)
    return (y * g.astype(jnp.float32)).astype(x.dtype)

def swiglu(h, wg, wu, wd):
    return (jax.nn.silu(h @ wg) * (h @ wu)) @ wd

def split_cols(p, sizes):
    return jnp.split(p, [int(c) for c in np.cumsum(sizes)[:-1]], axis=-1)

def masked_softmax(logits, mask):
    p = jax.nn.softmax(jnp.where(mask, logits, NEG_INF), axis=-1)
    return p * mask

def rel_bucket(dist):
    max_exact = N_BUCKETS // 2
    d = jnp.maximum(dist, 0)
    log_ratio = jnp.log(jnp.maximum(d, 1).astype(jnp.float32) / max_exact) / math.log(MAX_DISTANCE / max_exact)
    large = jnp.minimum(max_exact + (log_ratio * (N_BUCKETS - max_exact)).astype(jnp.int32), N_BUCKETS - 1)
    return jnp.where(d < max_exact, d, large)

def rel_bias(dist, tab):
    b = tab.astype(jnp.float32)[rel_bucket(dist)]
    nh = tab.ndim - 1
    return jnp.moveaxis(b, tuple(range(dist.ndim, dist.ndim + nh)), tuple(range(nh)))

def rope(x):
    S = x.shape[1]
    half = x.shape[-1] // 2
    inv = ROPE_THETA ** (-jnp.arange(half, dtype=jnp.float32) / half)
    ang = jnp.arange(S, dtype=jnp.float32)[:, None] * inv[None, :]
    shape = (S,) + (1,) * (x.ndim - 3) + (half,)
    cos, sin = jnp.cos(ang).reshape(shape), jnp.sin(ang).reshape(shape)
    x1 = x[..., :half].astype(jnp.float32)
    x2 = x[..., half:].astype(jnp.float32)
    return jnp.concatenate([x1 * cos - x2 * sin, x1 * sin + x2 * cos], axis=-1).astype(x.dtype)

def blockwise(fn, blk, *q_side):
    B, S = q_side[0].shape[:2]
    n = S // blk
    xs = tuple(jnp.moveaxis(a.reshape((B, n, blk) + a.shape[2:]), 1, 0) for a in q_side)
    out = lax.map(lambda a: fn(a[0], *a[1:]), (jnp.arange(n, dtype=jnp.int32),) + xs)
    return jnp.moveaxis(out, 0, 1).reshape((B, S) + out.shape[3:])

def gather_rows(a, idx):
    return jax.vmap(lambda ai, ii: ai[ii])(a, idx)

def nsa_mixer(q, kv6, gate_logits, tab, cmp_pe, cmp_w):
    B, S = q.shape[:2]
    q = q.reshape(B, S, A_KV, A_GRP, A_DH)
    gate_logits = gate_logits.reshape(B, S, A_KV, A_GRP, 3)
    kv6 = kv6.reshape(B, S, 6, A_KV, A_DH)
    k_c, v_c, k_s, v_s, k_w, v_w = (kv6[:, :, i] for i in range(6))
    tab_g = tab.reshape(N_BUCKETS, A_KV, A_GRP)
    scale = A_DH ** -0.5
    n_cmp = (S - CMP_LEN) // CMP_STRIDE + 1
    cmp_start = jnp.arange(n_cmp) * CMP_STRIDE
    cmp_end = cmp_start + CMP_LEN - 1
    tok = cmp_start[:, None] + jnp.arange(CMP_LEN)[None, :]
    k_cmp = jnp.einsum('bnlgd,lde->bnge', k_c[:, tok] + cmp_pe[0][:, None, :], cmp_w[0])
    v_cmp = jnp.einsum('bnlgd,lde->bnge', v_c[:, tok] + cmp_pe[1][:, None, :], cmp_w[1])
    n_sb = S // SLC_LEN
    n_top = min(SLC_TOP, n_sb)
    sb_start = jnp.arange(n_sb) * SLC_LEN
    overlap = ((cmp_start[:, None] < sb_start[None, :] + SLC_LEN)
               & (cmp_end[:, None] >= sb_start[None, :])).astype(jnp.float32)
    k_sb = k_s.reshape(B, n_sb, SLC_LEN, A_KV, A_DH).transpose(0, 3, 1, 2, 4)
    v_sb = v_s.reshape(B, n_sb, SLC_LEN, A_KV, A_DH).transpose(0, 3, 1, 2, 4)
    k_wp = jnp.pad(k_w, ((0, 0), (WIN, 0), (0, 0), (0, 0)))
    v_wp = jnp.pad(v_w, ((0, 0), (WIN, 0), (0, 0), (0, 0)))
    blk_ids = jnp.arange(n_sb)
    g_ids = jnp.arange(A_KV)[:, None, None]

    def block(qi, qb, gb):
        T = qb.shape[1]
        t = qi * T + jnp.arange(T)
        s_c = (jnp.einsum('btgrd,bngd->bgrtn', qb, k_cmp).astype(jnp.float32) * scale
               + rel_bias(t[:, None] - cmp_end[None, :], tab_g))
        p_c = masked_softmax(s_c, cmp_end[None, :] <= t[:, None])
        o_c = jnp.einsum('bgrtn,bngd->btgrd', p_c.astype(v_cmp.dtype), v_cmp)
        imp = jnp.einsum('bgrtn,nj->bgtj', p_c, overlap)
        cur = (t // SLC_LEN)[:, None]
        forced = (blk_ids == 0) | (blk_ids == cur) | (blk_ids == cur - 1)
        score = jnp.where(blk_ids <= cur, imp + FORCE_BONUS * forced, NEG_INF)
        _, sel = lax.top_k(score, n_top)
        k_sel = jax.vmap(gather_rows)(k_sb, sel).reshape(B, A_KV, T, n_top * SLC_LEN, A_DH)
        v_sel = jax.vmap(gather_rows)(v_sb, sel).reshape(B, A_KV, T, n_top * SLC_LEN, A_DH)
        pos = (sel[..., None] * SLC_LEN + jnp.arange(SLC_LEN)).reshape(B, A_KV, T, n_top * SLC_LEN)
        dist = t[:, None] - pos
        bias_s = jnp.moveaxis(tab_g.astype(jnp.float32)[rel_bucket(dist), g_ids], -1, 2)
        s_s = jnp.einsum('btgrd,bgtkd->bgrtk', qb, k_sel).astype(jnp.float32) * scale + bias_s
        p_s = masked_softmax(s_s, (dist >= 0)[:, :, None])
        o_s = jnp.einsum('bgrtk,bgtkd->btgrd', p_s.astype(v_sel.dtype), v_sel)
        k_win = lax.dynamic_slice_in_dim(k_wp, qi * T, T + WIN, axis=1)
        v_win = lax.dynamic_slice_in_dim(v_wp, qi * T, T + WIN, axis=1)
        s_pos = qi * T - WIN + jnp.arange(T + WIN)
        dist_w = t[:, None] - s_pos[None, :]
        vis_w = (dist_w >= 0) & (dist_w < WIN) & (s_pos[None, :] >= 0)
        s_w = (jnp.einsum('btgrd,bsgd->bgrts', qb, k_win).astype(jnp.float32) * scale
               + rel_bias(dist_w, tab_g))
        p_w = masked_softmax(s_w, vis_w)
        o_w = jnp.einsum('bgrts,bsgd->btgrd', p_w.astype(v_win.dtype), v_win)
        g = jax.nn.sigmoid(gb.astype(jnp.float32))
        o = g[..., 0:1] * o_c + g[..., 1:2] * o_s + g[..., 2:3] * o_w
        return o.astype(qb.dtype)

    out = blockwise(block, NSA_Q_BLOCK, q, gate_logits)
    return out.reshape(B, S, A_HEADS * A_DH)

def dsa_mixer(q, k, v, iq, ik, iw, tab):
    B, S = q.shape[:2]
    k_top = min(IDX_TOPK_MAX, S // 4)
    q = q.reshape(B, S, B_HEADS, B_DH)
    iq = iq.reshape(B, S, IDX_HEADS, IDX_DH)
    scale = B_DH ** -0.5
    key_pos = jnp.arange(S)

    def block(qi, qb, iqb, iwb):
        T = qb.shape[1]
        t = qi * T + jnp.arange(T)
        idx_logit = jax.nn.relu(jnp.einsum('bthd,bsd->bths', iqb, ik).astype(jnp.float32))
        idx_score = jnp.einsum('bth,bths->bts', iwb.astype(jnp.float32), idx_logit)
        idx_score = jnp.where(key_pos[None, :] <= t[:, None], idx_score, NEG_INF)
        _, sel = lax.top_k(idx_score, k_top)
        k_sel = gather_rows(k, sel)
        v_sel = gather_rows(v, sel)
        dist = t[:, None] - sel
        s = (jnp.einsum('bthd,btkd->bhtk', qb, k_sel).astype(jnp.float32) * scale
             + jnp.moveaxis(tab.astype(jnp.float32)[rel_bucket(dist)], -1, 1))
        p = masked_softmax(s, (dist >= 0)[:, None])
        o = jnp.einsum('bhtk,btkd->bthd', p.astype(v_sel.dtype), v_sel)
        return o.reshape(B, T, B_HEADS * B_DH)

    return blockwise(block, Q_BLOCK, q, iq, iw)

def mla_mixer(c_q, c_kv, k_rope, q_norm, kv_norm, w_uq, w_ukv):
    B, S = c_q.shape[:2]
    q = (rmsnorm(c_q, q_norm) @ w_uq).reshape(B, S, C_HEADS, C_DN + C_DR)
    q_nope, q_rope = q[..., :C_DN], rope(q[..., C_DN:])
    kv = (rmsnorm(c_kv, kv_norm) @ w_ukv).reshape(B, S, C_HEADS, C_DN + C_DV)
    k_nope, v = kv[..., :C_DN], kv[..., C_DN:]
    k_r = rope(k_rope)
    scale = (C_DN + C_DR) ** -0.5
    key_pos = jnp.arange(S)

    def block(qi, qn, qr):
        T = qn.shape[1]
        t = qi * T + jnp.arange(T)
        s = (jnp.einsum('bthd,bshd->bhts', qn, k_nope)
             + jnp.einsum('bthd,bsd->bhts', qr, k_r)).astype(jnp.float32) * scale
        p = masked_softmax(s, key_pos[None, :] <= t[:, None])
        o = jnp.einsum('bhts,bshd->bthd', p.astype(v.dtype), v)
        return o.reshape(B, T, C_HEADS * C_DV)

    return blockwise(block, Q_BLOCK, q_nope, q_rope)

def diff_mixer(q, k, v, lam, subln, tab, lam_init):
    B, S = q.shape[:2]
    q = q.reshape(B, S, D_HEADS, 2, D_DH)
    k = k.reshape(B, S, D_HEADS, 2, D_DH)
    v = v.reshape(B, S, D_HEADS, D_DV)
    lam32 = lam.astype(jnp.float32)
    lam_full = jnp.exp(jnp.sum(lam32[0] * lam32[1])) - jnp.exp(jnp.sum(lam32[2] * lam32[3])) + lam_init
    scale = D_DH ** -0.5
    key_pos = jnp.arange(S)

    def block(qi, qb):
        T = qb.shape[1]
        t = qi * T + jnp.arange(T)
        dist = t[:, None] - key_pos[None, :]
        s = jnp.einsum('bthed,bshed->behts', qb, k).astype(jnp.float32) * scale + rel_bias(dist, tab)
        p = masked_softmax(s, dist >= 0)
        a = p[:, 0] - lam_full * p[:, 1]
        o = jnp.einsum('bhts,bshd->bthd', a.astype(v.dtype), v)
        o = rmsnorm(o, subln) * (1.0 - lam_init)
        return o.reshape(B, T, D_HEADS * D_DV)

    return blockwise(block, Q_BLOCK, q)

def mem_xattn(h, m, wq, wkv, wo):
    B, S = h.shape[:2]
    q = (h @ wq).reshape(B, S, X_HEADS, X_DH)
    kv = (m @ wkv).reshape(B, m.shape[1], 2, X_HEADS, X_DH)
    k, v = kv[:, :, 0], kv[:, :, 1]
    s = jnp.einsum('bshd,bmhd->bhsm', q, k).astype(jnp.float32) * X_DH ** -0.5
    p = jax.nn.softmax(s, axis=-1)
    o = jnp.einsum('bhsm,bmhd->bshd', p.astype(v.dtype), v)
    return o.reshape(B, S, X_HEADS * X_DH) @ wo

def even_mixer(h, w_in, w_out, cmp_pe, cmp_w, rel_tab):
    qa, kva, ga, qb, kb, vb, iq, ik, iw = split_cols(h @ w_in, EV_SIZES)
    o_a = nsa_mixer(qa, kva, ga, rel_tab[:, :A_HEADS], cmp_pe, cmp_w)
    o_b = dsa_mixer(qb, kb, vb, iq, ik, iw, rel_tab[:, A_HEADS:A_HEADS + B_HEADS])
    return jnp.concatenate([o_a, o_b], axis=-1) @ w_out

def odd_mixer(h, w_in, w_out, q_norm, kv_norm, w_uq, w_ukv, lam, subln, rel_tab, lam_init):
    c_q, c_kv, k_rope, qd, kd, vd = split_cols(h @ w_in, OD_SIZES)
    o_c = mla_mixer(c_q, c_kv, k_rope, q_norm, kv_norm, w_uq, w_ukv)
    o_d = diff_mixer(qd, kd, vd, lam, subln, rel_tab[:, A_HEADS + B_HEADS:], lam_init)
    return jnp.concatenate([o_c, o_d], axis=-1) @ w_out

def setup_inputs(seed: int = 0) -> dict:
    key = jax.random.key(seed)
    ks = jax.random.split(key, 24)
    n_even = (DEPTH + 1) // 2
    n_odd = DEPTH // 2
    f32 = jnp.float32

    def dense(k, shape, fan_in):
        return jax.random.normal(k, shape, f32) * fan_in ** -0.5

    def gain(k, shape):
        return 1.0 + 0.05 * jax.random.normal(k, shape, f32)

    return {
        'x': jax.random.normal(ks[0], (BATCH, SEQ, D_MODEL), f32),
        'mem': jax.random.normal(ks[1], (BATCH, MEM_LEN, D_MODEL), f32),
        'rel_bias_table': 0.2 * jax.random.normal(ks[2], (N_BUCKETS, N_BIAS_HEADS), f32),
        'norm_pre': gain(ks[3], (DEPTH, 4, D_MODEL)),
        'norm_post': gain(ks[4], (DEPTH, 4, D_MODEL)),
        'mem_norm': gain(ks[5], (DEPTH, D_MODEL)),
        'ffn_wg': dense(ks[6], (DEPTH, 2, D_MODEL, D_FF), D_MODEL),
        'ffn_wu': dense(ks[7], (DEPTH, 2, D_MODEL, D_FF), D_MODEL),
        'ffn_wd': dense(ks[8], (DEPTH, 2, D_FF, D_MODEL), D_FF),
        'ev_w_in': dense(ks[9], (n_even, D_MODEL, EV_IN), D_MODEL),
        'ev_cmp_pe': 0.5 * jax.random.normal(ks[10], (n_even, 2, CMP_LEN, A_DH), f32),
        'ev_cmp_w': dense(ks[11], (n_even, 2, CMP_LEN, A_DH, A_DH), CMP_LEN * A_DH),
        'ev_w_out': dense(ks[12], (n_even, EV_OUT, D_MODEL), EV_OUT),
        'od_w_in': dense(ks[13], (n_odd, D_MODEL, OD_IN), D_MODEL),
        'od_q_norm': gain(ks[14], (n_odd, C_Q_RANK)),
        'od_kv_norm': gain(ks[15], (n_odd, C_KV_RANK)),
        'od_w_uq': dense(ks[16], (n_odd, C_Q_RANK, C_HEADS * (C_DN + C_DR)), C_Q_RANK),
        'od_w_ukv': dense(ks[17], (n_odd, C_KV_RANK, C_HEADS * (C_DN + C_DV)), C_KV_RANK),
        'od_lambda': 0.1 * jax.random.normal(ks[18], (n_odd, 4, D_DH), f32),
        'od_subln': gain(ks[19], (n_odd, D_DV)),
        'od_w_out': dense(ks[20], (n_odd, OD_OUT, D_MODEL), OD_OUT),
        'xa_wq': dense(ks[21], (DEPTH, D_MODEL, X_HEADS * X_DH), D_MODEL),
        'xa_wkv': dense(ks[22], (DEPTH, D_MODEL, 2 * X_HEADS * X_DH), D_MODEL),
        'xa_wo': dense(ks[23], (DEPTH, X_HEADS * X_DH, D_MODEL), X_HEADS * X_DH),
    }

def reference(x, mem, rel_bias_table, norm_pre, norm_post, mem_norm, ffn_wg, ffn_wu, ffn_wd,
              ev_w_in, ev_cmp_pe, ev_cmp_w, ev_w_out, od_w_in, od_q_norm, od_kv_norm, od_w_uq,
              od_w_ukv, od_lambda, od_subln, od_w_out, xa_wq, xa_wkv, xa_wo):
    for i in range(DEPTH):
        g_pre, g_post = norm_pre[i], norm_post[i]
        h = rmsnorm(x, g_pre[0])
        x = x + 0.5 * rmsnorm(swiglu(h, ffn_wg[i, 0], ffn_wu[i, 0], ffn_wd[i, 0]), g_post[0])
        h = rmsnorm(x, g_pre[1])
        if i % 2 == 0:
            e = i // 2
            y = even_mixer(h, ev_w_in[e], ev_w_out[e], ev_cmp_pe[e], ev_cmp_w[e], rel_bias_table)
        else:
            o = i // 2
            lam_init = 0.8 - 0.6 * math.exp(-0.3 * i)
            y = odd_mixer(h, od_w_in[o], od_w_out[o], od_q_norm[o], od_kv_norm[o], od_w_uq[o],
                          od_w_ukv[o], od_lambda[o], od_subln[o], rel_bias_table, lam_init)
        x = x + rmsnorm(y, g_post[1])
        h = rmsnorm(x, g_pre[2])
        m = rmsnorm(mem, mem_norm[i])
        x = x + rmsnorm(mem_xattn(h, m, xa_wq[i], xa_wkv[i], xa_wo[i]), g_post[2])
        h = rmsnorm(x, g_pre[3])
        x = x + 0.5 * rmsnorm(swiglu(h, ffn_wg[i, 1], ffn_wu[i, 1], ffn_wd[i, 1]), g_post[3])
    return x


_drawn_inputs = setup_inputs


def setup_inputs(seed=0):
    import zlib

    import numpy as np

    out = dict(_drawn_inputs(seed))
    spreads = {}
    factors = {'od_q_norm': 8.0, 'od_kv_norm': 3.786, 'od_subln': 14.03}
    for name, (base, spread) in spreads.items():
        noise = np.random.default_rng([zlib.crc32(name.encode()), seed]).standard_normal(out[name].shape)
        drawn = base * np.exp(spread * noise) if base else spread * noise
        out[name] = __import__('jax').numpy.asarray(drawn.astype(out[name].dtype))
    for name, factor in factors.items():
        out[name] = (out[name] * factor).astype(out[name].dtype)
    return out
```

```python
import math

import numpy as np
import concourse.bass as bass
from concourse import mybir

F32, F32R, BF16, I32 = mybir.dt.float32, mybir.dt.float32r, mybir.dt.bfloat16, mybir.dt.int32
ACT, ALU = mybir.ActivationFunctionType, mybir.AluOpType

P = 128
D, T, MEM, DFF, DEPTH = 1024, 512, 256, 2816, 2
KC = D // P
NT = T // P
MT = MEM // P
FC = DFF // P
BUCKETS, MAX_DIST = 32, 128
A_HEADS, B_HEADS, C_HEADS, D_HEADS, X_HEADS = 8, 8, 8, 4, 4
BIAS_HEADS = A_HEADS + B_HEADS + D_HEADS
DH, IDX_HEADS, IDX_DH, TOPK = 64, 8, 32, 128
CMP_LEN, CMP_STRIDE = 32, 16
N_CMP = (T - CMP_LEN) // CMP_STRIDE + 1
DN, DR, DV = 64, 32, 128
EPS = 1e-6
NEG = -1e30
TAKEN = -3e38
LAM_INIT = 0.8 - 0.6 * math.exp(-0.3)
LINE = T + P - 1
RSQRT_SEED = float(0x5F3759DF)

R = 4
DOWN_TILES = (8, 7, 7)
EV_IN, OD_IN = 19, 16
IQ, IK, VG, KB, QB, KCMP, VCMP, KS, VS, KW, VW, QA = 0, 2, 3, 4, 5, 9, 10, 11, 12, 13, 14, 15
CQ, CKV, KR, DQ, DK, DVT = 0, 2, 3, 4, 8, 12

C_ID, C_CAUSAL, C_ROPE, C_END = 0, P, P + T, P + 2 * T
G_PRE, G_POST, G_MEM, G_Q, G_KV, G_SUB = 0, 64, 128, 144, 146, 147
G_END = 148


def plan():
    units, chunks, u, c = {}, {}, 0, 0
    def add(name, nu, nc_):
        nonlocal u, c
        units[name], chunks[name] = u, c
        u, c = u + nu, c + nc_
    def ffn(n):
        add(f"up{n}", 2 * FC, 2 * FC)
        add(f"down{n}", 3 * KC, KC)
    def cross(n):
        add(f"xq{n}", X_HEADS, X_HEADS)
        add(f"xkv{n}", 2 * X_HEADS, 2 * X_HEADS)
        add(f"xo{n}", KC // 2, KC)
    ffn(0)
    add("ev_in", EV_IN, EV_IN)
    add("ev_out", KC, KC)
    cross(0)
    ffn(1)
    ffn(2)
    add("od_in", OD_IN, OD_IN)
    add("uq", 2, C_HEADS)
    add("ukv", 1, 4)
    add("od_out", KC, KC)
    cross(1)
    ffn(3)
    return units, chunks, u


def attention_jobs():
    even = [(k, h, i) for h in range(A_HEADS) for i in range(NT) for k in ("cmp", "slc", "win")]
    even += [("dsa", h, i) for h in range(B_HEADS) for i in range(NT)]
    diff = [(f"diff{e}", h, i) for h in range(D_HEADS) for i in range(NT) for e in range(2)]
    mla = [("mla", h, i) for h in range(C_HEADS) for i in range(NT)]
    cross = [("x", h, i) for h in range(X_HEADS) for i in range(NT)]
    return [even, cross, diff, mla, cross]


def build(nc, a):
    UNIT, CHUNK, N_UNITS = plan()
    JOBS = attention_jobs()
    JOB0 = [sum(len(j) for j in JOBS[:n]) for n in range(len(JOBS))]

    base = -(-nc.sbuf_base // 32) * 32

    class Region:
        def __init__(self, at):
            self.at = at

        def put(self, name, shape, dt):
            size = int(np.prod(shape[1:])) * (2 if dt == BF16 else 4)
            t = nc.alloc_sbuf_tensor_at(name, shape, dt, offset=self.at)
            self.at += -(-size // 32) * 32
            assert self.at <= nc.sbuf_usable_end, (name, self.at)
            return t

    keep = Region(base)
    x = keep.put("x_res", [P, KC, T], F32)
    raw = [keep.put(f"w_raw{j}", [P, KC * P], F32) for j in range(R)]
    w_hi = [keep.put(f"w_hi{j}", [P, KC * P], F32R) for j in range(R)]
    w_lo = [keep.put(f"w_lo{j}", [P, KC * P], F32R) for j in range(R)]
    at_h = keep.at
    h_hi = keep.put("h_hi", [P, KC, T], F32R)
    h_lo = keep.put("h_lo", [P, KC, T], F32R)
    y_ffn = Region(at_h).put("y_ffn", [P, KC, T], F32)
    r_sb = keep.put("r_tok", [P, T], F32)
    sq = [keep.put(f"sq{j}", [P, T], F32) for j in range(2)]
    sq_sum = keep.put("sq_sum", [P, T], F32)
    step = [keep.put(f"step{j}", [P, T], F32) for j in range(2)]
    gains = keep.put("gains", [P, G_END], F32)
    ident = keep.put("ident", [P, P], F32)
    ident_bf = keep.put("ident_bf", [P, P], BF16)
    ones = keep.put("ones", [P, 1], F32)
    zero = keep.put("zero", [P, 1], F32)
    row_ok = keep.put("row_ok", [P, 1], F32)
    rs = keep.put("rsqrt_tmp", [P, 4, 16], F32)
    lam = keep.put("lam", [P, 8], F32)
    neg_max = keep.put("neg_max", [P, 8], F32)
    row_sum = keep.put("row_sum", [P, 8], F32)
    coef = keep.put("coef", [P, 8], F32)
    at_var = keep.at

    m = Region(at_var)
    act_hi = m.put("act_hi", [P, FC, T], F32R)
    act_lo = m.put("act_lo", [P, FC, T], F32R)
    gate = [m.put(f"gate{j}", [P, T], F32) for j in range(2)]
    up = [m.put(f"up{j}", [P, T], F32) for j in range(2)]

    def attention_buffers(m, tag):
        return ([m.put(f"{tag}_logit{j}", [P, T], F32) for j in range(3)],
                [m.put(f"{tag}_prob{j}", [P, T], F32) for j in range(3)],
                [m.put(f"{tag}_probT{j}", [P, T], F32) for j in range(2)])

    m = Region(at_var)
    ev = m.put("ev_proj", [P, EV_IN, T], F32)
    ev_v = m.put("ev_v_rows", [P, 3, NT, P], F32)
    gates = m.put("gates", [P, NT, 3 * A_HEADS], F32)
    kcT = m.put("k_cmpT", [P, 32], F32)
    vc = m.put("v_cmp", [P, P], F32)
    at = m.at
    ev_bufs = attention_buffers(m, "ev")
    cmp_w = Region(at).put("cmp_w", [P, 2, CMP_LEN, DH], F32)
    taken_mask = m.put("sel_mask", [P, NT - 1, T], BF16)
    ev_strip = [m.put(f"ev_strip{j}", [P, T], F32) for j in range(3)]
    cmp_pe = m.put("cmp_pe", [P, 2, CMP_LEN], F32)
    ev_causal = m.put("ev_causal", [P, T], F32)
    top8 = m.put("top8", [P, 8], F32)
    at = m.at
    ev_o = m.put("ev_o", [P, NT, D], F32)
    n = Region(at)
    score = [n.put(f"score{j}", [P, T], F32) for j in range(3)]
    relu = [n.put(f"relu{j}", [P, T], F32) for j in range(2)]
    ev_y = Region(at).put("ev_y", [P, KC, T], F32)
    cmp_x = Region(at).put("cmp_x", [P, 2, CMP_LEN, N_CMP], F32)

    m = Region(at_var)
    at_od = m.at
    od = m.put("od_proj", [P, OD_IN, T], F32)
    at_dv = m.at
    dv = m.put("diff_v", [P, D_HEADS, NT, P], F32)
    od_bufs = attention_buffers(m, "od")
    cq_hi = m.put("cq_hi", [P, 2, T], F32R)
    cq_lo = m.put("cq_lo", [P, 2, T], F32R)
    ckv_hi = m.put("ckv_hi", [P, T], F32R)
    ckv_lo = m.put("ckv_lo", [P, T], F32R)
    at = m.at
    od_strip = [m.put(f"od_strip{j}", [P, T], F32) for j in range(3)]
    od_causal = Region(at).put("od_causal", [P, T], F32)
    rope_t = m.put("rope_table", [P, T], F32)
    at = m.at
    od_o = m.put("od_o", [P, NT, D], F32)
    od_y = Region(at).put("od_y", [P, KC, T], F32)
    n = Region(at_od)
    mla_v = n.put("mla_v", [P, NT, T], F32)
    mla_q = n.put("mla_q", [P, C_HEADS, T], F32)
    mla_k = n.put("mla_k", [P, C_HEADS, T], F32)

    m = Region(at_var)
    mem_sb = m.put("mem_sb", [P, KC, MEM], F32)
    mem_hi = m.put("mem_hi", [P, KC, MEM], F32R)
    mem_lo = m.put("mem_lo", [P, KC, MEM], F32R)
    r_mem = m.put("r_mem", [P, MEM], F32)
    mem_sq = [m.put(f"mem_sq{j}", [P, MEM], F32) for j in range(2)]
    mem_sum = m.put("mem_sum", [P, MEM], F32)
    xq = m.put("x_q", [P, X_HEADS, T], F32)
    xkv = m.put("x_kv", [P, 2 * X_HEADS, MEM], F32)
    xv = m.put("x_v", [P, X_HEADS, MT, P], F32)
    x_bufs = attention_buffers(m, "x")
    xo = m.put("x_o", [P, NT, X_HEADS * P], F32)
    x_y = m.put("x_y", [P, KC, T], F32)

    m = Region(at_var)
    onehot = m.put("onehot", [BUCKETS + 1, LINE + 1], F32)
    table = m.put("table", [BUCKETS + 1, BIAS_HEADS], F32)
    lines = m.put("lines", [BIAS_HEADS, LINE + 1], F32)
    lam_in = m.put("lam_in", [P, 4, DH], F32)
    lam_pr = m.put("lam_pr", [P, 2, DH], F32)
    lines_dram = nc.dram_tensor("bias_lines", [BIAS_HEADS, LINE + 1], F32, kind="Internal").ap()
    line_rows = nc.dram_tensor("bias_line_rows", [BIAS_HEADS, P, LINE + 1], F32, kind="Internal").ap()

    bank = [nc.alloc_psum_tensor(f"bank{b}", [P, 512], F32) for b in range(8)]
    B_STAT, B_RT = 4, 5
    B_S, B_T, B_O = (0, 1, 2), (6, 7), (3, 4)

    sems = {}

    def sem(name):
        sems.setdefault(name, nc.alloc_semaphore(name))
        return sems[name]

    raw_loaded = [sem(f"raw_loaded{j}") for j in range(R)]
    slot_taken = sem("slot_taken")
    hi_split = sem("hi_split")
    split_done = sem("split_done")
    unit_done = sem("unit_done")
    chunk_out = sem("chunk_out")
    silu_done = sem("silu_done")
    prod_done = sem("prod_done")
    act_hi_done = sem("act_hi_done")
    act_done = sem("act_done")
    sq_done = sem("sq_done")
    sq_added = sem("sq_added")
    stat_done = sem("stat_done")
    rsqrt_done = sem("rsqrt_done")
    r_turned = sem("r_turned")
    r_copied = sem("r_copied")
    x_done = sem("x_done")
    hi_done = sem("hi_done")
    lo_done = sem("lo_done")
    dve_done = sem("dve_done")
    turned = sem("turned")
    rows_done = sem("rows_done")
    mask_done = sem("mask_done")
    cmp_x_done = sem("cmp_x_done")
    qk_done = sem("qk_done")
    logit_done = sem("logit_done")
    exp_done = sem("exp_done")
    probT_done = sem("probT_done")
    probT_copied = sem("probT_copied")
    pv_done = sem("pv_done")
    coef_done = sem("coef_done")
    o_done = sem("o_done")
    idx_done = sem("idx_done")
    relu_done = sem("relu_done")
    idx_added = sem("idx_added")
    cmp_done = sem("cmp_done")
    gate_exp = sem("gate_exp")
    lam_exp = sem("lam_exp")
    q_nope = sem("q_nope")
    mla_ready = sem("mla_ready")
    sub_sq = sem("sub_sq")
    strip_in = [sem(f"strip_in{j}") for j in range(3)]
    const_in = sem("const_in")
    x_in = sem("x_in")
    start_in = sem("start_in")
    lines_out = sem("lines_out")
    aux_in = sem("aux_in")
    out_done = sem("out_done")
    ones_set = sem("ones_set")

    AUX = {"ev": 48, "mem0": 64, "rope": 80, "od_causal": 96, "mem1": 112}

    SQ = {}
    n_sq = n_stat = n_rs = n_rt = n_cp = 0
    for kind, k in [("pre", 0), ("post", 1), ("pre", 1), ("mem", 0), ("post", 2), ("pre", 2), ("post", 3), ("pre", 3),
                    ("post", 4), ("pre", 4), ("post", 5), ("pre", 5), ("cq", 0), ("ckv", 0), ("sub", 0), ("mem", 1),
                    ("post", 6), ("pre", 6), ("post", 7), ("pre", 7), ("post", 8)]:
        SQ[kind, k] = dict(sq=n_sq, stat=n_stat, rs=n_rs, rt=n_rt, cp=n_cp)
        n_sq += {"cq": 2, "ckv": 1, "sub": 0}.get(kind, 8)
        n_stat += {"pre": 8, "sub": 0}.get(kind, 1)
        n_rs += 1
        n_rt += kind != "sub"
        n_cp += kind in ("pre", "mem")
    ADD = {("post", k): 6 * (k - 1) + 7 * (k >= 2) + 7 * (k >= 6) for k in range(1, 9)}
    ADD["mem", 0], ADD["mem", 1] = 6, 6 * 5 + 7

    X0 = {s: KC * max(s - 1, 0) for s in range(9)}
    SPLIT, n_split = {}, 0
    for name, k in [("pre0", 8), ("pre1", 8), ("ev_o", 8), ("mem0", 8), ("pre2", 8), ("xo0", 4), ("pre3", 8),
                    ("pre4", 8), ("pre5", 8), ("cq", 2), ("ckv", 1), ("od_o", 8), ("mem1", 8), ("pre6", 8),
                    ("xo1", 4), ("pre7", 8)]:
        SPLIT[name] = n_split
        n_split += k
    TURN, n_turn = {}, 1
    for name, k in [("vg", 1), ("ev_v", 2), ("ev_o", 8), ("xv0", 4), ("xo0", 4), ("dv", 4), ("od_o", 8),
                    ("xv1", 4), ("xo1", 4)]:
        TURN[name] = n_turn
        n_turn += k
    V_ROWS = {"vg": 2, "ev_v": 3, "xv0": 9, "dv": 13, "xv1": 17}

    def strip_use(g):
        return g % 3, 16 * (g // 3 + 1)

    def kind_of(job):
        phase, (kind, h, i) = job
        w = P * (i + 1)
        q = slice(P * i, P * i + P)
        off = T - P - P * i
        s = dict(blocks=i + 1, rows=P, w=w, mask=None, scale=-DH ** -0.5, factor=None, add=None)
        if kind in ("cmp", "slc", "win"):
            g, e = h // 4, 64 * (h // 4)
            s["q"] = ev[e:e + DH, QA + h % 4, q]
            s["o"] = ev_o[:, i, DH * h:DH * h + DH]
            b = ("cmp", "slc", "win").index(kind)
            s["factor"] = gates[:, i, 3 * h + b:3 * h + b + 1]
            s["add"] = b > 0
            s["strip"] = h
            if kind == "cmp":
                n = 8 * i + 7
                s.update(w=n, blocks=1, rows=n, k=kcT[e:e + DH, 0:n], v=[vc[0:n, e:e + DH]],
                         bias=ev_strip[h % 3][:, off + CMP_LEN - 1:off + CMP_LEN - 1 + CMP_STRIDE * (n - 1) + 1:CMP_STRIDE])
            else:
                s["k"] = ev[e:e + DH, KS if b == 1 else KW, 0:w]
                s["v"] = [ev_v[:, b - 1, j, e:e + DH] for j in range(i + 1)]
                s["bias"] = ev_strip[h % 3][:, off:off + w]
        elif kind == "dsa":
            e = 64 * (h % 2)
            g = A_HEADS + h
            s.update(q=ev[e:e + DH, QB + h // 2, q], k=ev[e:e + DH, KB, 0:w], strip=g,
                     v=[ev_v[:, 2, j, 0:DH] for j in range(i + 1)], bias=ev_strip[g % 3][:, off:off + w],
                     o=ev_o[:, i, 512 + DH * h:512 + DH * h + DH], mask=taken_mask[:, i - 1, 0:w] if i else None)
        elif kind.startswith("diff"):
            e = int(kind[-1])
            g = A_HEADS + B_HEADS + h
            s.update(q=od[64 * e:64 * e + DH, DQ + h, q], k=od[64 * e:64 * e + DH, DK + h, 0:w], strip=g,
                     v=[dv[:, h, j, :] for j in range(i + 1)], bias=od_strip[g % 3][:, off:off + w],
                     o=od_o[:, i, 512 + DV * h:512 + DV * h + DV], add=e > 0,
                     factor=lam[:, 0:1] if e else None)
        elif kind == "mla":
            s.update(q=mla_q[0:DN + DR, h, q], k=mla_k[0:DN + DR, h, 0:w], scale=-(DN + DR) ** -0.5,
                     v=[mla_v[:, j, DH * h:DH * h + DH] for j in range(i + 1)],
                     bias=od_causal[:, off:off + w], o=od_o[:, i, DH * h:DH * h + DH], strip=None)
        else:
            s.update(q=xq[:, h, q], k=xkv[:, h, :], scale=-P ** -0.5, w=MEM, blocks=MT,
                     v=[xv[:, h, j, :] for j in range(MT)], bias=zero[:, 0:1].to_broadcast([P, MEM]),
                     o=xo[:, i, P * h:P * h + P], strip=None)
        return s

    BUFS = [ev_bufs, x_bufs, od_bufs, od_bufs, x_bufs]
    INFO = [[kind_of((p, job)) for job in jobs] for p, jobs in enumerate(JOBS)]

    def coefs(info):
        return 2 if info["factor"] is not None else 1

    COEF0, n_coef = [], 0
    for infos in INFO:
        COEF0.append([])
        for info in infos:
            n_coef += coefs(info)
            COEF0[-1].append(n_coef)

    w_up, w_down = a["w_up"], a["w_down"]

    with nc.Block() as block:

        @block.sync
        def _(sp):
            sp.dma_start(ident[:], a["consts"][:, C_ID:C_ID + P]).then_inc(const_in, 16)
            sp.dma_start(gains[:], a["gains"]).then_inc(const_in, 16)
            sp.dma_start(row_ok[:], a["row_ok"]).then_inc(const_in, 16)
            for c in range(KC):
                sp.dma_start(x[:, c, :], a["x"][:, c, :]).then_inc(x_in, 16)

            def load(u, j, src, cols):
                sp.dma_start(raw[j][:, 0:cols], src).then_inc(raw_loaded[j], 16)

            def stream(u0, n, source, first=0, cols=KC * P):
                for k in range(first, n):
                    if (n - k) % R == 0:
                        break
                    if u0 + k >= R:
                        sp.wait_ge(split_done, u0 + k - R + 1)
                    load(u0 + k, (u0 + k) % R, source(k), cols)
                else:
                    return
                loops = (n - k) // R
                with sp.Fori(0, loops) as i:
                    for b in range(R):
                        sp.wait_ge(split_done, R * i + u0 + k + b - R + 1)
                        load(None, (u0 + k + b) % R, source(R * i + k + b), cols)

            def ffn(f):
                first = 0
                if f == 0:
                    for k in range(R):
                        load(k, k, w_up[0, k], KC * P)
                    first = R
                stream(UNIT[f"up{f}"], 2 * FC, lambda k: w_up[f, k], first)
                u0 = UNIT[f"down{f}"]
                with sp.Fori(0, KC // R) as i:
                    for b in range(3 * R):
                        n, part = b // 3, b % 3
                        at, t = P * sum(DOWN_TILES[:part]), P * DOWN_TILES[part]
                        sp.wait_ge(split_done, 3 * R * i + u0 + b - R + 1)
                        load(None, (u0 + b) % R, w_down[f, R * i + n][:, at:at + t], t)

            ffn(0)
            stream(UNIT["ev_in"], EV_IN, lambda k: a["w_ev_in"][k])
            stream(UNIT["ev_out"], KC, lambda k: a["w_ev_out"][k])
            for n in range(2):
                if n == 1:
                    ffn(1)
                    ffn(2)
                    stream(UNIT["od_in"], OD_IN, lambda k: a["w_od_in"][k])
                    stream(UNIT["uq"], 2, lambda k: a["w_uq"][k])
                    stream(UNIT["ukv"], 1, lambda k: a["w_ukv"][k])
                    stream(UNIT["od_out"], KC, lambda k: a["w_od_out"][k])
                stream(UNIT[f"xq{n}"], X_HEADS, lambda k: a["w_xq"][n, k])
                stream(UNIT[f"xkv{n}"], 2 * X_HEADS, lambda k: a["w_xkv"][n, k])
                stream(UNIT[f"xo{n}"], KC // 2, lambda k: a["w_xo"][n, k])
            ffn(3)
            for c in range(KC):
                sp.wait_ge(x_done, X0[8] + c + 1)
                sp.dma_start(a["out"][:, c, :], x[:, c, :]).then_inc(out_done, 16)
            sp.wait_ge(out_done, 16 * KC)
            sp.wait_ge(lines_out, 32)

        @block.gpsimd
        def _(pool):
            pool.memset(ones[:], 1.0).then_inc(ones_set, 1)
            pool.memset(zero[:], 0.0).then_inc(ones_set, 1)
            pool.memset(table[:], NEG).then_inc(ones_set, 1)

            def split(j, cols, u, loaded, free):
                pool.wait_ge(raw_loaded[j], loaded)
                if free is not None:
                    pool.wait_ge(unit_done, free)
                pool.sem_inc(slot_taken, 1)
                pool.tensor_scalar(w_hi[j][:, 0:cols], raw[j][:, 0:cols], 1.0, 0.0, ALU.mult, ALU.add).then_inc(hi_split, 1)
                pool.wait_ge(hi_split, u + 1)
                pool.tensor_tensor(w_lo[j][:, 0:cols], raw[j][:, 0:cols], w_hi[j][:, 0:cols].bitcast(F32),
                                   ALU.subtract).then_inc(split_done, 1)

            def straight(u, cols=KC * P):
                split(u % R, cols, u, 16 * (u // R + 1), u - R + 1 if u >= R else None)

            def units(u0, n, first=0):
                for k in range(first, n):
                    if (n - k) % R == 0:
                        break
                    straight(u0 + k)
                else:
                    return
                with pool.Fori(0, (n - k) // R) as i:
                    for b in range(R):
                        u = u0 + k + b
                        split(u % R, KC * P, R * i + u, 16 * i + 16 * (u // R + 1), R * i + u - R + 1)

            def ffn(f):
                first = 0
                if f == 0:
                    for u in range(R):
                        straight(u)
                    first = R
                units(UNIT[f"up{f}"], 2 * FC, first)
                u0 = UNIT[f"down{f}"]
                with pool.Fori(0, KC // R) as i:
                    for b in range(3 * R):
                        u = u0 + b
                        split(u % R, P * DOWN_TILES[b % 3], 3 * R * i + u, 48 * i + 16 * (u // R + 1), 3 * R * i + u - R + 1)

            ffn(0)
            units(UNIT["ev_in"], EV_IN)
            units(UNIT["ev_out"], KC)
            for n in range(2):
                if n == 1:
                    ffn(1)
                    ffn(2)
                    units(UNIT["od_in"], OD_IN)
                    units(UNIT["uq"], 2)
                    units(UNIT["ukv"], 1)
                    units(UNIT["od_out"], KC)
                units(UNIT[f"xq{n}"], X_HEADS)
                units(UNIT[f"xkv{n}"], 2 * X_HEADS)
                units(UNIT[f"xo{n}"], KC // 2)
            ffn(3)

        @block.tensor
        def _(pe):
            def product(b, j, tile, hi, lo, first, last, n=T):
                w = slice(P * tile, P * tile + P)
                pe.matmul(bank[b][:, 0:n], w_hi[j][:, w], hi, start=first, stop=False)
                pe.matmul(bank[b][:, 0:n], w_hi[j][:, w], lo, start=False, stop=False)
                return pe.matmul(bank[b][:, 0:n], w_lo[j][:, w], hi, start=False, stop=last)

            def chunk_of_unit(u, c, j, b, hi, lo, n=T):
                pe.wait_ge(split_done, u + 1)
                pe.wait_ge(chunk_out, c - R + 1)
                for k in range(KC):
                    mm = product(b, j, k, hi[:, k, 0:n], lo[:, k, 0:n], k == 0, k == KC - 1, n)
                mm.then_inc(unit_done, 1)

            def chunks(name, n, first, hi, lo, cols=T):
                u0, c0 = UNIT[name], CHUNK[name]
                for k in range(first, n):
                    if (n - k) % R == 0:
                        break
                    chunk_of_unit(u0 + k, c0 + k, (u0 + k) % R, (c0 + k) % R, hi, lo, cols)
                else:
                    return
                with pe.Fori(0, (n - k) // R) as i:
                    for b in range(R):
                        chunk_of_unit(R * i + u0 + k + b, R * i + c0 + k + b, (u0 + k + b) % R, (c0 + k + b) % R,
                                      hi, lo, cols)

            def sums(src, tiles, first, last):
                for i in range(tiles):
                    mm = pe.matmul(bank[B_STAT][:, i:i + 1], src[:, P * i:P * i + P], ones[:],
                                   start=first and i == 0, stop=last, skip_group_check=True)
                return mm

            def turn_r(key, tiles):
                pe.wait_ge(rsqrt_done, SQ[key]["rs"] + 1)
                for i in range(tiles):
                    mm = pe.transpose(bank[B_RT][:, P * i:P * i + P], rs[:, 3, i:i + 1].to_broadcast([P, P]), ident[:])
                mm.then_inc(r_turned, 1)

            def post_norm(s):
                key = ("post", s)
                pe.wait_ge(sq_added, ADD[key] + 6)
                pe.wait_ge(sq_done, SQ[key]["sq"] + KC)
                sums(sq_sum, NT, True, False)
                sums(sq[1], NT, False, True).then_inc(stat_done, 1)
                turn_r(key, NT)

            def pre_norm(s, name):
                key, u0, c0 = ("pre", s), UNIT[name], CHUNK[name]
                for c in range(KC):
                    pe.wait_ge(sq_done, SQ[key]["sq"] + c + 1)
                    sums(sq[c % 2], NT, c == 0, c == KC - 1).then_inc(stat_done, 1)
                    if c == 0:
                        pe.wait_ge(split_done, u0 + R)
                        if c0:
                            pe.wait_ge(chunk_out, c0)
                    pe.wait_ge(lo_done, SPLIT[f"pre{s}"] + c + 1)
                    for k in range(R):
                        mm = product((c0 + k) % R, (u0 + k) % R, c, h_hi[:, c, :], h_lo[:, c, :], c == 0, c == KC - 1)
                        if c == KC - 1:
                            mm.then_inc(unit_done, 1)
                turn_r(key, NT)

            def ffn(s, f):
                pre_norm(s, f"up{f}")
                chunks(f"up{f}", 2 * FC, R, h_hi, h_lo)
                u0, c0 = UNIT[f"down{f}"], CHUNK[f"down{f}"]
                with pe.Fori(0, KC // R) as i:
                    for b in range(3 * R):
                        n, part, j = b // 3, b % 3, (u0 + b) % R
                        k0, tiles = sum(DOWN_TILES[:part]), DOWN_TILES[part]
                        pe.wait_ge(split_done, 3 * R * i + u0 + b + 1)
                        if part == 0:
                            pe.wait_ge(chunk_out, R * i + c0 + n - R + 1)
                        pe.wait_ge(act_done, FC * f + k0 + tiles)
                        for k in range(tiles):
                            mm = product((c0 + n) % R, j, k, act_hi[:, k0 + k, :], act_lo[:, k0 + k, :],
                                         k0 + k == 0, k0 + k == FC - 1)
                        mm.then_inc(unit_done, 1)
                post_norm(s + 1)

            def turn_rows(key, k, src, tiles):
                n = TURN[key] + k
                for i in range(tiles):
                    mm = pe.transpose(bank[B_T[n % 2]][:, P * i:P * i + P], src[:, P * i:P * i + P], ident[:])
                mm.then_inc(turned, 1)

            def turn_output(key, o, n, lo_key):
                for f in range(n):
                    if f >= 2:
                        pe.wait_ge(lo_done, SPLIT[lo_key] + f - 1)
                    k = TURN[key] + f
                    for i in range(NT):
                        mm = pe.transpose(bank[B_T[k % 2]][:, P * i:P * i + P], o[:, i, P * f:P * f + P], ident[:])
                    mm.then_inc(turned, 1)

            def attention(phase):
                infos, j0 = INFO[phase], JOB0[phase]
                logits, probs, probTs = BUFS[phase]
                n = len(infos)

                def logit(s):
                    j, info = infos and j0 + s, infos[s]
                    if s >= 3:
                        pe.wait_ge(logit_done, j - 2)
                    if info["mask"] is not None and JOBS[phase][s][1] == 0:
                        pe.wait_ge(mask_done, JOBS[phase][s][2])
                    out = bank[B_S[s % 3]][:, 0:info["w"]]
                    mm = pe.matmul(out, info["q"], info["k"], start=True, stop=info["mask"] is None)
                    if info["mask"] is not None:
                        mm = pe.matmul(out, ident_bf[:], info["mask"], start=False, stop=True)
                    mm.then_inc(qk_done, 1)

                def turn(s):
                    j, info = j0 + s, infos[s]
                    pe.wait_ge(exp_done, j + 1)
                    if s >= 2:
                        pe.wait_ge(probT_copied, j - 1)
                    for b in range(info["blocks"]):
                        mm = pe.transpose(bank[B_T[s % 2]][0:info["rows"], P * b:P * b + P],
                                          probs[s % 3][:, P * b:P * b + info["rows"]], ident[:])
                    mm.then_inc(probT_done, 1)

                def output(s):
                    j, info = j0 + s, infos[s]
                    pe.wait_ge(probT_copied, j + 1)
                    if s >= 2:
                        pe.wait_ge(o_done, j - 1)
                    for b, v in enumerate(info["v"]):
                        mm = pe.matmul(bank[B_O[s % 2]][:, 0:v.shape[-1]],
                                       probTs[s % 2][0:info["rows"], P * b:P * b + P], v,
                                       start=b == 0, stop=b == info["blocks"] - 1)
                    mm.then_inc(pv_done, 1)

                for s in range(n + 3):
                    if s < n:
                        logit(s)
                    if 2 <= s < n + 2:
                        turn(s - 2)
                    if s >= 3:
                        output(s - 3)
                pe.wait_ge(o_done, j0 + n)

            def out_projection(name, split_key, s, mem):
                u0, c0 = UNIT[name], CHUNK[name]
                pe.wait_ge(lo_done, SPLIT[split_key] + KC)
                for k in range(KC):
                    if k == R:
                        key = ("mem", mem)
                        pe.wait_ge(sq_added, ADD[key] + 7)
                        sums(mem_sum, MT, True, True).then_inc(stat_done, 1)
                    if k == R + 1:
                        turn_r(("mem", mem), MT)
                    chunk_of_unit(u0 + k, c0 + k, (u0 + k) % R, (c0 + k) % R, h_hi, h_lo)
                post_norm(s + 1)

            def even_mixer(s):
                pre_norm(s, "ev_in")
                c0 = CHUNK["ev_in"]
                pe.wait_ge(chunk_out, c0 + 4)
                turn_rows("vg", 0, ev[:, VG, :], NT)
                banks = (B_STAT, B_RT, B_T[(TURN["vg"] + 1) % 2])
                for k in range((NT - 1) * IDX_HEADS):
                    i, h = 1 + k // IDX_HEADS, k % IDX_HEADS
                    e = IDX_DH * (h % 4)
                    if k >= 3:
                        pe.wait_ge(relu_done, k - 2)
                    pe.matmul(bank[banks[k % 3]][:, 0:P * (i + 1)], ev[e:e + IDX_DH, IQ + h // 4, P * i:P * i + P],
                              ev[e:e + IDX_DH, IK, 0:P * (i + 1)], start=True, stop=True).then_inc(idx_done, 1)
                chunks("ev_in", EV_IN, R, h_hi, h_lo)
                pe.wait_ge(relu_done, (NT - 1) * IDX_HEADS)
                pe.wait_ge(rows_done, V_ROWS["vg"] + 1)
                for k, src in enumerate((VS, VW)):
                    pe.wait_ge(chunk_out, c0 + src + 1)
                    turn_rows("ev_v", k, ev[:, src, :], NT)
                pe.wait_ge(aux_in, AUX["ev"])
                pe.wait_ge(cmp_x_done, 1)
                pe.wait_ge(chunk_out, c0 + EV_IN)
                for g in range(2):
                    e = slice(DH * g, DH * g + DH)
                    for l in range(CMP_LEN):
                        mm = pe.matmul(bank[g][e, 0:N_CMP], cmp_w[e, 0, l, :], cmp_x[e, 0, l, :],
                                       start=l == 0, stop=l == CMP_LEN - 1)
                    mm.then_inc(cmp_done, 1)
                pe.wait_ge(cmp_x_done, 2)
                for g in range(2):
                    e = slice(DH * g, DH * g + DH)
                    for l in range(CMP_LEN):
                        mm = pe.matmul(bank[2 + g][0:N_CMP, 0:DH], cmp_x[e, 1, l, :], cmp_w[e, 1, l, :],
                                       start=l == 0, stop=l == CMP_LEN - 1)
                    mm.then_inc(cmp_done, 1)
                pe.wait_ge(rows_done, V_ROWS["ev_v"] + 2 + 4)
                attention(0)
                turn_output("ev_o", ev_o, KC, "ev_o")
                out_projection("ev_out", "ev_o", s, 0)

            def cross(s, n):
                pre_norm(s, f"xq{n}")
                pe.wait_ge(lo_done, SPLIT[f"mem{n}"] + KC)
                chunks(f"xkv{n}", 2 * X_HEADS, 0, mem_hi, mem_lo, MEM)
                for h in range(X_HEADS):
                    if h >= 2:
                        pe.wait_ge(rows_done, V_ROWS[f"xv{n}"] + h - 1)
                    pe.wait_ge(chunk_out, CHUNK[f"xkv{n}"] + X_HEADS + h + 1)
                    turn_rows(f"xv{n}", h, xkv[:, X_HEADS + h, :], MT)
                pe.wait_ge(rows_done, V_ROWS[f"xv{n}"] + X_HEADS)
                attention(1 if n == 0 else 4)
                turn_output(f"xo{n}", xo, X_HEADS, f"xo{n}")
                u0, c0 = UNIT[f"xo{n}"], CHUNK[f"xo{n}"]
                pe.wait_ge(lo_done, SPLIT[f"xo{n}"] + X_HEADS)
                for c in range(KC):
                    if c % 2 == 0:
                        pe.wait_ge(split_done, u0 + c // 2 + 1)
                    pe.wait_ge(chunk_out, c0 + c - R + 1)
                    for k in range(X_HEADS):
                        mm = product((c0 + c) % R, (u0 + c // 2) % R, X_HEADS * (c % 2) + k, h_hi[:, k, :],
                                     h_lo[:, k, :], k == 0, k == X_HEADS - 1)
                    if c % 2:
                        mm.then_inc(unit_done, 1)
                post_norm(s + 1)

            def odd_mixer(s):
                pre_norm(s, "od_in")
                c0 = CHUNK["od_in"]
                chunks("od_in", OD_IN, R, h_hi, h_lo)
                pe.wait_ge(sq_done, SQ["cq", 0]["sq"] + 2)
                sums(sq[0], NT, True, False)
                sums(sq[1], NT, False, True).then_inc(stat_done, 1)
                turn_r(("cq", 0), NT)
                for h in range(D_HEADS):
                    if h >= 2:
                        pe.wait_ge(rows_done, V_ROWS["dv"] + h - 1)
                    pe.wait_ge(chunk_out, c0 + DVT + h + 1)
                    turn_rows("dv", h, od[:, DVT + h, :], NT)
                pe.wait_ge(sq_done, SQ["ckv", 0]["sq"] + 1)
                sums(sq[0], NT, True, True).then_inc(stat_done, 1)
                turn_r(("ckv", 0), NT)
                pe.wait_ge(rows_done, V_ROWS["dv"] + D_HEADS)
                attention(2)
                u0, c0 = UNIT["uq"], CHUNK["uq"]
                pe.wait_ge(lo_done, SPLIT["ckv"] + 1)
                for h in range(C_HEADS):
                    if h % R == 0:
                        pe.wait_ge(split_done, u0 + h // R + 1)
                        if h:
                            pe.wait_ge(chunk_out, c0 + h)
                            pe.wait_ge(q_nope, h)
                    for k in range(2):
                        mm = product((c0 + h) % R, (u0 + h // R) % R, 2 * (h % R) + k, cq_hi[:, k, :], cq_lo[:, k, :],
                                     k == 0, k == 1)
                    if h % R == R - 1:
                        mm.then_inc(unit_done, 1)
                u0, c0 = UNIT["ukv"], CHUNK["ukv"]
                j = u0 % R
                pe.wait_ge(split_done, u0 + 1)
                for i in range(NT):
                    tok = slice(P * i, P * i + P)
                    out = bank[4 + i][:]
                    pe.matmul(out, ckv_hi[:, tok], w_hi[j][:, T:2 * T], start=True, stop=False)
                    pe.matmul(out, ckv_hi[:, tok], w_lo[j][:, T:2 * T], start=False, stop=False)
                    pe.matmul(out, ckv_lo[:, tok], w_hi[j][:, T:2 * T], start=False, stop=True)
                pe.wait_ge(chunk_out, c0)
                pe.wait_ge(q_nope, C_HEADS)
                for m_ in range(4):
                    mm = product((c0 + m_) % R, j, m_, ckv_hi[:], ckv_lo[:], True, True)
                mm.then_inc(unit_done, 1)
                pe.wait_ge(chunk_out, c0 + 4)
                pe.wait_ge(q_nope, C_HEADS + 4 + 2)
                pe.wait_ge(mla_ready, 5)
                attention(3)
                pe.wait_ge(mla_ready, 6)
                turn_output("od_o", od_o, KC, "od_o")
                out_projection("od_out", "od_o", s, 1)

            pe.wait_ge(start_in, 16 * 3)
            pe.wait_ge(ones_set, 3)
            pe.matmul(bank[0][0:BIAS_HEADS, 0:512], table[:], onehot[:, 0:512], start=True, stop=True)
            pe.matmul(bank[1][0:BIAS_HEADS, 0:LINE + 1 - 512], table[:], onehot[:, 512:LINE + 1], start=True,
                      stop=True).then_inc(turned, 1)
            pe.wait_ge(rows_done, 2)
            pe.wait_ge(const_in, 48)
            ffn(0, 0)
            even_mixer(1)
            cross(2, 0)
            ffn(3, 1)
            ffn(4, 2)
            odd_mixer(5)
            cross(6, 1)
            ffn(7, 3)

        @block.scalar
        def _(act):
            def pre_norm(s):
                key = ("pre", s)
                for c in range(KC):
                    if s:
                        act.wait_ge(x_done, X0[s] + c + 1)
                    else:
                        act.wait_ge(x_in, 16 * KC)
                    g = G_PRE + KC * s + c
                    act.activation(h_hi[:, c, :], x[:, c, :], ACT.Copy, scale=gains[:, g:g + 1]).then_inc(hi_done, 1)
                    if c >= 2:
                        act.wait_ge(stat_done, SQ[key]["stat"] + c - 1)
                    act.activation(sq[c % 2][:], x[:, c, :], ACT.Square).then_inc(sq_done, 1)
                act.wait_ge(r_turned, SQ[key]["rt"] + 1)
                act.activation(r_sb[:], bank[B_RT][:], ACT.Copy).then_inc(r_copied, 1)

            def squares(s, name, y, n0=0, n1=KC):
                key = ("post", s)
                for c in range(n0, n1):
                    act.wait_ge(chunk_out, CHUNK[name] + c + 1)
                    if c >= 3:
                        act.wait_ge(sq_added, ADD[key] + c - 2)
                    act.activation((sq_sum if c == 0 else sq[c % 2])[:], y[:, c, :], ACT.Square).then_inc(sq_done, 1)

            def ffn(s, f):
                pre_norm(s)
                c0 = CHUNK[f"up{f}"]
                with act.Fori(0, FC // 2) as i:
                    for p in range(2):
                        act.wait_ge(chunk_out, 4 * i + c0 + 2 * p + 1)
                        act.activation(gate[p][:], gate[p][:], ACT.Silu).then_inc(silu_done, 1)
                squares(s + 1, f"down{f}", y_ffn)

            def copy_rows(key, k, dst, tiles):
                n = TURN[key] + k
                act.wait_ge(turned, n + 1)
                src = bank[B_T[n % 2]][:, 0:P * tiles].rearrange("p (i t) -> p i t", i=tiles)
                act.activation(dst, src, ACT.Copy).then_inc(rows_done, 1)

            def split_output(key, n, gain=None):
                for f in range(n):
                    k = TURN[key] + f
                    act.wait_ge(turned, k + 1)
                    src = bank[B_T[k % 2]][:]
                    if gain is not None and f >= 4:
                        act.activation(h_hi[:, f, :], src, ACT.Copy, scale=gain).then_inc(hi_done, 1)
                    else:
                        act.activation(h_hi[:, f, :], src, ACT.Copy).then_inc(hi_done, 1)

            def load_strip(g, bufs):
                slot, _ = strip_use(g)
                src = bass.AP(line_rows.tensor, P * (LINE + 1) * g + P - 1, [[LINE, P], [1, T]])
                act.dma_start(bufs[slot][:], src).then_inc(strip_in[slot], 16)

            def attention(phase, strips=None, buf=None):
                infos, j0 = INFO[phase], JOB0[phase]
                logits, probs, probTs = BUFS[phase]
                seen = set()
                if strips:
                    for g in range(strips[0], min(strips[0] + 3, strips[1])):
                        load_strip(g, buf)

                def exp(s):
                    j, info = j0 + s, infos[s]
                    act.wait_ge(logit_done, j + 1)
                    g = info["strip"]
                    if strips and g not in seen:
                        if seen and g + 2 < strips[1]:
                            load_strip(g + 2, buf)
                        seen.add(g)
                    if s >= 3:
                        act.wait_ge(probT_done, j - 2)
                    w = info["w"]
                    act.activation(probs[s % 3][:, 0:w], logits[s % 3][:, 0:w], ACT.Exp, scale=-1.0,
                                   bias=neg_max[:, j % 8:j % 8 + 1],
                                   accum_out=row_sum[:, j % 8:j % 8 + 1]).then_inc(exp_done, 1)

                def copy(s):
                    j, info = j0 + s, infos[s]
                    act.wait_ge(probT_done, j + 1)
                    if s >= 2:
                        act.wait_ge(pv_done, j - 1)
                    w = P * info["blocks"]
                    act.activation(probTs[s % 2][0:info["rows"], 0:w], bank[B_T[s % 2]][0:info["rows"], 0:w],
                                   ACT.Copy).then_inc(probT_copied, 1)

                for s in range(len(infos) + 2):
                    if s < len(infos):
                        exp(s)
                    if s >= 2:
                        copy(s - 2)

            def memory(n, split_key):
                act.wait_ge(lo_done, SPLIT[split_key] + KC)
                act.dma_start(mem_sb[:], a["mem"]).then_inc(aux_in, 16)
                act.wait_ge(aux_in, AUX[f"mem{n}"])
                for c in range(KC):
                    g = G_MEM + KC * n + c
                    act.activation(mem_hi[:, c, :], mem_sb[:, c, :], ACT.Copy, scale=gains[:, g:g + 1]).then_inc(hi_done, 1)
                    if c >= 3:
                        act.wait_ge(sq_added, ADD["mem", n] + c - 2)
                    act.activation((mem_sum if c == 0 else mem_sq[c % 2])[:], mem_sb[:, c, :],
                                   ACT.Square).then_inc(sq_done, 1)

            def memory_r(n):
                act.wait_ge(r_turned, SQ["mem", n]["rt"] + 1)
                act.activation(r_mem[:], bank[B_RT][:, 0:MEM], ACT.Copy).then_inc(r_copied, 1)

            def even_mixer(s):
                pre_norm(s)
                act.dma_start(cmp_w[:], a["cmp_w"]).then_inc(aux_in, 16)
                act.dma_start(cmp_pe[:], a["cmp_pe"]).then_inc(aux_in, 16)
                act.dma_start(ev_causal[:], a["consts"][:, C_CAUSAL:C_CAUSAL + T]).then_inc(aux_in, 16)
                act.wait_ge(lines_out, 32)
                copy_rows("vg", 0, ev_v[:, 2, :, :], NT)
                act.wait_ge(rows_done, V_ROWS["vg"] + 1)
                act.activation(gates[:], ev_v[:, 2, :, DH:DH + 3 * A_HEADS], ACT.Exp, scale=-1.0).then_inc(gate_exp, 1)
                banks = (B_STAT, B_RT, B_T[(TURN["vg"] + 1) % 2])
                for k in range((NT - 1) * IDX_HEADS):
                    i = 1 + k // IDX_HEADS
                    act.wait_ge(idx_done, k + 1)
                    if k >= 2:
                        act.wait_ge(idx_added, k - 1)
                    act.activation(relu[k % 2][:, 0:P * (i + 1)], bank[banks[k % 3]][:, 0:P * (i + 1)],
                                   ACT.Relu).then_inc(relu_done, 1)
                copy_rows("ev_v", 0, ev_v[:, 0, :, :], NT)
                copy_rows("ev_v", 1, ev_v[:, 1, :, :], NT)
                for g in range(2):
                    e = slice(DH * g, DH * g + DH)
                    act.wait_ge(cmp_done, g + 1)
                    act.activation(kcT[e, 0:N_CMP], bank[g][e, 0:N_CMP], ACT.Copy).then_inc(rows_done, 1)
                for g in range(2):
                    act.wait_ge(cmp_done, g + 3)
                    act.activation(vc[0:N_CMP, DH * g:DH * g + DH], bank[2 + g][0:N_CMP, 0:DH],
                                   ACT.Copy).then_inc(rows_done, 1)
                attention(0, (0, A_HEADS + B_HEADS), ev_strip)
                split_output("ev_o", KC)
                memory(0, "ev_o")
                squares(s + 1, "ev_out", ev_y, 0, 5)
                memory_r(0)
                squares(s + 1, "ev_out", ev_y, 5, KC)

            def cross(s, n):
                pre_norm(s)
                for h in range(X_HEADS):
                    copy_rows(f"xv{n}", h, xv[:, h, :, :], MT)
                attention(1 if n == 0 else 4)
                split_output(f"xo{n}", X_HEADS)
                squares(s + 1, f"xo{n}", x_y)

            def odd_mixer(s):
                pre_norm(s)
                act.dma_start(rope_t[:], a["consts"][:, C_ROPE:C_ROPE + T]).then_inc(aux_in, 16)
                c0 = CHUNK["od_in"]
                for k in range(2):
                    act.wait_ge(chunk_out, c0 + CQ + k + 1)
                    act.activation(sq[k][:], od[:, CQ + k, :], ACT.Square).then_inc(sq_done, 1)
                act.wait_ge(stat_done, SQ["cq", 0]["stat"] + 1)
                act.activation(sq[0][:], od[:, CKV, :], ACT.Square).then_inc(sq_done, 1)
                for h in range(2):
                    copy_rows("dv", h, dv[:, h, :, :], NT)
                for k in range(2):
                    act.wait_ge(mla_ready, k + 1)
                    act.activation(cq_hi[:, k, :], od[:, CQ + k, :], ACT.Copy).then_inc(hi_done, 1)
                for h in range(2, D_HEADS):
                    copy_rows("dv", h, dv[:, h, :, :], NT)
                act.wait_ge(mla_ready, 3)
                act.activation(ckv_hi[:], od[:, CKV, :], ACT.Copy).then_inc(hi_done, 1)
                attention(2, (A_HEADS + B_HEADS, BIAS_HEADS), od_strip)
                act.wait_ge(o_done, JOB0[3])
                act.dma_start(od_causal[:], a["consts"][:, C_CAUSAL:C_CAUSAL + T]).then_inc(aux_in, 16)
                for h in range(C_HEADS):
                    act.wait_ge(unit_done, UNIT["uq"] + h // R + 1)
                    act.activation(mla_q[0:DN, h, :], bank[(CHUNK["uq"] + h) % R][0:DN, :], ACT.Copy).then_inc(q_nope, 1)
                act.wait_ge(unit_done, UNIT["ukv"] + 1)
                for k in range(4):
                    act.activation(mla_k[0:DN, 2 * k, :], bank[(CHUNK["ukv"] + k) % R][0:DN, :],
                                   ACT.Copy).then_inc(q_nope, 1)
                act.wait_ge(mla_ready, 4)
                for i in range(2):
                    act.activation(mla_v[:, i, :], bank[4 + i][:], ACT.Copy).then_inc(q_nope, 1)
                for i in range(NT):
                    for h in range(D_HEADS):
                        n = D_HEADS * i + h
                        act.activation(sub_tmp(n), od_o[:, i, 512 + DV * h:512 + DV * h + DV], ACT.Square,
                                       accum_out=rs[:, 0, n:n + 1]).then_inc(sub_sq, 1)
                attention(3)
                split_output("od_o", KC, lam[:, 5:6])
                memory(1, "od_o")
                squares(s + 1, "od_out", od_y, 0, 5)
                memory_r(1)
                squares(s + 1, "od_out", od_y, 5, KC)

            def sub_tmp(n):
                return (od_bufs[0] + od_bufs[1])[n // 4][:, DV * (n % 4):DV * (n % 4) + DV]

            act.wait_ge(ones_set, 3)
            act.dma_start(onehot[:], a["onehot"]).then_inc(start_in, 16)
            act.dma_start(table[0:BUCKETS, :], a["table"]).then_inc(start_in, 16)
            act.dma_start(lam_in[:], a["lam"].partition_broadcast(P)).then_inc(start_in, 16)
            act.wait_ge(turned, 1)
            act.activation(lines[:, 0:512], bank[0][0:BIAS_HEADS, :], ACT.Copy).then_inc(rows_done, 1)
            act.activation(lines[:, 512:LINE + 1], bank[1][0:BIAS_HEADS, 0:LINE + 1 - 512], ACT.Copy).then_inc(rows_done, 1)
            act.wait_ge(rows_done, 2)
            act.dma_start(lines_dram, lines[:]).then_inc(lines_out, 16)
            act.wait_ge(dve_done, 2)
            act.activation(lam[:, 3:5], lam[:, 1:3], ACT.Exp).then_inc(lam_exp, 1)
            act.wait_ge(const_in, 48)
            act.activation(ident_bf[:], ident[:], ACT.Copy).then_inc(lam_exp, 1)
            act.wait_ge(lines_out, 16)
            rows = bass.AP(lines_dram.tensor, 0, [[LINE + 1, BIAS_HEADS], [0, P], [1, LINE + 1]])
            act.dma_start(line_rows, rows).then_inc(lines_out, 16)
            ffn(0, 0)
            even_mixer(1)
            cross(2, 0)
            ffn(3, 1)
            ffn(4, 2)
            odd_mixer(5)
            cross(6, 1)
            ffn(7, 3)

        @block.vector
        def _(dve):
            n_small = [0]

            def small(ins):
                n_small[0] += 1
                ins.then_inc(dve_done, 1)
                dve.wait_ge(dve_done, n_small[0])

            def rsqrt(key, w, d, stats=1, src=None):
                value, half, y = (rs[:, k, 0:w] for k in (0, 2, 3))
                square = rs[:, 1, 0:w]
                if src is None:
                    dve.wait_ge(stat_done, SQ[key]["stat"] + stats)
                    src = bank[B_STAT][:, 0:w]
                small(dve.tensor_scalar(value, src, 1.0 / d, EPS, ALU.mult, ALU.add))
                small(dve.tensor_scalar(square.bitcast(I32), value.bitcast(I32), 1, None, ALU.logical_shift_right))
                small(dve.tensor_scalar(y.bitcast(I32), square.bitcast(I32), -1.0, RSQRT_SEED, ALU.mult, ALU.add))
                for k in range(4):
                    small(dve.tensor_tensor(square, y, y, ALU.mult))
                    small(dve.scalar_tensor_tensor(half, square, -0.5, value, ALU.mult, ALU.mult))
                    last = dve.scalar_tensor_tensor(y, half, 1.5, y, ALU.add, ALU.mult)
                    if k < 3:
                        small(last)
                last.then_inc(rsqrt_done, 1)

            def pre_norm(s, c):
                g = G_PRE + KC * s + c
                dve.wait_ge(hi_done, SPLIT[f"pre{s}"] + c + 1)
                dve.scalar_tensor_tensor(h_lo[:, c, :], x[:, c, :], gains[:, g:g + 1], h_hi[:, c, :].bitcast(F32),
                                         ALU.mult, ALU.subtract).then_inc(lo_done, 1)

            def pre_norm_r(s):
                rsqrt(("pre", s), NT, D, KC)
                dve.wait_ge(r_copied, SQ["pre", s]["cp"] + 1)

            def seam(s, y):
                rsqrt(("post", s), NT, D)
                dve.wait_ge(r_turned, SQ["post", s]["rt"] + 1)

                def scaled(c):
                    g = G_POST + KC * (s - 1) + c
                    if c >= 2:
                        dve.wait_ge(x_done, X0[s] + c - 1)
                    dve.scalar_tensor_tensor(step[c % 2][:], y[:, c, :], gains[:, g:g + 1], bank[B_RT][:],
                                             ALU.mult, ALU.mult).then_inc(dve_done, 1)
                    n_small[0] += 1

                scaled(0)
                for c in range(KC):
                    if c + 1 < KC:
                        scaled(c + 1)
                    dve.wait_ge(dve_done, n_small[0] - (c + 1 < KC))
                    dve.tensor_tensor(x[:, c, :], x[:, c, :], step[c % 2][:], ALU.add).then_inc(x_done, 1)
                    if s < 8 and c >= 1:
                        pre_norm(s, c - 1)
                if s < 8:
                    pre_norm(s, KC - 1)
                    pre_norm_r(s)

            def leave(name, c, unit, dst, r):
                dve.wait_ge(unit_done, UNIT[name] + unit)
                b = (CHUNK[name] + c) % R
                dve.tensor_tensor(dst, bank[b][:, 0:r.shape[-1]], r, ALU.mult).then_inc(chunk_out, 1)

            def output_chunks(s, name, y, unit_of, c0=0, c1=KC):
                key = ("post", s)

                def add(c):
                    dve.wait_ge(sq_done, SQ[key]["sq"] + c + 1)
                    if c > 1:
                        dve.wait_ge(sq_added, ADD[key] + c - 1)
                    dve.tensor_tensor(sq_sum[:], sq_sum[:], sq[c % 2][:], ALU.add).then_inc(sq_added, 1)

                for c in range(c0, c1):
                    dve.wait_ge(unit_done, UNIT[name] + unit_of(c))
                    dve.tensor_copy(y[:, c, :], bank[(CHUNK[name] + c) % R][:]).then_inc(chunk_out, 1)
                    if c >= 2:
                        add(c - 1)

            def ffn(s, f):
                u0, c0 = UNIT[f"up{f}"], CHUNK[f"up{f}"]
                with dve.Fori(0, FC // 2) as i:
                    for p in range(2):
                        k = 2 * p
                        dve.wait_ge(unit_done, 4 * i + u0 + k + 1)
                        dve.tensor_tensor(gate[p][:], bank[(c0 + k) % R][:], r_sb[:], ALU.mult).then_inc(chunk_out, 1)
                        dve.wait_ge(unit_done, 4 * i + u0 + k + 2)
                        dve.tensor_tensor(up[p][:], bank[(c0 + k + 1) % R][:], r_sb[:], ALU.mult).then_inc(chunk_out, 1)
                        dve.wait_ge(silu_done, 2 * i + FC * f + p + 1)
                        dve.wait_ge(chunk_out, 4 * i + c0 + k + 2)
                        dve.tensor_tensor(up[p][:], gate[p][:], up[p][:], ALU.mult).then_inc(prod_done, 1)
                        dve.wait_ge(prod_done, 2 * i + FC * f + p + 1)
                        dve.tensor_scalar(act_hi[:, 2 * i + p, :], up[p][:], 1.0, None, ALU.mult).then_inc(act_hi_done, 1)
                        dve.wait_ge(act_hi_done, 2 * i + FC * f + p + 1)
                        dve.tensor_tensor(act_lo[:, 2 * i + p, :], up[p][:], act_hi[:, 2 * i + p, :].bitcast(F32),
                                          ALU.subtract).then_inc(act_done, 1)
                output_chunks(s + 1, f"down{f}", y_ffn, lambda c: 3 * (c + 1))
                seam(s + 1, y_ffn)

            def split_output(key, n, gain=None):
                for f in range(n):
                    k = TURN[key] + f
                    dve.wait_ge(hi_done, SPLIT[key] + f + 1)
                    src, hi = bank[B_T[k % 2]][:], h_hi[:, f, :].bitcast(F32)
                    if gain is not None and f >= 4:
                        dve.scalar_tensor_tensor(h_lo[:, f, :], src, gain, hi, ALU.mult, ALU.subtract).then_inc(lo_done, 1)
                    else:
                        dve.tensor_tensor(h_lo[:, f, :], src, hi, ALU.subtract).then_inc(lo_done, 1)

            def memory(n):
                key = ("mem", n)
                for c in range(KC):
                    g = G_MEM + KC * n + c
                    dve.wait_ge(hi_done, SPLIT[f"mem{n}"] + c + 1)
                    dve.scalar_tensor_tensor(mem_lo[:, c, :], mem_sb[:, c, :], gains[:, g:g + 1],
                                             mem_hi[:, c, :].bitcast(F32), ALU.mult, ALU.subtract).then_inc(lo_done, 1)
                    if c:
                        dve.wait_ge(sq_done, SQ[key]["sq"] + c + 1)
                        if c > 1:
                            dve.wait_ge(sq_added, ADD[key] + c - 1)
                        dve.tensor_tensor(mem_sum[:], mem_sum[:], mem_sq[c % 2][:], ALU.add).then_inc(sq_added, 1)

            def attention(phase, strips=False):
                infos, j0 = INFO[phase], JOB0[phase]
                logits = BUFS[phase][0]
                n, seen = len(infos), set()

                def logit(s):
                    j, info = j0 + s, infos[s]
                    g = info["strip"]
                    if strips and g not in seen:
                        slot, count = strip_use(g)
                        dve.wait_ge(strip_in[slot], count)
                        seen.add(g)
                    dve.wait_ge(qk_done, j + 1)
                    if s >= 3:
                        dve.wait_ge(exp_done, j - 2)
                    w = info["w"]
                    dve.tensor_tensor_reduce(out=logits[s % 3][:, 0:w], in0=bank[B_S[s % 3]][:, 0:w], in1=info["bias"],
                                             scale=info["scale"], scalar=3e38, op0=ALU.add, op1=ALU.min,
                                             accum_out=neg_max[:, j % 8:j % 8 + 1]).then_inc(logit_done, 1)

                def factor(s):
                    j, info = j0 + s, infos[s]
                    col = slice(j % 8, j % 8 + 1)
                    dve.wait_ge(exp_done, j + 1)
                    dve.reciprocal(coef[:, col], row_sum[:, col]).then_inc(coef_done, 1)
                    if info["factor"] is not None:
                        dve.wait_ge(coef_done, COEF0[phase][s] - 1)
                        dve.tensor_tensor(coef[:, col], coef[:, col], info["factor"], ALU.mult).then_inc(coef_done, 1)

                def output(s):
                    j, info = j0 + s, infos[s]
                    col = slice(j % 8, j % 8 + 1)
                    dve.wait_ge(pv_done, j + 1)
                    dve.wait_ge(coef_done, COEF0[phase][s])
                    src = bank[B_O[s % 2]][:, 0:info["o"].shape[-1]]
                    if info["add"]:
                        dve.wait_ge(o_done, j)
                        dve.scalar_tensor_tensor(info["o"], src, coef[:, col], info["o"], ALU.mult,
                                                 ALU.add).then_inc(o_done, 1)
                    else:
                        dve.tensor_scalar(info["o"], src, coef[:, col], None, ALU.mult).then_inc(o_done, 1)

                for s in range(n + 4):
                    if s < n:
                        logit(s)
                    if 3 <= s < n + 3:
                        factor(s - 3)
                    if s >= 4:
                        output(s - 4)
                dve.wait_ge(o_done, j0 + n)

            def even_mixer(s):
                out = [0]

                def leave_next():
                    c = out[0]
                    if c < EV_IN:
                        leave("ev_in", c, c + 1, ev[:, c, :], r_sb[:])
                        out[0] += 1

                for _ in range(4):
                    leave_next()
                dve.wait_ge(gate_exp, 1)
                small(dve.tensor_scalar(gates[:], gates[:], 1.0, None, ALU.add))
                small(dve.reciprocal(gates[:], gates[:]))
                first = gates[:, 0, 0:3 * A_HEADS:3]
                small(dve.tensor_scalar(first, first, row_ok[:], None, ALU.mult))
                dve.wait_ge(aux_in, AUX["ev"])
                for k in range((NT - 1) * IDX_HEADS):
                    i, h = 1 + k // IDX_HEADS, k % IDX_HEADS
                    w = P * (i + 1)
                    off = T - w
                    sc = score[i - 1][:, 0:w]
                    dve.wait_ge(relu_done, k + 1)
                    if h:
                        dve.wait_ge(idx_added, k)
                    dve.scalar_tensor_tensor(sc, relu[k % 2][:, 0:w], ev_v[:, 2, i, 88 + h:89 + h],
                                             sc if h else ev_causal[:, off:off + w], ALU.mult,
                                             ALU.add).then_inc(idx_added, 1)
                dve.wait_ge(idx_added, (NT - 1) * IDX_HEADS)
                for i in range(1, NT):
                    sc = score[i - 1][:, 0:P * (i + 1)]
                    for k in range(TOPK // 8):
                        small(dve.max(top8[:], sc))
                        small(dve.match_replace(sc, top8[:], sc, TAKEN))
                        if k % 3 == 2:
                            leave_next()
                    dve.tensor_scalar(taken_mask[:, i - 1, 0:P * (i + 1)], sc, TAKEN / 2, NEG, ALU.is_gt,
                                      ALU.mult).then_inc(mask_done, 1)
                for _ in range(EV_IN):
                    leave_next()
                dve.wait_ge(chunk_out, CHUNK["ev_in"] + EV_IN)
                dve.wait_ge(mask_done, NT - 1)
                for kv, src in enumerate((KCMP, VCMP)):
                    proj = ev[:, src, :]
                    blocks = bass.AP(proj.tensor, proj.offset, [list(proj.ap[0]), [1, CMP_LEN], [CMP_STRIDE, N_CMP]])
                    pe_ = cmp_pe[:, kv, :].unsqueeze(2).to_broadcast([P, CMP_LEN, N_CMP])
                    dve.tensor_tensor(cmp_x[:, kv, :, :], blocks, pe_, ALU.add).then_inc(cmp_x_done, 1)
                dve.wait_ge(cmp_x_done, 2)
                attention(0, True)
                split_output("ev_o", KC)
                memory(0)
                output_chunks(s + 1, "ev_out", ev_y, lambda c: c + 1, 0, R)
                rsqrt(("mem", 0), MT, D)
                output_chunks(s + 1, "ev_out", ev_y, lambda c: c + 1, R, KC)
                seam(s + 1, ev_y)

            def cross(s, n):
                for h in range(X_HEADS):
                    leave(f"xq{n}", h, h + 1, xq[:, h, :], r_sb[:])
                dve.wait_ge(r_copied, SQ["mem", n]["cp"] + 1)
                for h in range(2 * X_HEADS):
                    leave(f"xkv{n}", h, h + 1, xkv[:, h, :], r_mem[:])
                attention(1 if n == 0 else 4)
                split_output(f"xo{n}", X_HEADS)
                output_chunks(s + 1, f"xo{n}", x_y, lambda c: c // 2 + 1)
                seam(s + 1, x_y)

            def odd_mixer(s):
                for c in range(OD_IN):
                    leave("od_in", c, c + 1, od[:, c, :], r_sb[:])
                dve.wait_ge(chunk_out, CHUNK["od_in"] + OD_IN)
                for key, d, cs, g0, lo in ((("cq", 0), 2 * P, (CQ, CQ + 1), G_Q, (cq_lo[:, 0, :], cq_lo[:, 1, :])),
                                           (("ckv", 0), P, (CKV,), G_KV, (ckv_lo[:],))):
                    rsqrt(key, NT, d)
                    dve.wait_ge(r_turned, SQ[key]["rt"] + 1)
                    for k, c in enumerate(cs):
                        dve.scalar_tensor_tensor(od[:, c, :], od[:, c, :], gains[:, g0 + k:g0 + k + 1], bank[B_RT][:],
                                                 ALU.mult, ALU.mult).then_inc(mla_ready, 1)
                    for k, c in enumerate(cs):
                        hi = cq_hi[:, k, :] if key[0] == "cq" else ckv_hi[:]
                        dve.wait_ge(hi_done, SPLIT[key[0]] + k + 1)
                        dve.tensor_tensor(lo[k], od[:, c, :], hi.bitcast(F32), ALU.subtract).then_inc(lo_done, 1)
                attention(2, True)
                dve.wait_ge(aux_in, AUX["rope"])
                e = slice(DN, DN + DR)
                small(dve.tensor_tensor(step[1][e, :], od[0:DR, KR, :], rope_t[0:DR, :], ALU.mult))
                small(dve.tensor_tensor(step[0][e, :], od[DR:2 * DR, KR, :], rope_t[DR:2 * DR, :], ALU.mult))
                small(dve.tensor_tensor(step[1][e, :], step[1][e, :], step[0][e, :], ALU.add))
                dve.tensor_copy(mla_k[e, :, :], step[1][e, :].unsqueeze(1).to_broadcast([DR, C_HEADS, T])).then_inc(mla_ready, 1)
                for h in range(C_HEADS):
                    b = (CHUNK["uq"] + h) % R
                    dve.wait_ge(unit_done, UNIT["uq"] + h // R + 1)
                    dve.tensor_tensor(mla_q[e, h, :], bank[b][e, :], rope_t[e, :], ALU.mult).then_inc(dve_done, 1)
                    n_small[0] += 1
                    dve.tensor_tensor(step[h % 2][e, :], bank[b][DN + DR:P, :], rope_t[DN + DR:P, :], ALU.mult).then_inc(chunk_out, 1)
                    dve.wait_ge(chunk_out, CHUNK["uq"] + h + 1)
                    dve.wait_ge(dve_done, n_small[0])
                    small(dve.tensor_tensor(mla_q[e, h, :], mla_q[e, h, :], step[h % 2][e, :], ALU.add))
                dve.wait_ge(unit_done, UNIT["ukv"] + 1)
                for k in range(4):
                    dve.tensor_copy(mla_k[0:DN, 2 * k + 1, :], bank[(CHUNK["ukv"] + k) % R][DN:P, :]).then_inc(chunk_out, 1)
                dve.wait_ge(chunk_out, CHUNK["ukv"] + 4)
                small(dve.tensor_copy(mla_v[:, 2, :], bank[6][:]))
                dve.tensor_copy(mla_v[:, 3, :], bank[7][:]).then_inc(mla_ready, 1)
                dve.wait_ge(mla_ready, 5)
                dve.wait_ge(sub_sq, NT * D_HEADS)
                rsqrt(("sub", 0), NT * D_HEADS, DV, src=rs[:, 0, 0:NT * D_HEADS])
                dve.wait_ge(rsqrt_done, SQ["sub", 0]["rs"] + 1)
                o4 = od_o[:, :, 512:D].rearrange("p i (h t) -> p i h t", h=D_HEADS)
                for i in range(NT):
                    r4 = rs[:, 3, D_HEADS * i:D_HEADS * i + D_HEADS].unsqueeze(2).to_broadcast([P, D_HEADS, DV])
                    ins = dve.tensor_tensor(o4[:, i], o4[:, i], r4, ALU.mult)
                    if i < NT - 1:
                        small(ins)
                ins.then_inc(mla_ready, 1)
                dve.wait_ge(aux_in, AUX["od_causal"])
                attention(3)
                split_output("od_o", KC, lam[:, 5:6])
                memory(1)
                output_chunks(s + 1, "od_out", od_y, lambda c: c + 1, 0, R)
                rsqrt(("mem", 1), MT, D)
                output_chunks(s + 1, "od_out", od_y, lambda c: c + 1, R, KC)
                seam(s + 1, od_y)

            dve.wait_ge(start_in, 16 * 3)
            for k in range(2):
                dve.tensor_tensor_reduce(out=lam_pr[:, k, :], in0=lam_in[:, 2 * k, :], in1=lam_in[:, 2 * k + 1, :],
                                         scale=1.0, scalar=0.0, op0=ALU.mult, op1=ALU.add,
                                         accum_out=lam[:, 1 + k:2 + k]).then_inc(dve_done, 1)
                n_small[0] += 1
            dve.wait_ge(lam_exp, 1)
            small(dve.tensor_scalar(lam[:, 0:1], lam[:, 4:5], lam[:, 3:4], LAM_INIT, ALU.subtract, ALU.subtract))
            dve.wait_ge(const_in, 48)
            small(dve.tensor_scalar(lam[:, 5:6], gains[:, G_SUB:G_SUB + 1], 1.0 - LAM_INIT, None, ALU.mult))
            for at_, to in ((0, 1), (3, 5), (7, 8)):
                half = gains[:, G_POST + KC * at_:G_POST + KC * to]
                small(dve.tensor_scalar(half, half, 0.5, None, ALU.mult))
            dve.wait_ge(x_in, 16 * KC)
            for c in range(KC):
                pre_norm(0, c)
            pre_norm_r(0)
            dve.wait_ge(lines_out, 16)
            ffn(0, 0)
            even_mixer(1)
            cross(2, 0)
            ffn(3, 1)
            ffn(4, 2)
            odd_mixer(5)
            cross(6, 1)
            ffn(7, 3)


def constants():
    c = np.zeros((P, C_END), np.float32)
    c[:, C_ID:C_ID + P] = np.eye(P)
    dist = (T - P) + np.arange(P)[:, None] - np.arange(T)[None, :]
    c[:, C_CAUSAL:C_CAUSAL + T] = np.where(dist < 0, NEG, 0.0)
    half = DR // 2
    inv = np.float32(10000.0) ** (-np.arange(half, dtype=np.float32) / np.float32(half))
    ang = np.arange(T, dtype=np.float32)[None, :] * inv[:, None]
    cos, sin = np.cos(ang), np.sin(ang)
    c[:, C_ROPE:C_ROPE + T] = np.concatenate([cos, cos, -sin, sin] * 2)
    row_ok = (np.arange(P) >= CMP_LEN - 1).astype(np.float32).reshape(P, 1)
    d = T - 1 - np.arange(LINE + 1)
    near = BUCKETS // 2
    ratio = np.log(np.maximum(d, 1).astype(np.float32) / np.float32(near)) / np.float32(math.log(MAX_DIST / near))
    far = np.minimum(near + (ratio * np.float32(BUCKETS - near)).astype(np.int32), BUCKETS - 1)
    bucket = np.where(d < 0, BUCKETS, np.where(d < near, d, far))
    onehot = np.zeros((BUCKETS + 1, LINE + 1), np.float32)
    onehot[bucket, np.arange(LINE + 1)] = np.where(d < 0, 1.0, DH ** 0.5)
    return c, onehot, row_ok


def tiles(w, kt, cols):
    return w.reshape(kt, P, cols, P).transpose(2, 1, 0, 3).reshape(cols, P, kt * P)


def vectors(g):
    return g.reshape(-1, P).T


def kernel(x, mem, rel_bias_table, norm_pre, norm_post, mem_norm, ffn_wg, ffn_wu, ffn_wd,
           ev_w_in, ev_cmp_pe, ev_cmp_w, ev_w_out, od_w_in, od_q_norm, od_kv_norm, od_w_uq,
           od_w_ukv, od_lambda, od_subln, od_w_out, xa_wq, xa_wkv, xa_wo):
    import concourse.bacc as bacc
    from concourse.bass_utils import run_bass_kernel_spmd

    consts, onehot, row_ok = constants()
    ins = {"consts": consts, "onehot": onehot, "row_ok": row_ok}
    ins["x"] = x[0].T.reshape(KC, P, T).transpose(1, 0, 2)
    ins["mem"] = mem[0].T.reshape(KC, P, MEM).transpose(1, 0, 2)
    ins["table"] = rel_bias_table
    ins["lam"] = od_lambda[0]
    ins["gains"] = np.concatenate([vectors(norm_pre), vectors(norm_post), vectors(mem_norm), vectors(od_q_norm),
                                   vectors(od_kv_norm), vectors(od_subln)], 1)
    wg, wu, wd = (w.reshape((2 * DEPTH,) + w.shape[2:]) for w in (ffn_wg, ffn_wu, ffn_wd))
    ins["w_up"] = np.stack([np.stack([tiles(wg[f], KC, FC), tiles(wu[f], KC, FC)], 1).reshape(2 * FC, P, D)
                            for f in range(2 * DEPTH)])
    ins["w_down"] = np.stack([tiles(wd[f], FC, KC) for f in range(2 * DEPTH)])
    w = ev_w_in[0]
    sizes = (A_HEADS * DH, 12 * DH, 3 * A_HEADS, B_HEADS * DH, DH, DH, IDX_HEADS * IDX_DH, IDX_DH, IDX_HEADS)
    at = np.cumsum((0,) + sizes)
    qa, kva, ga, qb, kb, vb, iq, ik, iw = (w[:, at[n]:at[n + 1]] for n in range(9))
    pair = [qa[:, DH * h:DH * h + DH] for c in range(4) for h in (c, c + 4)]
    cols = [iq, ik, ik, ik, ik, vb, ga, iw, ik, kb, kb, qb, kva] + pair
    ins["w_ev_in"] = tiles(np.concatenate(cols, 1), KC, EV_IN)
    ins["w_ev_out"] = tiles(ev_w_out[0], KC, KC)
    ins["cmp_w"] = np.concatenate([ev_cmp_w[0].transpose(2, 0, 1, 3)] * 2)
    ins["cmp_pe"] = np.concatenate([ev_cmp_pe[0].transpose(2, 0, 1)] * 2)
    w = od_w_in[0]
    cq, ckv, kr, rest = w[:, :256], w[:, 256:384], w[:, 384:416], w[:, 416:]
    cols = [cq, ckv, kr, kr[:, 16:], kr[:, :16], kr, kr, rest]
    ins["w_od_in"] = tiles(np.concatenate(cols, 1), KC, OD_IN)
    ins["w_od_out"] = tiles(od_w_out[0], KC, KC)
    q = od_w_uq[0].reshape(256, C_HEADS, DN + DR)
    q = np.concatenate([q, q[:, :, DN + DR // 2:], q[:, :, DN:DN + DR // 2]], 2).reshape(256, C_HEADS * P)
    ins["w_uq"] = tiles(q, 2, C_HEADS).reshape(2, 4, P, 2 * P).transpose(0, 2, 1, 3).reshape(2, P, D)
    kv = od_w_ukv[0].reshape(P, C_HEADS, 2, DN).transpose(0, 2, 1, 3)
    ins["w_ukv"] = kv.reshape(1, P, D)
    ins["w_xq"] = np.stack([tiles(w, KC, X_HEADS) for w in xa_wq])
    ins["w_xkv"] = np.stack([tiles(w, KC, 2 * X_HEADS) for w in xa_wkv])
    wo = np.stack([tiles(w, X_HEADS, KC) for w in xa_wo])
    ins["w_xo"] = wo.reshape(DEPTH, KC // 2, 2, P, 512).transpose(0, 1, 3, 2, 4).reshape(DEPTH, KC // 2, P, D)

    nc = bacc.Bacc("TRN2", target_bir_lowering=False, num_devices=1)
    arrays, aps = {}, {}
    for name, value in ins.items():
        arrays[f"in_{name}"] = np.ascontiguousarray(value)
        aps[name] = nc.dram_tensor(f"in_{name}", value.shape, F32, kind="ExternalInput").ap()
    aps["out"] = nc.dram_tensor("out", (P, KC, T), F32, kind="ExternalOutput").ap()
    build(nc, aps)
    r = run_bass_kernel_spmd(nc, [arrays], core_ids=[0])
    out = np.asarray(r.results[0]["out"])
    return out.transpose(1, 0, 2).reshape(D, T).T[None]
```

```python
import math

import numpy as np
import concourse.bass as bass
from concourse import mybir

F32, F32R, BF16, I32 = mybir.dt.float32, mybir.dt.float32r, mybir.dt.bfloat16, mybir.dt.int32
ACT, ALU = mybir.ActivationFunctionType, mybir.AluOpType

P = 128
D, T, MEM, DFF, DEPTH = 1024, 512, 256, 2816, 2
KC = D // P
NT = T // P
MT = MEM // P
FC = DFF // P
BUCKETS, MAX_DIST = 32, 128
A_HEADS, B_HEADS, C_HEADS, D_HEADS, X_HEADS = 8, 8, 8, 4, 4
BIAS_HEADS = A_HEADS + B_HEADS + D_HEADS
DH, IDX_HEADS, IDX_DH, TOPK = 64, 8, 32, 128
CMP_LEN, CMP_STRIDE = 32, 16
N_CMP = (T - CMP_LEN) // CMP_STRIDE + 1
DN, DR, DV = 64, 32, 128
EPS = 1e-6
NEG = -1e30
TAKEN = -3e38
LAM_INIT = 0.8 - 0.6 * math.exp(-0.3)
LINE = T + P - 1
RSQRT_SEED = float(0x5F3759DF)

R = 4
N_LOGIT, N_PROB, N_PROBT = 3, 5, 3
TURN_AT, OUT_AT = 3, 4
DOWN_TILES = (8, 7, 7)
EV_IN, OD_IN = 19, 16
IQ, IK, VG, KB, QB, KCMP, VCMP, KS, VS, KW, VW, QA = 0, 2, 3, 4, 5, 9, 10, 11, 12, 13, 14, 15
CQ, CKV, KR, DQ, DK, DVT = 0, 2, 3, 4, 8, 12

C_ID, C_CAUSAL, C_ROPE, C_END = 0, P, P + T, P + 2 * T
G_PRE, G_POST, G_MEM, G_Q, G_KV, G_SUB = 0, 64, 128, 144, 146, 147
G_END = 148


def plan():
    units, chunks, u, c = {}, {}, 0, 0
    def add(name, nu, nc_):
        nonlocal u, c
        units[name], chunks[name] = u, c
        u, c = u + nu, c + nc_
    def ffn(n):
        add(f"up{n}", 2 * FC, 2 * FC)
        add(f"down{n}", 3 * KC, KC)
    def cross(n):
        add(f"xq{n}", X_HEADS, X_HEADS)
        add(f"xkv{n}", 2 * X_HEADS, 2 * X_HEADS)
        add(f"xo{n}", KC // 2, KC)
    ffn(0)
    add("ev_in", EV_IN, EV_IN)
    add("ev_out", KC, KC)
    cross(0)
    ffn(1)
    ffn(2)
    add("od_in", OD_IN, OD_IN)
    add("uq", 2, C_HEADS)
    add("ukv", 1, 4)
    add("od_out", KC, KC)
    cross(1)
    ffn(3)
    return units, chunks, u


def attention_jobs():
    even = [(k, h, i) for h in range(A_HEADS) for i in range(NT) for k in ("cmp", "slc", "win")]
    even += [("dsa", h, i) for h in range(B_HEADS) for i in range(NT)]
    diff = [(f"diff{e}", h, i) for h in range(D_HEADS) for i in range(NT) for e in range(2)]
    mla = [("mla", h, i) for h in range(C_HEADS) for i in range(NT)]
    cross = [("x", h, i) for h in range(X_HEADS) for i in range(NT)]
    return [even, cross, diff, mla, cross]


def build(nc, a):
    UNIT, CHUNK, N_UNITS = plan()
    JOBS = attention_jobs()
    JOB0 = [sum(len(j) for j in JOBS[:n]) for n in range(len(JOBS))]

    base = -(-nc.sbuf_base // 32) * 32

    class Region:
        def __init__(self, at):
            self.at = at

        def put(self, name, shape, dt):
            size = int(np.prod(shape[1:])) * (2 if dt == BF16 else 4)
            t = nc.alloc_sbuf_tensor_at(name, shape, dt, offset=self.at)
            self.at += -(-size // 32) * 32
            assert self.at <= nc.sbuf_usable_end, (name, self.at)
            return t

    keep = Region(base)
    x = keep.put("x_res", [P, KC, T], F32)
    raw = [keep.put(f"w_raw{j}", [P, KC * P], F32) for j in range(R)]
    w_hi = [keep.put(f"w_hi{j}", [P, KC * P], F32R) for j in range(R)]
    w_lo = [keep.put(f"w_lo{j}", [P, KC * P], F32R) for j in range(R)]
    at_h = keep.at
    h_hi = keep.put("h_hi", [P, KC, T], F32R)
    h_lo = keep.put("h_lo", [P, KC, T], F32R)
    y_ffn = Region(at_h).put("y_ffn", [P, KC, T], F32)
    r_sb = keep.put("r_tok", [P, T], F32)
    sq = [keep.put(f"sq{j}", [P, T], F32) for j in range(2)]
    sq_sum = keep.put("sq_sum", [P, T], F32)
    step = [keep.put(f"step{j}", [P, T], F32) for j in range(2)]
    gains = keep.put("gains", [P, G_END], F32)
    ident = keep.put("ident", [P, P], F32)
    ident_bf = keep.put("ident_bf", [P, P], BF16)
    ones = keep.put("ones", [P, 1], F32)
    zero = keep.put("zero", [P, 1], F32)
    row_ok = keep.put("row_ok", [P, 1], F32)
    rs = keep.put("rsqrt_tmp", [P, 4, 16], F32)
    lam = keep.put("lam", [P, 8], F32)
    neg_max = keep.put("neg_max", [P, 8], F32)
    row_sum = keep.put("row_sum", [P, 8], F32)
    coef = keep.put("coef", [P, 8], F32)
    at_var = keep.at

    m = Region(at_var)
    act_hi = m.put("act_hi", [P, FC, T], F32R)
    act_lo = m.put("act_lo", [P, FC, T], F32R)
    gate = [m.put(f"gate{j}", [P, T], F32) for j in range(2)]
    up = [m.put(f"up{j}", [P, T], F32) for j in range(2)]

    def attention_buffers(m, tag):
        return ([m.put(f"{tag}_logit{j}", [P, T], F32) for j in range(N_LOGIT)],
                [m.put(f"{tag}_prob{j}", [P, T], F32) for j in range(N_PROB)],
                [m.put(f"{tag}_probT{j}", [P, T], F32) for j in range(N_PROBT)])

    m = Region(at_var)
    ev = m.put("ev_proj", [P, EV_IN, T], F32)
    ev_v = m.put("ev_v_rows", [P, 3, NT, P], F32)
    gates = m.put("gates", [P, NT, 3 * A_HEADS], F32)
    kcT = m.put("k_cmpT", [P, 32], F32)
    vc = m.put("v_cmp", [P, P], F32)
    at = m.at
    ev_bufs = attention_buffers(m, "ev")
    n = Region(at)
    cmp_w = n.put("cmp_w", [P, 2, CMP_LEN // 2, DH], F32)
    cmp_x = n.put("cmp_x", [P, 2, CMP_LEN // 2, 2, N_CMP], F32)
    vcT = n.put("v_cmpT", [DH, 2, N_CMP], F32)
    taken_mask = m.put("sel_mask", [P, NT - 1, T], BF16)
    ev_strip = [m.put(f"ev_strip{j}", [P, T], F32) for j in range(3)]
    cmp_pe = m.put("cmp_pe", [P, 2, CMP_LEN], F32)
    ev_causal = m.put("ev_causal", [P, T], F32)
    top8 = m.put("top8", [P, 8], F32)
    at = m.at
    n = Region(at)
    score = [n.put(f"score{j}", [P, T], F32) for j in range(3)]
    relu = [n.put(f"relu{j}", [P, T], F32) for j in range(2)]
    ev_y = Region(at).put("ev_y", [P, KC, T], F32)
    k_st = [[Region(at + 4096 * n + 2048 * p).put(f"k_st{n}_{p}", [P, T], F32R) for p in range(2)] for n in range(4)]
    k_st.append([Region(at_var + 2048 * c).put(f"k_st4_{c}", [P, T], F32R) for c in (KCMP, VCMP)])
    q_st = [Region(at_var + 2048 * j).put(f"q_st{j}", [P, T], F32R) for j in range(4)]

    m = Region(at_var)
    at_od = m.at
    od = m.put("od_proj", [P, OD_IN, T], F32)
    at_dv = m.at
    dv = m.put("diff_v", [P, D_HEADS, NT, P], F32)
    od_bufs = attention_buffers(m, "od")
    cq_hi = m.put("cq_hi", [P, 2, T], F32R)
    cq_lo = m.put("cq_lo", [P, 2, T], F32R)
    ckv_hi = m.put("ckv_hi", [P, T], F32R)
    ckv_lo = m.put("ckv_lo", [P, T], F32R)
    at = m.at
    od_strip = [m.put(f"od_strip{j}", [P, T], F32) for j in range(3)]
    od_causal = Region(at).put("od_causal", [P, T], F32)
    rope_t = m.put("rope_table", [P, T], F32)
    at = m.at
    diff_o = m.put("diff_o", [P, D_HEADS, T], F32)
    diff_sq = m.put("diff_sq", [P, D_HEADS, T], F32)
    od_y = Region(at).put("od_y", [P, KC, T], F32)
    n = Region(at_od)
    mla_v = n.put("mla_v", [P, NT, T], F32)
    mla_q = n.put("mla_q", [P, C_HEADS, T], F32)
    mla_k = n.put("mla_k", [P, C_HEADS, T], F32)

    m = Region(at_var)
    mem_sb = m.put("mem_sb", [P, KC, MEM], F32)
    mem_hi = m.put("mem_hi", [P, KC, MEM], F32R)
    mem_lo = m.put("mem_lo", [P, KC, MEM], F32R)
    r_mem = m.put("r_mem", [P, MEM], F32)
    mem_sq = [m.put(f"mem_sq{j}", [P, MEM], F32) for j in range(2)]
    mem_sum = m.put("mem_sum", [P, MEM], F32)
    xq = m.put("x_q", [P, X_HEADS, T], F32)
    xkv = m.put("x_kv", [P, 2 * X_HEADS, MEM], F32)
    xv = m.put("x_v", [P, X_HEADS, MT, P], F32)
    x_bufs = attention_buffers(m, "x")
    x_y = m.put("x_y", [P, KC, T], F32)

    m = Region(at_var)
    onehot = m.put("onehot", [BUCKETS + 1, LINE + 1], F32)
    table = m.put("table", [BUCKETS + 1, BIAS_HEADS], F32)
    lines = m.put("lines", [BIAS_HEADS, LINE + 1], F32)
    lam_in = m.put("lam_in", [P, 4, DH], F32)
    lam_pr = m.put("lam_pr", [P, 2, DH], F32)
    lines_dram = nc.dram_tensor("bias_lines", [BIAS_HEADS, LINE + 1], F32, kind="Internal").ap()
    line_rows = nc.dram_tensor("bias_line_rows", [BIAS_HEADS, P, LINE + 1], F32, kind="Internal").ap()

    bank = [nc.alloc_psum_tensor(f"bank{b}", [P, 512], F32) for b in range(8)]
    B_STAT, B_RT = 4, 5
    B_S, B_T, B_O = (0, 1, 2), (6, 7), (3, 4)

    sems = {}

    def sem(name):
        sems.setdefault(name, nc.alloc_semaphore(name))
        return sems[name]

    raw_loaded = [sem(f"raw_loaded{j}") for j in range(R)]
    slot_taken = sem("slot_taken")
    hi_split = sem("hi_split")
    split_done = sem("split_done")
    unit_done = sem("unit_done")
    chunk_out = sem("chunk_out")
    silu_done = sem("silu_done")
    prod_done = sem("prod_done")
    act_hi_done = sem("act_hi_done")
    act_done = sem("act_done")
    sq_done = sem("sq_done")
    sq_added = sem("sq_added")
    stat_done = sem("stat_done")
    rsqrt_done = sem("rsqrt_done")
    r_turned = sem("r_turned")
    r_copied = sem("r_copied")
    x_done = sem("x_done")
    hi_done = sem("hi_done")
    lo_done = sem("lo_done")
    dve_done = sem("dve_done")
    turned = sem("turned")
    rows_done = sem("rows_done")
    mask_done = sem("mask_done")
    k_hi_done = sem("k_hi_done")
    k_lo_done = sem("k_lo_done")
    q_hi_done = sem("q_hi_done")
    q_lo_done = sem("q_lo_done")
    cmp_x_done = sem("cmp_x_done")
    qk_done = sem("qk_done")
    logit_done = sem("logit_done")
    exp_done = sem("exp_done")
    probT_done = sem("probT_done")
    probT_copied = sem("probT_copied")
    pv_done = sem("pv_done")
    coef_done = sem("coef_done")
    scaled = sem("scaled")
    idx_done = sem("idx_done")
    relu_done = sem("relu_done")
    idx_added = sem("idx_added")
    cmp_done = sem("cmp_done")
    gate_exp = sem("gate_exp")
    lam_exp = sem("lam_exp")
    q_nope = sem("q_nope")
    mla_ready = sem("mla_ready")
    diff_out = sem("diff_out")
    sub_sq = sem("sub_sq")
    sub_turned = sem("sub_turned")
    sub_normed = sem("sub_normed")
    sub_hi = sem("sub_hi")
    sub_lo = sem("sub_lo")
    strip_in = [sem(f"strip_in{j}") for j in range(3)]
    const_in = sem("const_in")
    x_in = sem("x_in")
    start_in = sem("start_in")
    lines_out = sem("lines_out")
    aux_in = sem("aux_in")
    out_done = sem("out_done")
    ones_set = sem("ones_set")

    AUX = {"ev": 48, "mem0": 64, "rope": 80, "od_causal": 96, "mem1": 112}

    SQ = {}
    n_sq = n_stat = n_rs = n_rt = n_cp = 0
    for kind, k in [("pre", 0), ("post", 1), ("pre", 1), ("mem", 0), ("post", 2), ("pre", 2), ("post", 3), ("pre", 3),
                    ("post", 4), ("pre", 4), ("post", 5), ("pre", 5), ("cq", 0), ("ckv", 0), ("sub", 0), ("mem", 1),
                    ("post", 6), ("pre", 6), ("post", 7), ("pre", 7), ("post", 8)]:
        SQ[kind, k] = dict(sq=n_sq, stat=n_stat, rs=n_rs, rt=n_rt, cp=n_cp)
        n_sq += {"cq": 2, "ckv": 1, "sub": 0}.get(kind, 8)
        n_stat += {"pre": 8}.get(kind, 1)
        n_rs += 1
        n_rt += kind != "sub"
        n_cp += kind in ("pre", "mem")
    ADD = {("post", k): 6 * (k - 1) + 7 * (k >= 2) + 7 * (k >= 6) for k in range(1, 9)}
    ADD["mem", 0], ADD["mem", 1] = 6, 6 * 5 + 7

    X0 = {s: KC * max(s - 1, 0) for s in range(9)}
    SPLIT, n_split = {}, 0
    for name, k in [("pre0", 8), ("pre1", 8), ("ev_o", 8), ("mem0", 8), ("pre2", 8), ("xo0", 4), ("pre3", 8),
                    ("pre4", 8), ("pre5", 8), ("cq", 2), ("ckv", 1), ("od_o", 4), ("mem1", 8), ("pre6", 8),
                    ("xo1", 4), ("pre7", 8)]:
        SPLIT[name] = n_split
        n_split += k
    TURN, n_turn = {}, 1
    for name, k in [("vg", 1), ("ev_v", 2), ("xv0", 4), ("dv", 4), ("xv1", 4)]:
        TURN[name] = n_turn
        n_turn += k
    V_ROWS = {"vg": 2, "ev_v": 3, "xv0": 9, "dv": 13, "xv1": 17}

    def strip_use(g):
        return g % 3, 16 * (g // 3 + 1)

    def kind_of(job):
        phase, (kind, h, i) = job
        w = P * (i + 1)
        q = slice(P * i, P * i + P)
        off = T - P - P * i
        e = DH * (h % 2)
        s = dict(blocks=i + 1, rows=P, w=w, mask=None, k_lo=None, scale=-DH ** -0.5, factor=None,
                 out=(h // 2, slice(e, e + DH), q))
        if kind in ("cmp", "slc", "win"):
            g, e = h // 4, 64 * (h // 4)
            s["q"] = ev[e:e + DH, QA + h % 4, q]
            b = ("cmp", "slc", "win").index(kind)
            s["factor"] = gates[:, i, 3 * h + b:3 * h + b + 1]
            s["strip"] = h
            if kind == "cmp":
                n = 8 * i + 7
                s.update(w=n, blocks=1, rows=n, k=kcT[e:e + DH, 0:n], v=[vc[0:n, e:e + DH]],
                         bias=ev_strip[h % 3][:, off + CMP_LEN - 1:off + CMP_LEN - 1 + CMP_STRIDE * (n - 1) + 1:CMP_STRIDE])
            else:
                n = 2 * (b - 1) + g
                s.update(q=q_st[h % 4][:, q], k=k_st[n][0][:, 0:w], k_lo=k_st[n][1][:, 0:w])
                s["v"] = [ev_v[:, b - 1, j, e:e + DH] for j in range(i + 1)]
                s["bias"] = ev_strip[h % 3][:, off:off + w]
        elif kind == "dsa":
            e = DH * (h % 2)
            g = A_HEADS + h
            s.update(q=q_st[g % 4][:, q], k=k_st[4][0][:, 0:w], k_lo=k_st[4][1][:, 0:w], strip=g,
                     v=[ev_v[:, 2, j, 0:DH] for j in range(i + 1)], bias=ev_strip[g % 3][:, off:off + w],
                     out=(4 + h // 2, slice(e, e + DH), q), mask=taken_mask[:, i - 1, 0:w] if i else None)
        elif kind.startswith("diff"):
            e = int(kind[-1])
            g = A_HEADS + B_HEADS + h
            s.update(q=od[64 * e:64 * e + DH, DQ + h, q], k=od[64 * e:64 * e + DH, DK + h, 0:w], strip=g,
                     v=[dv[:, h, j, :] for j in range(i + 1)], bias=od_strip[g % 3][:, off:off + w],
                     out=(h, slice(0, P), q), factor=lam[:, 0:1] if e else None)
        elif kind == "mla":
            s.update(q=mla_q[0:DN + DR, h, q], k=mla_k[0:DN + DR, h, 0:w], scale=-(DN + DR) ** -0.5,
                     v=[mla_v[:, j, DH * h:DH * h + DH] for j in range(i + 1)],
                     bias=od_causal[:, off:off + w], strip=None)
        else:
            s.update(q=xq[:, h, q], k=xkv[:, h, :], scale=-P ** -0.5, w=MEM, blocks=MT,
                     v=[xv[:, h, j, :] for j in range(MT)], bias=zero[:, 0:1].to_broadcast([P, MEM]),
                     out=(h, slice(0, P), q), strip=None)
        return s

    OUT_KEY = ["ev_o", "xo0", None, "od_o", "xo1"]
    SUB_AT = 5
    BUFS = [ev_bufs, x_bufs, od_bufs, od_bufs, x_bufs]
    INFO = [[kind_of((p, job)) for job in jobs] for p, jobs in enumerate(JOBS)]

    for infos in INFO:
        for n, info in enumerate(infos):
            before, after = infos[n - 1]["out"] if n else None, infos[n + 1]["out"] if n + 1 < len(infos) else None
            info["opens"], info["closes"] = before != info["out"], after != info["out"]
            info["ends"] = after is None or after[0] != info["out"][0]

    def q_head(g):
        if g < A_HEADS:
            chunk, e = QA + g % 4, DH * (g // 4)
        else:
            chunk, e = QB + (g - A_HEADS) // 2, DH * (g % 2)
        other = DH - e
        return ev[e:e + DH, chunk, :], q_st[g % 4][e:e + DH, :], q_st[g % 4][other:other + DH, :]

    def coefs(info):
        return 2 if info["factor"] is not None else 1

    COEF0, n_coef = [], 0
    for infos in INFO:
        COEF0.append([])
        for info in infos:
            n_coef += coefs(info)
            COEF0[-1].append(n_coef)

    w_up, w_down = a["w_up"], a["w_down"]

    with nc.Block() as block:

        @block.sync
        def _(sp):
            sp.dma_start(ident[:], a["consts"][:, C_ID:C_ID + P]).then_inc(const_in, 16)
            sp.dma_start(gains[:], a["gains"]).then_inc(const_in, 16)
            sp.dma_start(row_ok[:], a["row_ok"]).then_inc(const_in, 16)
            for c in range(KC):
                sp.dma_start(x[:, c, :], a["x"][:, c, :]).then_inc(x_in, 16)

            def load(u, j, src, cols):
                sp.dma_start(raw[j][:, 0:cols], src).then_inc(raw_loaded[j], 16)

            def stream(u0, n, source, first=0, cols=KC * P):
                for k in range(first, n):
                    if (n - k) % R == 0:
                        break
                    if u0 + k >= R:
                        sp.wait_ge(split_done, u0 + k - R + 1)
                    load(u0 + k, (u0 + k) % R, source(k), cols)
                else:
                    return
                loops = (n - k) // R
                with sp.Fori(0, loops) as i:
                    for b in range(R):
                        sp.wait_ge(split_done, R * i + u0 + k + b - R + 1)
                        load(None, (u0 + k + b) % R, source(R * i + k + b), cols)

            def ffn(f):
                first = 0
                if f == 0:
                    for k in range(R):
                        load(k, k, w_up[0, k], KC * P)
                    first = R
                stream(UNIT[f"up{f}"], 2 * FC, lambda k: w_up[f, k], first)
                u0 = UNIT[f"down{f}"]
                with sp.Fori(0, KC // R) as i:
                    for b in range(3 * R):
                        n, part = b // 3, b % 3
                        at, t = P * sum(DOWN_TILES[:part]), P * DOWN_TILES[part]
                        sp.wait_ge(split_done, 3 * R * i + u0 + b - R + 1)
                        load(None, (u0 + b) % R, w_down[f, R * i + n][:, at:at + t], t)

            ffn(0)
            stream(UNIT["ev_in"], EV_IN, lambda k: a["w_ev_in"][k])
            stream(UNIT["ev_out"], KC, lambda k: a["w_ev_out"][k])
            for n in range(2):
                if n == 1:
                    ffn(1)
                    ffn(2)
                    stream(UNIT["od_in"], OD_IN, lambda k: a["w_od_in"][k])
                    stream(UNIT["uq"], 2, lambda k: a["w_uq"][k])
                    stream(UNIT["ukv"], 1, lambda k: a["w_ukv"][k])
                    stream(UNIT["od_out"], KC, lambda k: a["w_od_out"][k])
                stream(UNIT[f"xq{n}"], X_HEADS, lambda k: a["w_xq"][n, k])
                stream(UNIT[f"xkv{n}"], 2 * X_HEADS, lambda k: a["w_xkv"][n, k])
                stream(UNIT[f"xo{n}"], KC // 2, lambda k: a["w_xo"][n, k])
            ffn(3)
            for c in range(KC):
                sp.wait_ge(x_done, X0[8] + c + 1)
                sp.dma_start(a["out"][:, c, :], x[:, c, :]).then_inc(out_done, 16)
            sp.wait_ge(out_done, 16 * KC)
            sp.wait_ge(lines_out, 32)

        @block.gpsimd
        def _(pool):
            pool.memset(ones[:], 1.0).then_inc(ones_set, 1)
            pool.memset(zero[:], 0.0).then_inc(ones_set, 1)
            pool.memset(table[:], NEG).then_inc(ones_set, 1)

            def split(j, cols, u, loaded, free):
                pool.wait_ge(raw_loaded[j], loaded)
                if free is not None:
                    pool.wait_ge(unit_done, free)
                pool.sem_inc(slot_taken, 1)
                pool.tensor_scalar(w_hi[j][:, 0:cols], raw[j][:, 0:cols], 1.0, 0.0, ALU.mult, ALU.add).then_inc(hi_split, 1)
                pool.wait_ge(hi_split, u + 1)
                pool.tensor_tensor(w_lo[j][:, 0:cols], raw[j][:, 0:cols], w_hi[j][:, 0:cols].bitcast(F32),
                                   ALU.subtract).then_inc(split_done, 1)

            def straight(u, cols=KC * P):
                split(u % R, cols, u, 16 * (u // R + 1), u - R + 1 if u >= R else None)

            def units(u0, n, first=0):
                for k in range(first, n):
                    if (n - k) % R == 0:
                        break
                    straight(u0 + k)
                else:
                    return
                with pool.Fori(0, (n - k) // R) as i:
                    for b in range(R):
                        u = u0 + k + b
                        split(u % R, KC * P, R * i + u, 16 * i + 16 * (u // R + 1), R * i + u - R + 1)

            def ffn(f):
                first = 0
                if f == 0:
                    for u in range(R):
                        straight(u)
                    first = R
                units(UNIT[f"up{f}"], 2 * FC, first)
                u0 = UNIT[f"down{f}"]
                with pool.Fori(0, KC // R) as i:
                    for b in range(3 * R):
                        u = u0 + b
                        split(u % R, P * DOWN_TILES[b % 3], 3 * R * i + u, 48 * i + 16 * (u // R + 1), 3 * R * i + u - R + 1)

            ffn(0)
            units(UNIT["ev_in"], EV_IN)
            units(UNIT["ev_out"], KC)
            for n in range(2):
                if n == 1:
                    ffn(1)
                    ffn(2)
                    units(UNIT["od_in"], OD_IN)
                    units(UNIT["uq"], 2)
                    units(UNIT["ukv"], 1)
                    units(UNIT["od_out"], KC)
                units(UNIT[f"xq{n}"], X_HEADS)
                units(UNIT[f"xkv{n}"], 2 * X_HEADS)
                units(UNIT[f"xo{n}"], KC // 2)
            ffn(3)

        @block.tensor
        def _(pe):
            def product(b, j, tile, hi, lo, first, last, n=T):
                w = slice(P * tile, P * tile + P)
                pe.matmul(bank[b][:, 0:n], w_hi[j][:, w], hi, start=first, stop=False)
                pe.matmul(bank[b][:, 0:n], w_hi[j][:, w], lo, start=False, stop=False)
                return pe.matmul(bank[b][:, 0:n], w_lo[j][:, w], hi, start=False, stop=last)

            def chunk_of_unit(u, c, j, b, hi, lo, n=T):
                pe.wait_ge(split_done, u + 1)
                pe.wait_ge(chunk_out, c - R + 1)
                for k in range(KC):
                    mm = product(b, j, k, hi[:, k, 0:n], lo[:, k, 0:n], k == 0, k == KC - 1, n)
                mm.then_inc(unit_done, 1)

            def chunks(name, n, first, hi, lo, cols=T):
                u0, c0 = UNIT[name], CHUNK[name]
                for k in range(first, n):
                    if (n - k) % R == 0:
                        break
                    chunk_of_unit(u0 + k, c0 + k, (u0 + k) % R, (c0 + k) % R, hi, lo, cols)
                else:
                    return
                with pe.Fori(0, (n - k) // R) as i:
                    for b in range(R):
                        chunk_of_unit(R * i + u0 + k + b, R * i + c0 + k + b, (u0 + k + b) % R, (c0 + k + b) % R,
                                      hi, lo, cols)

            def sums(src, tiles, first, last):
                for i in range(tiles):
                    mm = pe.matmul(bank[B_STAT][:, i:i + 1], src[:, P * i:P * i + P], ones[:],
                                   start=first and i == 0, stop=last, skip_group_check=True)
                return mm

            def turn_r(key, tiles):
                pe.wait_ge(rsqrt_done, SQ[key]["rs"] + 1)
                for i in range(tiles):
                    mm = pe.transpose(bank[B_RT][:, P * i:P * i + P], rs[:, 3, i:i + 1].to_broadcast([P, P]), ident[:])
                mm.then_inc(r_turned, 1)

            def post_norm(s):
                key = ("post", s)
                pe.wait_ge(sq_added, ADD[key] + 6)
                pe.wait_ge(sq_done, SQ[key]["sq"] + KC)
                sums(sq_sum, NT, True, False)
                sums(sq[1], NT, False, True).then_inc(stat_done, 1)
                turn_r(key, NT)

            def pre_norm(s, name):
                key, u0, c0 = ("pre", s), UNIT[name], CHUNK[name]
                for c in range(KC):
                    pe.wait_ge(sq_done, SQ[key]["sq"] + c + 1)
                    sums(sq[c % 2], NT, c == 0, c == KC - 1).then_inc(stat_done, 1)
                    if c == 0:
                        pe.wait_ge(split_done, u0 + R)
                        if c0:
                            pe.wait_ge(chunk_out, c0)
                    pe.wait_ge(lo_done, SPLIT[f"pre{s}"] + c + 1)
                    for k in range(R):
                        mm = product((c0 + k) % R, (u0 + k) % R, c, h_hi[:, c, :], h_lo[:, c, :], c == 0, c == KC - 1)
                        if c == KC - 1:
                            mm.then_inc(unit_done, 1)
                turn_r(key, NT)

            def ffn(s, f):
                pre_norm(s, f"up{f}")
                chunks(f"up{f}", 2 * FC, R, h_hi, h_lo)
                u0, c0 = UNIT[f"down{f}"], CHUNK[f"down{f}"]
                with pe.Fori(0, KC // R) as i:
                    for b in range(3 * R):
                        n, part, j = b // 3, b % 3, (u0 + b) % R
                        k0, tiles = sum(DOWN_TILES[:part]), DOWN_TILES[part]
                        pe.wait_ge(split_done, 3 * R * i + u0 + b + 1)
                        if part == 0:
                            pe.wait_ge(chunk_out, R * i + c0 + n - R + 1)
                        pe.wait_ge(act_done, FC * f + k0 + tiles)
                        for k in range(tiles):
                            mm = product((c0 + n) % R, j, k, act_hi[:, k0 + k, :], act_lo[:, k0 + k, :],
                                         k0 + k == 0, k0 + k == FC - 1)
                        mm.then_inc(unit_done, 1)
                post_norm(s + 1)

            def turn_rows(key, k, src, tiles):
                n = TURN[key] + k
                for i in range(tiles):
                    mm = pe.transpose(bank[B_T[n % 2]][:, P * i:P * i + P], src[:, P * i:P * i + P], ident[:])
                mm.then_inc(turned, 1)

            def attention(phase, hooks={}):
                infos, j0 = INFO[phase], JOB0[phase]
                probs, probTs = BUFS[phase][1:]
                n = len(infos)

                def logit(s):
                    j, info = j0 + s, infos[s]
                    if s >= 3:
                        pe.wait_ge(logit_done, j - 2)
                    if info["mask"] is not None and JOBS[phase][s][1] == 0:
                        pe.wait_ge(mask_done, JOBS[phase][s][2])
                    out = bank[B_S[s % 3]][:, 0:info["w"]]
                    if phase == 0 and JOBS[0][s][2] == 0 and JOBS[0][s][0] in ("cmp", "dsa"):
                        pe.wait_ge(q_lo_done, info["strip"] + 1)
                    more = info["mask"] is not None
                    if info["k_lo"] is not None:
                        pe.matmul(out, info["q"], info["k"], start=True, stop=False)
                        mm = pe.matmul(out, info["q"], info["k_lo"], start=False, stop=not more)
                    else:
                        mm = pe.matmul(out, info["q"], info["k"], start=True, stop=not more)
                    if info["mask"] is not None:
                        mm = pe.matmul(out, ident_bf[:], info["mask"], start=False, stop=True)
                    mm.then_inc(qk_done, 1)

                def turn(s):
                    j, info = j0 + s, infos[s]
                    pe.wait_ge(scaled, j + 1)
                    if s >= 2:
                        pe.wait_ge(probT_copied, j - 1)
                    for b in range(info["blocks"]):
                        mm = pe.transpose(bank[B_T[s % 2]][0:info["rows"], P * b:P * b + P],
                                          probs[s % N_PROB][:, P * b:P * b + info["rows"]], ident[:])
                    mm.then_inc(probT_done, 1)

                def output(s):
                    j, info = j0 + s, infos[s]
                    chunk, features, tokens = info["out"]
                    pe.wait_ge(probT_copied, j + 1)
                    if chunk >= 2 and info["opens"] and tokens.start == 0 and features.start == 0:
                        if phase == 2:
                            pe.wait_ge(sub_sq, chunk - 1)
                        else:
                            pe.wait_ge(lo_done, SPLIT[OUT_KEY[phase]] + chunk - 1)
                    for b, v in enumerate(info["v"]):
                        mm = pe.matmul(bank[B_O[chunk % 2]][features, tokens], v,
                                       probTs[s % N_PROBT][0:info["rows"], P * b:P * b + P],
                                       start=info["opens"] and b == 0, stop=info["closes"] and b == info["blocks"] - 1)
                    mm.then_inc(pv_done, 1)

                for s in range(n + OUT_AT):
                    if s < n:
                        logit(s)
                    if TURN_AT <= s < n + TURN_AT:
                        turn(s - TURN_AT)
                    if s >= OUT_AT:
                        output(s - OUT_AT)
                    if s in hooks:
                        hooks[s]()

            def out_projection(name, s, mem):
                u0, c0 = UNIT[name], CHUNK[name]
                for k in range(KC):
                    if k == R:
                        key = ("mem", mem)
                        pe.wait_ge(sq_added, ADD[key] + 7)
                        sums(mem_sum, MT, True, True).then_inc(stat_done, 1)
                    if k == R + 1:
                        turn_r(("mem", mem), MT)
                    chunk_of_unit(u0 + k, c0 + k, (u0 + k) % R, (c0 + k) % R, h_hi, h_lo)
                post_norm(s + 1)

            def even_mixer(s):
                pre_norm(s, "ev_in")
                c0 = CHUNK["ev_in"]
                pe.wait_ge(chunk_out, c0 + 4)
                turn_rows("vg", 0, ev[:, VG, :], NT)
                banks = (B_STAT, B_RT, B_T[(TURN["vg"] + 1) % 2])
                for k in range((NT - 1) * IDX_HEADS):
                    i, h = 1 + k // IDX_HEADS, k % IDX_HEADS
                    e = IDX_DH * (h % 4)
                    if k >= 3:
                        pe.wait_ge(relu_done, k - 2)
                    pe.matmul(bank[banks[k % 3]][:, 0:P * (i + 1)], ev[e:e + IDX_DH, IQ + h // 4, P * i:P * i + P],
                              ev[e:e + IDX_DH, IK, 0:P * (i + 1)], start=True, stop=True).then_inc(idx_done, 1)
                chunks("ev_in", EV_IN, R, h_hi, h_lo)
                pe.wait_ge(relu_done, (NT - 1) * IDX_HEADS)
                pe.wait_ge(rows_done, V_ROWS["vg"] + 1)
                for k, src in enumerate((VS, VW)):
                    pe.wait_ge(chunk_out, c0 + src + 1)
                    turn_rows("ev_v", k, ev[:, src, :], NT)
                pe.wait_ge(aux_in, AUX["ev"])
                pe.wait_ge(chunk_out, c0 + EV_IN)
                for kv in range(2):
                    pe.wait_ge(cmp_x_done, 4 * kv + 4)
                    for l in range(CMP_LEN // 2):
                        mm = pe.matmul(bank[kv][0:DH, 0:2 * N_CMP], cmp_w[:, kv, l, :], cmp_x[:, kv, l, :, :],
                                       start=l == 0, stop=l == CMP_LEN // 2 - 1)
                    mm.then_inc(cmp_done, 1)
                pe.wait_ge(rows_done, V_ROWS["ev_v"] + 5)
                for g in range(2):
                    mm = pe.transpose(bank[2][0:N_CMP, DH * g:DH * g + DH], vcT[:, g, :], ident[0:DH, 0:DH])
                mm.then_inc(cmp_done, 1)
                pe.wait_ge(rows_done, V_ROWS["ev_v"] + 2 + 4)
                pe.wait_ge(k_lo_done, 9)
                attention(0)
                pe.wait_ge(lo_done, SPLIT["ev_o"] + KC)
                out_projection("ev_out", s, 0)

            def cross(s, n):
                pre_norm(s, f"xq{n}")
                pe.wait_ge(lo_done, SPLIT[f"mem{n}"] + KC)
                chunks(f"xkv{n}", 2 * X_HEADS, 0, mem_hi, mem_lo, MEM)
                for h in range(X_HEADS):
                    if h >= 2:
                        pe.wait_ge(rows_done, V_ROWS[f"xv{n}"] + h - 1)
                    pe.wait_ge(chunk_out, CHUNK[f"xkv{n}"] + X_HEADS + h + 1)
                    turn_rows(f"xv{n}", h, xkv[:, X_HEADS + h, :], MT)
                pe.wait_ge(rows_done, V_ROWS[f"xv{n}"] + X_HEADS)
                attention(1 if n == 0 else 4)
                u0, c0 = UNIT[f"xo{n}"], CHUNK[f"xo{n}"]
                pe.wait_ge(lo_done, SPLIT[f"xo{n}"] + X_HEADS)
                for c in range(KC):
                    if c % 2 == 0:
                        pe.wait_ge(split_done, u0 + c // 2 + 1)
                    pe.wait_ge(chunk_out, c0 + c - R + 1)
                    for k in range(X_HEADS):
                        mm = product((c0 + c) % R, (u0 + c // 2) % R, X_HEADS * (c % 2) + k, h_hi[:, k, :],
                                     h_lo[:, k, :], k == 0, k == X_HEADS - 1)
                    if c % 2:
                        mm.then_inc(unit_done, 1)
                post_norm(s + 1)

            def odd_mixer(s):
                pre_norm(s, "od_in")
                c0 = CHUNK["od_in"]
                chunks("od_in", OD_IN, R, h_hi, h_lo)
                pe.wait_ge(sq_done, SQ["cq", 0]["sq"] + 2)
                sums(sq[0], NT, True, False)
                sums(sq[1], NT, False, True).then_inc(stat_done, 1)
                turn_r(("cq", 0), NT)
                for h in range(D_HEADS):
                    if h >= 2:
                        pe.wait_ge(rows_done, V_ROWS["dv"] + h - 1)
                    pe.wait_ge(chunk_out, c0 + DVT + h + 1)
                    turn_rows("dv", h, od[:, DVT + h, :], NT)
                pe.wait_ge(sq_done, SQ["ckv", 0]["sq"] + 1)
                sums(sq[0], NT, True, True).then_inc(stat_done, 1)
                turn_r(("ckv", 0), NT)
                pe.wait_ge(rows_done, V_ROWS["dv"] + D_HEADS)
                attention(2)
                pe.wait_ge(sub_sq, D_HEADS)
                for h in range(D_HEADS):
                    for i in range(NT):
                        n = NT * h + i
                        mm = pe.matmul(bank[B_STAT][:, n:n + 1], diff_sq[:, h, P * i:P * i + P], ones[:],
                                       start=n == 0, stop=n == NT * D_HEADS - 1, skip_group_check=True)
                mm.then_inc(stat_done, 1)
                u0, c0 = UNIT["uq"], CHUNK["uq"]
                pe.wait_ge(lo_done, SPLIT["ckv"] + 1)
                for h in range(C_HEADS):
                    if h % R == 0:
                        pe.wait_ge(split_done, u0 + h // R + 1)
                        if h:
                            pe.wait_ge(chunk_out, c0 + h)
                            pe.wait_ge(q_nope, h)
                    for k in range(2):
                        mm = product((c0 + h) % R, (u0 + h // R) % R, 2 * (h % R) + k, cq_hi[:, k, :], cq_lo[:, k, :],
                                     k == 0, k == 1)
                    if h % R == R - 1:
                        mm.then_inc(unit_done, 1)
                u0, c0 = UNIT["ukv"], CHUNK["ukv"]
                j = u0 % R
                pe.wait_ge(split_done, u0 + 1)
                pe.wait_ge(rsqrt_done, SQ["sub", 0]["rs"] + 1)
                for i in range(NT):
                    tok = slice(P * i, P * i + P)
                    out = bank[4 + i][:]
                    pe.matmul(out, ckv_hi[:, tok], w_hi[j][:, T:2 * T], start=True, stop=False)
                    pe.matmul(out, ckv_hi[:, tok], w_lo[j][:, T:2 * T], start=False, stop=False)
                    pe.matmul(out, ckv_lo[:, tok], w_hi[j][:, T:2 * T], start=False, stop=True)
                pe.wait_ge(chunk_out, c0)
                pe.wait_ge(q_nope, C_HEADS)
                for m_ in range(4):
                    mm = product((c0 + m_) % R, j, m_, ckv_hi[:], ckv_lo[:], True, True)
                mm.then_inc(unit_done, 1)
                pe.wait_ge(chunk_out, c0 + 4)
                pe.wait_ge(q_nope, C_HEADS + 4 + 2)
                pe.wait_ge(mla_ready, 5)

                def turn_sub(h):
                    if h:
                        pe.wait_ge(sub_normed, h)
                    for i in range(NT):
                        r = rs[:, 3, NT * h + i:NT * h + i + 1].to_broadcast([P, P])
                        mm = pe.transpose(bank[B_RT][:, P * i:P * i + P], r, ident[:])
                    mm.then_inc(sub_turned, 1)

                attention(3, {SUB_AT * (h + 1): lambda h=h: turn_sub(h) for h in range(D_HEADS)})
                pe.wait_ge(lo_done, SPLIT["od_o"] + 4)
                pe.wait_ge(sub_lo, D_HEADS)
                out_projection("od_out", s, 1)

            pe.wait_ge(start_in, 16 * 3)
            pe.wait_ge(ones_set, 3)
            pe.matmul(bank[0][0:BIAS_HEADS, 0:512], table[:], onehot[:, 0:512], start=True, stop=True)
            pe.matmul(bank[1][0:BIAS_HEADS, 0:LINE + 1 - 512], table[:], onehot[:, 512:LINE + 1], start=True,
                      stop=True).then_inc(turned, 1)
            pe.wait_ge(rows_done, 2)
            pe.wait_ge(const_in, 48)
            ffn(0, 0)
            even_mixer(1)
            cross(2, 0)
            ffn(3, 1)
            ffn(4, 2)
            odd_mixer(5)
            cross(6, 1)
            ffn(7, 3)

        @block.scalar
        def _(act):
            def pre_norm(s):
                key = ("pre", s)
                for c in range(KC):
                    if s:
                        act.wait_ge(x_done, X0[s] + c + 1)
                    else:
                        act.wait_ge(x_in, 16 * KC)
                    g = G_PRE + KC * s + c
                    act.activation(h_hi[:, c, :], x[:, c, :], ACT.Copy, scale=gains[:, g:g + 1]).then_inc(hi_done, 1)
                    if c >= 2:
                        act.wait_ge(stat_done, SQ[key]["stat"] + c - 1)
                    act.activation(sq[c % 2][:], x[:, c, :], ACT.Square).then_inc(sq_done, 1)
                act.wait_ge(r_turned, SQ[key]["rt"] + 1)
                act.activation(r_sb[:], bank[B_RT][:], ACT.Copy).then_inc(r_copied, 1)

            def squares(s, name, y, n0=0, n1=KC):
                key = ("post", s)
                for c in range(n0, n1):
                    act.wait_ge(chunk_out, CHUNK[name] + c + 1)
                    if c >= 3:
                        act.wait_ge(sq_added, ADD[key] + c - 2)
                    act.activation((sq_sum if c == 0 else sq[c % 2])[:], y[:, c, :], ACT.Square).then_inc(sq_done, 1)

            def ffn(s, f):
                pre_norm(s)
                c0 = CHUNK[f"up{f}"]
                with act.Fori(0, FC // 2) as i:
                    for p in range(2):
                        act.wait_ge(chunk_out, 4 * i + c0 + 2 * p + 1)
                        act.activation(gate[p][:], gate[p][:], ACT.Silu).then_inc(silu_done, 1)
                squares(s + 1, f"down{f}", y_ffn)

            def copy_rows(key, k, dst, tiles):
                n = TURN[key] + k
                act.wait_ge(turned, n + 1)
                src = bank[B_T[n % 2]][:, 0:P * tiles].rearrange("p (i t) -> p i t", i=tiles)
                act.activation(dst, src, ACT.Copy).then_inc(rows_done, 1)

            def q_high(g):
                src, hi, _ = q_head(g)
                act.activation(hi, src, ACT.Copy).then_inc(q_hi_done, 1)

            def load_strip(g, bufs):
                slot, _ = strip_use(g)
                src = bass.AP(line_rows.tensor, P * (LINE + 1) * g + P - 1, [[LINE, P], [1, T]])
                act.dma_start(bufs[slot][:], src).then_inc(strip_in[slot], 16)

            def attention(phase, strips=None, buf=None, hooks={}):
                infos, j0 = INFO[phase], JOB0[phase]
                logits, probs, probTs = BUFS[phase]
                seen = set()
                if strips:
                    for g in range(strips[0], min(strips[0] + 3, strips[1])):
                        load_strip(g, buf)

                def exp(s):
                    j, info = j0 + s, infos[s]
                    act.wait_ge(logit_done, j + 1)
                    g = info["strip"]
                    new = strips and g not in seen
                    if new:
                        if seen and g + 2 < strips[1]:
                            load_strip(g + 2, buf)
                        seen.add(g)
                    if s >= N_PROB:
                        act.wait_ge(probT_done, j - N_PROB + 1)
                    w = info["w"]
                    act.activation(probs[s % N_PROB][:, 0:w], logits[s % N_LOGIT][:, 0:w], ACT.Exp, scale=-1.0,
                                   bias=neg_max[:, j % 8:j % 8 + 1],
                                   accum_out=row_sum[:, j % 8:j % 8 + 1]).then_inc(exp_done, 1)
                    if phase == 0 and new and g + 2 < strips[1]:
                        q_high(g + 2)

                def copy(s):
                    j, info = j0 + s, infos[s]
                    act.wait_ge(probT_done, j + 1)
                    if s >= N_PROBT:
                        act.wait_ge(pv_done, j - N_PROBT + 1)
                    w = P * info["blocks"]
                    act.activation(probTs[s % N_PROBT][0:info["rows"], 0:w], bank[B_T[s % 2]][0:info["rows"], 0:w],
                                   ACT.Copy).then_inc(probT_copied, 1)

                def chunk_out_(s):
                    f = infos[s]["out"][0]
                    act.wait_ge(pv_done, j0 + s + 1)
                    src = bank[B_O[f % 2]][:]
                    if phase == 2:
                        act.activation(diff_o[:, f, :], src, ACT.Copy).then_inc(diff_out, 1)
                        act.activation(diff_sq[:, f, :], src, ACT.Square).then_inc(sub_sq, 1)
                    else:
                        act.activation(h_hi[:, f, :], src, ACT.Copy).then_inc(hi_done, 1)

                for s in range(len(infos) + OUT_AT + 1):
                    if s < len(infos):
                        exp(s)
                    if TURN_AT <= s < len(infos) + TURN_AT:
                        copy(s - TURN_AT)
                    if s > OUT_AT and infos[s - OUT_AT - 1]["ends"]:
                        chunk_out_(s - OUT_AT - 1)
                    if s in hooks:
                        hooks[s]()

            def memory(n, split_key):
                act.wait_ge(lo_done, SPLIT[split_key] + (KC if n == 0 else 4))
                act.dma_start(mem_sb[:], a["mem"]).then_inc(aux_in, 16)
                act.wait_ge(aux_in, AUX[f"mem{n}"])
                for c in range(KC):
                    g = G_MEM + KC * n + c
                    act.activation(mem_hi[:, c, :], mem_sb[:, c, :], ACT.Copy, scale=gains[:, g:g + 1]).then_inc(hi_done, 1)
                    if c >= 3:
                        act.wait_ge(sq_added, ADD["mem", n] + c - 2)
                    act.activation((mem_sum if c == 0 else mem_sq[c % 2])[:], mem_sb[:, c, :],
                                   ACT.Square).then_inc(sq_done, 1)

            def memory_r(n):
                act.wait_ge(r_turned, SQ["mem", n]["rt"] + 1)
                act.activation(r_mem[:], bank[B_RT][:, 0:MEM], ACT.Copy).then_inc(r_copied, 1)

            def even_mixer(s):
                pre_norm(s)
                act.dma_start(cmp_w[:], a["cmp_w"]).then_inc(aux_in, 16)
                act.dma_start(cmp_pe[:], a["cmp_pe"]).then_inc(aux_in, 16)
                act.dma_start(ev_causal[:], a["consts"][:, C_CAUSAL:C_CAUSAL + T]).then_inc(aux_in, 16)
                act.wait_ge(lines_out, 32)
                copy_rows("vg", 0, ev_v[:, 2, :, :], NT)
                act.wait_ge(rows_done, V_ROWS["vg"] + 1)
                act.activation(gates[:], ev_v[:, 2, :, DH:DH + 3 * A_HEADS], ACT.Exp, scale=-1.0).then_inc(gate_exp, 1)
                banks = (B_STAT, B_RT, B_T[(TURN["vg"] + 1) % 2])
                for k in range((NT - 1) * IDX_HEADS):
                    i = 1 + k // IDX_HEADS
                    act.wait_ge(idx_done, k + 1)
                    if k >= 2:
                        act.wait_ge(idx_added, k - 1)
                    act.activation(relu[k % 2][:, 0:P * (i + 1)], bank[banks[k % 3]][:, 0:P * (i + 1)],
                                   ACT.Relu).then_inc(relu_done, 1)
                copy_rows("ev_v", 0, ev_v[:, 0, :, :], NT)
                copy_rows("ev_v", 1, ev_v[:, 1, :, :], NT)
                act.wait_ge(cmp_done, 1)
                for g in range(2):
                    act.activation(kcT[DH * g:DH * g + DH, 0:N_CMP], bank[0][0:DH, N_CMP * g:N_CMP * g + N_CMP],
                                   ACT.Copy).then_inc(rows_done, 1)
                act.wait_ge(cmp_done, 2)
                act.activation(vcT[:], bank[1][0:DH, 0:2 * N_CMP], ACT.Copy).then_inc(rows_done, 1)
                act.wait_ge(mask_done, NT - 1)
                for n in range(4):
                    g, src = n % 2, (KS, KW)[n // 2]
                    e = slice(DH * g, DH * g + DH)
                    for half in range(2):
                        act.activation(k_st[n][0][DH * half:DH * half + DH, :], ev[e, src, :],
                                       ACT.Copy).then_inc(k_hi_done, 1)
                act.wait_ge(cmp_x_done, 8)
                act.activation(k_st[4][0][:], ev[:, KB, :], ACT.Copy).then_inc(k_hi_done, 1)
                act.wait_ge(cmp_done, 3)
                act.activation(vc[0:N_CMP, :], bank[2][0:N_CMP, 0:P], ACT.Copy).then_inc(rows_done, 1)
                q_high(0)
                q_high(1)
                attention(0, (0, A_HEADS + B_HEADS), ev_strip)
                memory(0, "ev_o")
                squares(s + 1, "ev_out", ev_y, 0, 5)
                memory_r(0)
                squares(s + 1, "ev_out", ev_y, 5, KC)

            def cross(s, n):
                pre_norm(s)
                for h in range(X_HEADS):
                    copy_rows(f"xv{n}", h, xv[:, h, :, :], MT)
                attention(1 if n == 0 else 4)
                squares(s + 1, f"xo{n}", x_y)

            def odd_mixer(s):
                pre_norm(s)
                act.dma_start(rope_t[:], a["consts"][:, C_ROPE:C_ROPE + T]).then_inc(aux_in, 16)
                c0 = CHUNK["od_in"]
                for k in range(2):
                    act.wait_ge(chunk_out, c0 + CQ + k + 1)
                    act.activation(sq[k][:], od[:, CQ + k, :], ACT.Square).then_inc(sq_done, 1)
                act.wait_ge(stat_done, SQ["cq", 0]["stat"] + 1)
                act.activation(sq[0][:], od[:, CKV, :], ACT.Square).then_inc(sq_done, 1)
                for h in range(2):
                    copy_rows("dv", h, dv[:, h, :, :], NT)
                for k in range(2):
                    act.wait_ge(mla_ready, k + 1)
                    act.activation(cq_hi[:, k, :], od[:, CQ + k, :], ACT.Copy).then_inc(hi_done, 1)
                for h in range(2, D_HEADS):
                    copy_rows("dv", h, dv[:, h, :, :], NT)
                act.wait_ge(mla_ready, 3)
                act.activation(ckv_hi[:], od[:, CKV, :], ACT.Copy).then_inc(hi_done, 1)
                attention(2, (A_HEADS + B_HEADS, BIAS_HEADS), od_strip)
                act.wait_ge(logit_done, JOB0[3])
                act.dma_start(od_causal[:], a["consts"][:, C_CAUSAL:C_CAUSAL + T]).then_inc(aux_in, 16)
                for h in range(C_HEADS):
                    act.wait_ge(unit_done, UNIT["uq"] + h // R + 1)
                    act.activation(mla_q[0:DN, h, :], bank[(CHUNK["uq"] + h) % R][0:DN, :], ACT.Copy).then_inc(q_nope, 1)
                act.wait_ge(unit_done, UNIT["ukv"] + 1)
                for k in range(4):
                    act.activation(mla_k[0:DN, 2 * k, :], bank[(CHUNK["ukv"] + k) % R][0:DN, :],
                                   ACT.Copy).then_inc(q_nope, 1)
                act.wait_ge(mla_ready, 4)
                for i in range(2):
                    act.activation(mla_v[:, i, :], bank[4 + i][:], ACT.Copy).then_inc(q_nope, 1)

                def sub_high(h):
                    act.wait_ge(sub_normed, h + 1)
                    act.activation(h_hi[:, 4 + h, :], diff_o[:, h, :], ACT.Copy).then_inc(sub_hi, 1)

                attention(3, hooks={SUB_AT * (h + 1) + 2: lambda h=h: sub_high(h) for h in range(D_HEADS)})
                act.wait_ge(sub_lo, D_HEADS)
                memory(1, "od_o")
                squares(s + 1, "od_out", od_y, 0, 5)
                memory_r(1)
                squares(s + 1, "od_out", od_y, 5, KC)

            act.wait_ge(ones_set, 3)
            act.dma_start(onehot[:], a["onehot"]).then_inc(start_in, 16)
            act.dma_start(table[0:BUCKETS, :], a["table"]).then_inc(start_in, 16)
            act.dma_start(lam_in[:], a["lam"].partition_broadcast(P)).then_inc(start_in, 16)
            act.wait_ge(turned, 1)
            act.activation(lines[:, 0:512], bank[0][0:BIAS_HEADS, :], ACT.Copy).then_inc(rows_done, 1)
            act.activation(lines[:, 512:LINE + 1], bank[1][0:BIAS_HEADS, 0:LINE + 1 - 512], ACT.Copy).then_inc(rows_done, 1)
            act.wait_ge(rows_done, 2)
            act.dma_start(lines_dram, lines[:]).then_inc(lines_out, 16)
            act.wait_ge(dve_done, 2)
            act.activation(lam[:, 3:5], lam[:, 1:3], ACT.Exp).then_inc(lam_exp, 1)
            act.wait_ge(const_in, 48)
            act.activation(ident_bf[:], ident[:], ACT.Copy).then_inc(lam_exp, 1)
            act.wait_ge(lines_out, 16)
            rows = bass.AP(lines_dram.tensor, 0, [[LINE + 1, BIAS_HEADS], [0, P], [1, LINE + 1]])
            act.dma_start(line_rows, rows).then_inc(lines_out, 16)
            ffn(0, 0)
            even_mixer(1)
            cross(2, 0)
            ffn(3, 1)
            ffn(4, 2)
            odd_mixer(5)
            cross(6, 1)
            ffn(7, 3)

        @block.vector
        def _(dve):
            n_small = [0]

            def small(ins):
                n_small[0] += 1
                ins.then_inc(dve_done, 1)
                dve.wait_ge(dve_done, n_small[0])

            def rsqrt(key, w, d, stats=1, src=None):
                value, half, y = (rs[:, k, 0:w] for k in (0, 2, 3))
                square = rs[:, 1, 0:w]
                if src is None:
                    dve.wait_ge(stat_done, SQ[key]["stat"] + stats)
                    src = bank[B_STAT][:, 0:w]
                small(dve.tensor_scalar(value, src, 1.0 / d, EPS, ALU.mult, ALU.add))
                small(dve.tensor_scalar(square.bitcast(I32), value.bitcast(I32), 1, None, ALU.logical_shift_right))
                small(dve.tensor_scalar(y.bitcast(I32), square.bitcast(I32), -1.0, RSQRT_SEED, ALU.mult, ALU.add))
                for k in range(4):
                    small(dve.tensor_tensor(square, y, y, ALU.mult))
                    small(dve.scalar_tensor_tensor(half, square, -0.5, value, ALU.mult, ALU.mult))
                    last = dve.scalar_tensor_tensor(y, half, 1.5, y, ALU.add, ALU.mult)
                    if k < 3:
                        small(last)
                last.then_inc(rsqrt_done, 1)

            def pre_norm(s, c):
                g = G_PRE + KC * s + c
                dve.wait_ge(hi_done, SPLIT[f"pre{s}"] + c + 1)
                dve.scalar_tensor_tensor(h_lo[:, c, :], x[:, c, :], gains[:, g:g + 1], h_hi[:, c, :].bitcast(F32),
                                         ALU.mult, ALU.subtract).then_inc(lo_done, 1)

            def pre_norm_r(s):
                rsqrt(("pre", s), NT, D, KC)
                dve.wait_ge(r_copied, SQ["pre", s]["cp"] + 1)

            def seam(s, y):
                rsqrt(("post", s), NT, D)
                dve.wait_ge(r_turned, SQ["post", s]["rt"] + 1)

                def scaled(c):
                    g = G_POST + KC * (s - 1) + c
                    if c >= 2:
                        dve.wait_ge(x_done, X0[s] + c - 1)
                    dve.scalar_tensor_tensor(step[c % 2][:], y[:, c, :], gains[:, g:g + 1], bank[B_RT][:],
                                             ALU.mult, ALU.mult).then_inc(dve_done, 1)
                    n_small[0] += 1

                scaled(0)
                for c in range(KC):
                    if c + 1 < KC:
                        scaled(c + 1)
                    dve.wait_ge(dve_done, n_small[0] - (c + 1 < KC))
                    dve.tensor_tensor(x[:, c, :], x[:, c, :], step[c % 2][:], ALU.add).then_inc(x_done, 1)
                    if s < 8 and c >= 1:
                        pre_norm(s, c - 1)
                if s < 8:
                    pre_norm(s, KC - 1)
                    pre_norm_r(s)

            def leave(name, c, unit, dst, r):
                dve.wait_ge(unit_done, UNIT[name] + unit)
                b = (CHUNK[name] + c) % R
                dve.tensor_tensor(dst, bank[b][:, 0:r.shape[-1]], r, ALU.mult).then_inc(chunk_out, 1)

            def output_chunks(s, name, y, unit_of, c0=0, c1=KC):
                key = ("post", s)

                def add(c):
                    dve.wait_ge(sq_done, SQ[key]["sq"] + c + 1)
                    if c > 1:
                        dve.wait_ge(sq_added, ADD[key] + c - 1)
                    dve.tensor_tensor(sq_sum[:], sq_sum[:], sq[c % 2][:], ALU.add).then_inc(sq_added, 1)

                for c in range(c0, c1):
                    dve.wait_ge(unit_done, UNIT[name] + unit_of(c))
                    dve.tensor_copy(y[:, c, :], bank[(CHUNK[name] + c) % R][:]).then_inc(chunk_out, 1)
                    if c >= 2:
                        add(c - 1)

            def ffn(s, f):
                u0, c0 = UNIT[f"up{f}"], CHUNK[f"up{f}"]
                with dve.Fori(0, FC // 2) as i:
                    for p in range(2):
                        k = 2 * p
                        dve.wait_ge(unit_done, 4 * i + u0 + k + 1)
                        dve.tensor_tensor(gate[p][:], bank[(c0 + k) % R][:], r_sb[:], ALU.mult).then_inc(chunk_out, 1)
                        dve.wait_ge(unit_done, 4 * i + u0 + k + 2)
                        dve.tensor_tensor(up[p][:], bank[(c0 + k + 1) % R][:], r_sb[:], ALU.mult).then_inc(chunk_out, 1)
                        dve.wait_ge(silu_done, 2 * i + FC * f + p + 1)
                        dve.wait_ge(chunk_out, 4 * i + c0 + k + 2)
                        dve.tensor_tensor(up[p][:], gate[p][:], up[p][:], ALU.mult).then_inc(prod_done, 1)
                        dve.wait_ge(prod_done, 2 * i + FC * f + p + 1)
                        dve.tensor_scalar(act_hi[:, 2 * i + p, :], up[p][:], 1.0, None, ALU.mult).then_inc(act_hi_done, 1)
                        dve.wait_ge(act_hi_done, 2 * i + FC * f + p + 1)
                        dve.tensor_tensor(act_lo[:, 2 * i + p, :], up[p][:], act_hi[:, 2 * i + p, :].bitcast(F32),
                                          ALU.subtract).then_inc(act_done, 1)
                output_chunks(s + 1, f"down{f}", y_ffn, lambda c: 3 * (c + 1))
                seam(s + 1, y_ffn)

            def memory(n):
                key = ("mem", n)
                for c in range(KC):
                    g = G_MEM + KC * n + c
                    dve.wait_ge(hi_done, SPLIT[f"mem{n}"] + c + 1)
                    dve.scalar_tensor_tensor(mem_lo[:, c, :], mem_sb[:, c, :], gains[:, g:g + 1],
                                             mem_hi[:, c, :].bitcast(F32), ALU.mult, ALU.subtract).then_inc(lo_done, 1)
                    if c:
                        dve.wait_ge(sq_done, SQ[key]["sq"] + c + 1)
                        if c > 1:
                            dve.wait_ge(sq_added, ADD[key] + c - 1)
                        dve.tensor_tensor(mem_sum[:], mem_sum[:], mem_sq[c % 2][:], ALU.add).then_inc(sq_added, 1)

            def q_low(g):
                src, hi, lo = q_head(g)
                dve.wait_ge(q_hi_done, g + 1)
                dve.tensor_tensor(lo, src, hi.bitcast(F32), ALU.subtract).then_inc(q_lo_done, 1)

            def attention(phase, strips=False, hooks={}):
                infos, j0 = INFO[phase], JOB0[phase]
                logits, probs = BUFS[phase][0:2]
                n, seen = len(infos), set()

                def logit(s):
                    j, info = j0 + s, infos[s]
                    g = info["strip"]
                    if strips and g not in seen:
                        slot, count = strip_use(g)
                        dve.wait_ge(strip_in[slot], count)
                        seen.add(g)
                    dve.wait_ge(qk_done, j + 1)
                    if s >= N_LOGIT:
                        dve.wait_ge(exp_done, j - N_LOGIT + 1)
                    w = info["w"]
                    dve.tensor_tensor_reduce(out=logits[s % N_LOGIT][:, 0:w], in0=bank[B_S[s % 3]][:, 0:w], in1=info["bias"],
                                             scale=info["scale"], scalar=3e38, op0=ALU.add, op1=ALU.min,
                                             accum_out=neg_max[:, j % 8:j % 8 + 1]).then_inc(logit_done, 1)

                def factor(s):
                    j, info = j0 + s, infos[s]
                    col = slice(j % 8, j % 8 + 1)
                    dve.wait_ge(exp_done, j + 1)
                    dve.reciprocal(coef[:, col], row_sum[:, col]).then_inc(coef_done, 1)
                    if info["factor"] is not None:
                        dve.wait_ge(coef_done, COEF0[phase][s] - 1)
                        dve.tensor_tensor(coef[:, col], coef[:, col], info["factor"], ALU.mult).then_inc(coef_done, 1)
                    dve.wait_ge(coef_done, COEF0[phase][s])
                    prob = probs[s % N_PROB][:, 0:info["w"]]
                    dve.tensor_scalar(prob, prob, coef[:, col], None, ALU.mult).then_inc(scaled, 1)

                def low(s):
                    f = infos[s]["out"][0]
                    dve.wait_ge(hi_done, SPLIT[OUT_KEY[phase]] + f + 1)
                    dve.tensor_tensor(h_lo[:, f, :], bank[B_O[f % 2]][:], h_hi[:, f, :].bitcast(F32),
                                      ALU.subtract).then_inc(lo_done, 1)

                for s in range(n + OUT_AT + 2):
                    if s < n:
                        logit(s)
                    if 1 <= s < n + 1:
                        factor(s - 1)
                        g = infos[s - 1]["strip"]
                        if phase == 0 and g + 2 < A_HEADS + B_HEADS and (s == 1 or infos[s - 2]["strip"] != g):
                            q_low(g + 2)
                    if phase != 2 and s > OUT_AT + 1 and infos[s - OUT_AT - 2]["ends"]:
                        low(s - OUT_AT - 2)
                    if s in hooks:
                        hooks[s]()

            def even_mixer(s):
                out = [0]

                def leave_next():
                    c = out[0]
                    if c < EV_IN:
                        leave("ev_in", c, c + 1, ev[:, c, :], r_sb[:])
                        out[0] += 1

                for _ in range(4):
                    leave_next()
                dve.wait_ge(gate_exp, 1)
                small(dve.tensor_scalar(gates[:], gates[:], 1.0, None, ALU.add))
                small(dve.reciprocal(gates[:], gates[:]))
                first = gates[:, 0, 0:3 * A_HEADS:3]
                small(dve.tensor_scalar(first, first, row_ok[:], None, ALU.mult))
                dve.wait_ge(aux_in, AUX["ev"])
                for k in range((NT - 1) * IDX_HEADS):
                    i, h = 1 + k // IDX_HEADS, k % IDX_HEADS
                    w = P * (i + 1)
                    off = T - w
                    sc = score[i - 1][:, 0:w]
                    dve.wait_ge(relu_done, k + 1)
                    if h:
                        dve.wait_ge(idx_added, k)
                    dve.scalar_tensor_tensor(sc, relu[k % 2][:, 0:w], ev_v[:, 2, i, 88 + h:89 + h],
                                             sc if h else ev_causal[:, off:off + w], ALU.mult,
                                             ALU.add).then_inc(idx_added, 1)
                dve.wait_ge(idx_added, (NT - 1) * IDX_HEADS)
                for i in range(1, NT):
                    sc = score[i - 1][:, 0:P * (i + 1)]
                    for k in range(TOPK // 8):
                        small(dve.max(top8[:], sc))
                        small(dve.match_replace(sc, top8[:], sc, TAKEN))
                        if k % 3 == 2:
                            leave_next()
                    dve.tensor_scalar(taken_mask[:, i - 1, 0:P * (i + 1)], sc, TAKEN / 2, NEG, ALU.is_gt,
                                      ALU.mult).then_inc(mask_done, 1)
                for _ in range(EV_IN):
                    leave_next()
                dve.wait_ge(chunk_out, CHUNK["ev_in"] + EV_IN)
                for kv, src in enumerate((KCMP, VCMP)):
                    for g in range(2):
                        e = slice(DH * g, DH * g + DH)
                        proj = ev[e, src, :]
                        for odd in range(2):
                            blocks = bass.AP(proj.tensor, proj.offset + odd,
                                             [list(proj.ap[0]), [2, CMP_LEN // 2], [CMP_STRIDE, N_CMP]])
                            pe_ = cmp_pe[e, kv, odd:CMP_LEN:2].unsqueeze(2).to_broadcast([DH, CMP_LEN // 2, N_CMP])
                            dve.tensor_tensor(cmp_x[DH * odd:DH * odd + DH, kv, :, g, :], blocks, pe_,
                                              ALU.add).then_inc(cmp_x_done, 1)
                for n in range(4):
                    g, src = n % 2, (KS, KW)[n // 2]
                    e = slice(DH * g, DH * g + DH)
                    dve.wait_ge(k_hi_done, 2 * n + 2)
                    for half in range(2):
                        dve.tensor_tensor(k_st[n][1][DH * half:DH * half + DH, :], ev[e, src, :],
                                          k_st[n][0][e, :].bitcast(F32), ALU.subtract).then_inc(k_lo_done, 1)
                dve.wait_ge(k_hi_done, 9)
                dve.wait_ge(cmp_x_done, 8)
                dve.tensor_tensor(k_st[4][1][:], ev[:, KB, :], k_st[4][0][:].bitcast(F32), ALU.subtract).then_inc(k_lo_done, 1)
                q_low(0)
                q_low(1)
                attention(0, True)
                memory(0)
                output_chunks(s + 1, "ev_out", ev_y, lambda c: c + 1, 0, R)
                rsqrt(("mem", 0), MT, D)
                output_chunks(s + 1, "ev_out", ev_y, lambda c: c + 1, R, KC)
                seam(s + 1, ev_y)

            def cross(s, n):
                for h in range(X_HEADS):
                    leave(f"xq{n}", h, h + 1, xq[:, h, :], r_sb[:])
                dve.wait_ge(r_copied, SQ["mem", n]["cp"] + 1)
                for h in range(2 * X_HEADS):
                    leave(f"xkv{n}", h, h + 1, xkv[:, h, :], r_mem[:])
                attention(1 if n == 0 else 4)
                output_chunks(s + 1, f"xo{n}", x_y, lambda c: c // 2 + 1)
                seam(s + 1, x_y)

            def odd_mixer(s):
                for c in range(OD_IN):
                    leave("od_in", c, c + 1, od[:, c, :], r_sb[:])
                dve.wait_ge(chunk_out, CHUNK["od_in"] + OD_IN)
                for key, d, cs, g0, lo in ((("cq", 0), 2 * P, (CQ, CQ + 1), G_Q, (cq_lo[:, 0, :], cq_lo[:, 1, :])),
                                           (("ckv", 0), P, (CKV,), G_KV, (ckv_lo[:],))):
                    rsqrt(key, NT, d)
                    dve.wait_ge(r_turned, SQ[key]["rt"] + 1)
                    for k, c in enumerate(cs):
                        dve.scalar_tensor_tensor(od[:, c, :], od[:, c, :], gains[:, g0 + k:g0 + k + 1], bank[B_RT][:],
                                                 ALU.mult, ALU.mult).then_inc(mla_ready, 1)
                    for k, c in enumerate(cs):
                        hi = cq_hi[:, k, :] if key[0] == "cq" else ckv_hi[:]
                        dve.wait_ge(hi_done, SPLIT[key[0]] + k + 1)
                        dve.tensor_tensor(lo[k], od[:, c, :], hi.bitcast(F32), ALU.subtract).then_inc(lo_done, 1)
                attention(2, True)
                rsqrt(("sub", 0), NT * D_HEADS, DV)
                dve.wait_ge(aux_in, AUX["rope"])
                e = slice(DN, DN + DR)
                small(dve.tensor_tensor(step[1][e, :], od[0:DR, KR, :], rope_t[0:DR, :], ALU.mult))
                small(dve.tensor_tensor(step[0][e, :], od[DR:2 * DR, KR, :], rope_t[DR:2 * DR, :], ALU.mult))
                small(dve.tensor_tensor(step[1][e, :], step[1][e, :], step[0][e, :], ALU.add))
                dve.tensor_copy(mla_k[e, :, :], step[1][e, :].unsqueeze(1).to_broadcast([DR, C_HEADS, T])).then_inc(mla_ready, 1)
                for h in range(C_HEADS):
                    b = (CHUNK["uq"] + h) % R
                    dve.wait_ge(unit_done, UNIT["uq"] + h // R + 1)
                    dve.tensor_tensor(mla_q[e, h, :], bank[b][e, :], rope_t[e, :], ALU.mult).then_inc(dve_done, 1)
                    n_small[0] += 1
                    dve.tensor_tensor(step[h % 2][e, :], bank[b][DN + DR:P, :], rope_t[DN + DR:P, :], ALU.mult).then_inc(chunk_out, 1)
                    dve.wait_ge(chunk_out, CHUNK["uq"] + h + 1)
                    dve.wait_ge(dve_done, n_small[0])
                    small(dve.tensor_tensor(mla_q[e, h, :], mla_q[e, h, :], step[h % 2][e, :], ALU.add))
                dve.wait_ge(unit_done, UNIT["ukv"] + 1)
                for k in range(4):
                    dve.tensor_copy(mla_k[0:DN, 2 * k + 1, :], bank[(CHUNK["ukv"] + k) % R][DN:P, :]).then_inc(chunk_out, 1)
                dve.wait_ge(chunk_out, CHUNK["ukv"] + 4)
                small(dve.tensor_copy(mla_v[:, 2, :], bank[6][:]))
                dve.tensor_copy(mla_v[:, 3, :], bank[7][:]).then_inc(mla_ready, 1)
                dve.wait_ge(mla_ready, 5)
                dve.wait_ge(aux_in, AUX["od_causal"])

                def norm_sub(h):
                    dve.wait_ge(sub_turned, h + 1)
                    dve.wait_ge(diff_out, h + 1)
                    dve.scalar_tensor_tensor(diff_o[:, h, :], diff_o[:, h, :], lam[:, 5:6], bank[B_RT][:],
                                             ALU.mult, ALU.mult).then_inc(sub_normed, 1)

                def sub_low(h):
                    dve.wait_ge(sub_hi, h + 1)
                    dve.tensor_tensor(h_lo[:, 4 + h, :], diff_o[:, h, :], h_hi[:, 4 + h, :].bitcast(F32),
                                      ALU.subtract).then_inc(sub_lo, 1)

                hooks = {SUB_AT * (h + 1) + 1: lambda h=h: norm_sub(h) for h in range(D_HEADS)}
                hooks.update({SUB_AT * (h + 1) + 3: lambda h=h: sub_low(h) for h in range(D_HEADS)})
                attention(3, hooks=hooks)
                memory(1)
                output_chunks(s + 1, "od_out", od_y, lambda c: c + 1, 0, R)
                rsqrt(("mem", 1), MT, D)
                output_chunks(s + 1, "od_out", od_y, lambda c: c + 1, R, KC)
                seam(s + 1, od_y)

            dve.wait_ge(start_in, 16 * 3)
            for k in range(2):
                dve.tensor_tensor_reduce(out=lam_pr[:, k, :], in0=lam_in[:, 2 * k, :], in1=lam_in[:, 2 * k + 1, :],
                                         scale=1.0, scalar=0.0, op0=ALU.mult, op1=ALU.add,
                                         accum_out=lam[:, 1 + k:2 + k]).then_inc(dve_done, 1)
                n_small[0] += 1
            dve.wait_ge(lam_exp, 1)
            small(dve.tensor_scalar(lam[:, 0:1], lam[:, 4:5], lam[:, 3:4], LAM_INIT, ALU.subtract, ALU.subtract))
            dve.wait_ge(const_in, 48)
            small(dve.tensor_scalar(lam[:, 5:6], gains[:, G_SUB:G_SUB + 1], 1.0 - LAM_INIT, None, ALU.mult))
            for at_, to in ((0, 1), (3, 5), (7, 8)):
                half = gains[:, G_POST + KC * at_:G_POST + KC * to]
                small(dve.tensor_scalar(half, half, 0.5, None, ALU.mult))
            dve.wait_ge(x_in, 16 * KC)
            for c in range(KC):
                pre_norm(0, c)
            pre_norm_r(0)
            dve.wait_ge(lines_out, 16)
            ffn(0, 0)
            even_mixer(1)
            cross(2, 0)
            ffn(3, 1)
            ffn(4, 2)
            odd_mixer(5)
            cross(6, 1)
            ffn(7, 3)


def constants():
    c = np.zeros((P, C_END), np.float32)
    c[:, C_ID:C_ID + P] = np.eye(P)
    dist = (T - P) + np.arange(P)[:, None] - np.arange(T)[None, :]
    c[:, C_CAUSAL:C_CAUSAL + T] = np.where(dist < 0, NEG, 0.0)
    half = DR // 2
    inv = np.float32(10000.0) ** (-np.arange(half, dtype=np.float32) / np.float32(half))
    ang = np.arange(T, dtype=np.float32)[None, :] * inv[:, None]
    cos, sin = np.cos(ang), np.sin(ang)
    c[:, C_ROPE:C_ROPE + T] = np.concatenate([cos, cos, -sin, sin] * 2)
    row_ok = (np.arange(P) >= CMP_LEN - 1).astype(np.float32).reshape(P, 1)
    d = T - 1 - np.arange(LINE + 1)
    near = BUCKETS // 2
    ratio = np.log(np.maximum(d, 1).astype(np.float32) / np.float32(near)) / np.float32(math.log(MAX_DIST / near))
    far = np.minimum(near + (ratio * np.float32(BUCKETS - near)).astype(np.int32), BUCKETS - 1)
    bucket = np.where(d < 0, BUCKETS, np.where(d < near, d, far))
    onehot = np.zeros((BUCKETS + 1, LINE + 1), np.float32)
    onehot[bucket, np.arange(LINE + 1)] = np.where(d < 0, 1.0, DH ** 0.5)
    return c, onehot, row_ok


def tiles(w, kt, cols):
    return w.reshape(kt, P, cols, P).transpose(2, 1, 0, 3).reshape(cols, P, kt * P)


def vectors(g):
    return g.reshape(-1, P).T


def kernel(x, mem, rel_bias_table, norm_pre, norm_post, mem_norm, ffn_wg, ffn_wu, ffn_wd,
           ev_w_in, ev_cmp_pe, ev_cmp_w, ev_w_out, od_w_in, od_q_norm, od_kv_norm, od_w_uq,
           od_w_ukv, od_lambda, od_subln, od_w_out, xa_wq, xa_wkv, xa_wo):
    import concourse.bacc as bacc
    from concourse.bass_utils import run_bass_kernel_spmd

    consts, onehot, row_ok = constants()
    ins = {"consts": consts, "onehot": onehot, "row_ok": row_ok}
    ins["x"] = x[0].T.reshape(KC, P, T).transpose(1, 0, 2)
    ins["mem"] = mem[0].T.reshape(KC, P, MEM).transpose(1, 0, 2)
    ins["table"] = rel_bias_table
    ins["lam"] = od_lambda[0]
    ins["gains"] = np.concatenate([vectors(norm_pre), vectors(norm_post), vectors(mem_norm), vectors(od_q_norm),
                                   vectors(od_kv_norm), vectors(od_subln)], 1)
    wg, wu, wd = (w.reshape((2 * DEPTH,) + w.shape[2:]) for w in (ffn_wg, ffn_wu, ffn_wd))
    ins["w_up"] = np.stack([np.stack([tiles(wg[f], KC, FC), tiles(wu[f], KC, FC)], 1).reshape(2 * FC, P, D)
                            for f in range(2 * DEPTH)])
    ins["w_down"] = np.stack([tiles(wd[f], FC, KC) for f in range(2 * DEPTH)])
    w = ev_w_in[0]
    sizes = (A_HEADS * DH, 12 * DH, 3 * A_HEADS, B_HEADS * DH, DH, DH, IDX_HEADS * IDX_DH, IDX_DH, IDX_HEADS)
    at = np.cumsum((0,) + sizes)
    qa, kva, ga, qb, kb, vb, iq, ik, iw = (w[:, at[n]:at[n + 1]] for n in range(9))
    pair = [qa[:, DH * h:DH * h + DH] for c in range(4) for h in (c, c + 4)]
    cols = [iq, ik, ik, ik, ik, vb, ga, iw, ik, kb, kb, qb, kva] + pair
    ins["w_ev_in"] = tiles(np.concatenate(cols, 1), KC, EV_IN)
    ins["w_ev_out"] = tiles(ev_w_out[0], KC, KC)
    w = ev_cmp_w[0].reshape(2, CMP_LEN // 2, 2, DH, DH)
    ins["cmp_w"] = w.transpose(2, 3, 0, 1, 4).reshape(P, 2, CMP_LEN // 2, DH)
    ins["cmp_pe"] = np.concatenate([ev_cmp_pe[0].transpose(2, 0, 1)] * 2)
    w = od_w_in[0]
    cq, ckv, kr, rest = w[:, :256], w[:, 256:384], w[:, 384:416], w[:, 416:]
    cols = [cq, ckv, kr, kr[:, 16:], kr[:, :16], kr, kr, rest]
    ins["w_od_in"] = tiles(np.concatenate(cols, 1), KC, OD_IN)
    ins["w_od_out"] = tiles(od_w_out[0], KC, KC)
    q = od_w_uq[0].reshape(256, C_HEADS, DN + DR)
    q = np.concatenate([q, q[:, :, DN + DR // 2:], q[:, :, DN:DN + DR // 2]], 2).reshape(256, C_HEADS * P)
    ins["w_uq"] = tiles(q, 2, C_HEADS).reshape(2, 4, P, 2 * P).transpose(0, 2, 1, 3).reshape(2, P, D)
    kv = od_w_ukv[0].reshape(P, C_HEADS, 2, DN).transpose(0, 2, 1, 3)
    ins["w_ukv"] = kv.reshape(1, P, D)
    ins["w_xq"] = np.stack([tiles(w, KC, X_HEADS) for w in xa_wq])
    ins["w_xkv"] = np.stack([tiles(w, KC, 2 * X_HEADS) for w in xa_wkv])
    wo = np.stack([tiles(w, X_HEADS, KC) for w in xa_wo])
    ins["w_xo"] = wo.reshape(DEPTH, KC // 2, 2, P, 512).transpose(0, 1, 3, 2, 4).reshape(DEPTH, KC // 2, P, D)

    nc = bacc.Bacc("TRN2", target_bir_lowering=False, num_devices=1)
    arrays, aps = {}, {}
    for name, value in ins.items():
        arrays[f"in_{name}"] = np.ascontiguousarray(value)
        aps[name] = nc.dram_tensor(f"in_{name}", value.shape, F32, kind="ExternalInput").ap()
    aps["out"] = nc.dram_tensor("out", (P, KC, T), F32, kind="ExternalOutput").ap()
    build(nc, aps)
    r = run_bass_kernel_spmd(nc, [arrays], core_ids=[0])
    out = np.asarray(r.results[0]["out"])
    return out.transpose(1, 0, 2).reshape(D, T).T[None]
```

```python
import math

import numpy as np
import concourse.bass as bass
from concourse import mybir

F32, F32R, BF16, I32 = mybir.dt.float32, mybir.dt.float32r, mybir.dt.bfloat16, mybir.dt.int32
ACT, ALU = mybir.ActivationFunctionType, mybir.AluOpType

P = 128
D, T, MEM, DFF, DEPTH = 1024, 512, 256, 2816, 2
KC = D // P
NT = T // P
MT = MEM // P
FC = DFF // P
BUCKETS, MAX_DIST = 32, 128
A_HEADS, B_HEADS, C_HEADS, D_HEADS, X_HEADS = 8, 8, 8, 4, 4
BIAS_HEADS = A_HEADS + B_HEADS + D_HEADS
DH, IDX_HEADS, IDX_DH, TOPK = 64, 8, 32, 128
CMP_LEN, CMP_STRIDE = 32, 16
N_CMP = (T - CMP_LEN) // CMP_STRIDE + 1
GC = 32
DN, DR, DV = 64, 32, 128
EPS = 1e-6
NEG = -1e30
TAKEN = -3e38
LAM_INIT = 0.8 - 0.6 * math.exp(-0.3)
LINE = T + P - 1
RSQRT_SEED = float(0x5F3759DF)

R = 4
N_LOGIT, N_PROB, N_PROBT = 3, 5, 3
SCALE_AT, TURN_AT, OUT_AT = 3, 4, 6
DOWN_TILES = (8, 7, 7)
EV_IN, OD_IN = 19, 16
IQ, IK, VG, KB, QB, KCMP, VCMP, KS, VS, KW, VW, QA = 0, 2, 3, 4, 5, 9, 10, 11, 12, 13, 14, 15
CQ, CKV, KR, DQ, DK, DVT = 0, 2, 3, 4, 8, 12

C_ID, C_CAUSAL, C_ROPE, C_END = 0, P, P + T, P + 3 * T
G_PRE, G_POST, G_MEM, G_Q, G_KV, G_SUB = 0, 64, 128, 144, 146, 147
G_END = 148


def plan():
    units, chunks, u, c = {}, {}, 0, 0
    def add(name, nu, nc_):
        nonlocal u, c
        units[name], chunks[name] = u, c
        u, c = u + nu, c + nc_
    def ffn(n):
        add(f"up{n}", 2 * FC, 2 * FC)
        add(f"down{n}", 3 * KC, KC)
    def cross(n):
        add(f"xkv{n}", 2 * X_HEADS, 2 * X_HEADS)
        add(f"xq{n}", X_HEADS, X_HEADS)
        add(f"xo{n}", KC // 2, KC)
    ffn(0)
    add("ev_in", EV_IN, EV_IN)
    add("ev_out", KC, KC)
    cross(0)
    ffn(1)
    ffn(2)
    add("od_in", OD_IN, OD_IN)
    add("uq", 2, C_HEADS)
    add("ukv", 1, 4)
    add("od_out", KC, KC)
    cross(1)
    ffn(3)
    return units, chunks, u


def attention_jobs():
    even = []
    for f in range(A_HEADS // 2):
        for i in range(NT):
            even += [("cmp", f, i), ("slc", f, i), ("win", f, i), ("slc", f + 4, i), ("win", f + 4, i)]
    even += [("dsa", h, i) for h in range(B_HEADS) for i in range(NT)]
    diff = [(f"diff{e}", h, i) for h in range(D_HEADS) for i in range(NT) for e in range(2)]
    mla = [("mla", h, i) for h in range(C_HEADS) for i in range(NT)]
    cross = [("x", h, i) for h in range(X_HEADS) for i in range(NT)]
    return [even, cross, diff, mla, cross]


def build(nc, a):
    UNIT, CHUNK, N_UNITS = plan()
    JOBS = attention_jobs()
    JOB0 = [sum(len(j) for j in JOBS[:n]) for n in range(len(JOBS))]

    base = -(-nc.sbuf_base // 32) * 32

    class Region:
        def __init__(self, at):
            self.at = at

        def put(self, name, shape, dt):
            size = int(np.prod(shape[1:])) * (2 if dt == BF16 else 4)
            t = nc.alloc_sbuf_tensor_at(name, shape, dt, offset=self.at)
            self.at += -(-size // 32) * 32
            assert self.at <= nc.sbuf_usable_end, (name, self.at)
            return t

    keep = Region(base)
    x = keep.put("x_res", [P, KC, T], F32)
    raw = [keep.put(f"w_raw{j}", [P, KC * P], F32) for j in range(R)]
    w_hi = [keep.put(f"w_hi{j}", [P, KC * P], F32R) for j in range(R)]
    w_lo = [keep.put(f"w_lo{j}", [P, KC * P], F32R) for j in range(R)]
    at_h = keep.at
    h_hi = keep.put("h_hi", [P, KC, T], F32R)
    h_lo = keep.put("h_lo", [P, KC, T], F32R)
    y_ffn = Region(at_h).put("y_ffn", [P, KC, T], F32)
    r_sb = keep.put("r_tok", [P, T], F32)
    sq = [keep.put(f"sq{j}", [P, T], F32) for j in range(2)]
    sq_sum = keep.put("sq_sum", [P, T], F32)
    step = [keep.put(f"step{j}", [P, T], F32) for j in range(2)]
    gains = keep.put("gains", [P, G_END], F32)
    ident = keep.put("ident", [P, P], F32)
    ident_bf = keep.put("ident_bf", [P, P], BF16)
    columns = keep.put("columns", [P, 3], F32)
    ones, zero = columns[:, 0:1], columns[:, 1:2]
    row_ok = columns[:, 2:3]
    rs = keep.put("rsqrt_tmp", [P, 4, 16], F32)
    lam = keep.put("lam", [P, 8], F32)
    neg_max = keep.put("neg_max", [P, 8, 2], F32)
    row_sum = keep.put("row_sum", [P, 8, 2], F32)
    coef = keep.put("coef", [P, 8, 2], F32)
    at_var = keep.at

    m = Region(at_var)
    act_hi = m.put("act_hi", [P, FC, T], F32R)
    act_lo = m.put("act_lo", [P, FC, T], F32R)
    gate = [m.put(f"gate{j}", [P, T], F32) for j in range(2)]
    up = [m.put(f"up{j}", [P, T], F32) for j in range(2)]

    def attention_buffers(m, tag):
        return ([m.put(f"{tag}_logit{j}", [P, T], F32) for j in range(N_LOGIT)],
                [m.put(f"{tag}_prob{j}", [P, T], F32) for j in range(N_PROB)],
                [m.put(f"{tag}_probT{j}", [P, T], F32) for j in range(N_PROBT)])

    m = Region(at_var)
    ev = m.put("ev_proj", [P, EV_IN, T], F32)
    ev_v = m.put("ev_v_rows", [P, 3, NT, P], F32)
    gates = m.put("gates", [P, NT, 3 * A_HEADS], F32)
    kc = m.put("k_cmp", [P, 2 * GC], F32)
    vc = m.put("v_cmp", [P, P], F32)
    cmp_prob = m.put("cmp_prob", [P, 2, NT, 2 * GC], F32)
    at = m.at
    ev_bufs = attention_buffers(m, "ev")
    n = Region(at)
    cmp_w = n.put("cmp_w", [P, 2, CMP_LEN // 2, DH], F32)
    cmp_x = n.put("cmp_x", [P, 2, CMP_LEN // 2, 2, N_CMP], F32)
    vcT = n.put("v_cmpT", [DH, 2, N_CMP], F32)
    ev_causal = n.put("ev_causal", [P, T], F32)
    taken_mask = m.put("sel_mask", [P, NT - 1, T], BF16)
    ev_strip = [m.put(f"ev_strip{j}", [P, T], F32) for j in range(4)]
    cmp_pe = m.put("cmp_pe", [P, 2, CMP_LEN], F32)
    top8 = m.put("top8", [P, NT - 1, 8], F32)
    at = m.at
    n = Region(at + 6144)
    relu = [n.put(f"relu{j}", [P, T], F32) for j in range(2)]
    score = [n.put(f"score{j}", [P, T], F32) for j in range(3)]
    ev_y = Region(at).put("ev_y", [P, KC, T], F32)
    k_st = [[Region(at + 4096 * n + 2048 * p).put(f"k_st{n}_{p}", [P, T], F32R) for p in range(2)] for n in range(4)]
    k_st.append([Region(at_var + 2048 * c).put(f"k_st4_{c}", [P, T], F32R) for c in (KCMP, VCMP)])
    q_st = [Region(at_var + 2048 * j).put(f"q_st{j}", [P, T], F32R) for j in range(4)]

    m = Region(at_var)
    at_od = m.at
    od = m.put("od_proj", [P, OD_IN, T], F32)
    dv = m.put("diff_v", [P, D_HEADS, NT, P], F32)
    od_bufs = attention_buffers(m, "od")
    cq_hi = m.put("cq_hi", [P, 2, T], F32R)
    cq_lo = m.put("cq_lo", [P, 2, T], F32R)
    ckv_hi = m.put("ckv_hi", [P, T], F32R)
    ckv_lo = m.put("ckv_lo", [P, T], F32R)
    at = m.at
    od_strip = [m.put(f"od_strip{j}", [P, T], F32) for j in range(3)]
    n = Region(at)
    od_causal = n.put("od_causal", [P, T], F32)
    rope_t = n.put("rope_table", [P, 2, T], F32)
    rope_x = od_bufs[1][0:4]
    at = m.at
    diff_o = m.put("diff_o", [P, D_HEADS, T], F32)
    diff_sq = m.put("diff_sq", [P, D_HEADS, T], F32)
    od_y = Region(at).put("od_y", [P, KC, T], F32)
    n = Region(at_od)
    mla_v = n.put("mla_v", [P, NT, T], F32)
    mla_q = n.put("mla_q", [P, C_HEADS, T], F32)
    mla_k = n.put("mla_k", [P, C_HEADS, T], F32)

    m = Region(at_var)
    mem_sb = m.put("mem_sb", [P, KC, MEM], F32)
    mem_hi = m.put("mem_hi", [P, KC, MEM], F32R)
    mem_lo = m.put("mem_lo", [P, KC, MEM], F32R)
    r_mem = m.put("r_mem", [P, MEM], F32)
    mem_sq = [m.put(f"mem_sq{j}", [P, MEM], F32) for j in range(2)]
    mem_sum = m.put("mem_sum", [P, MEM], F32)
    xq = m.put("x_q", [P, X_HEADS, T], F32)
    xkv = m.put("x_kv", [P, 2 * X_HEADS, MEM], F32)
    xv = m.put("x_v", [P, X_HEADS, MT, P], F32)
    x_bufs = attention_buffers(m, "x")
    x_y = m.put("x_y", [P, KC, T], F32)

    m = Region(at_var)
    onehot = m.put("onehot", [BUCKETS + 1, LINE + 1], F32)
    table = m.put("table", [BUCKETS + 1, BIAS_HEADS], F32)
    lines = m.put("lines", [BIAS_HEADS, LINE + 1], F32)
    lam_in = m.put("lam_in", [P, 4, DH], F32)
    lam_pr = m.put("lam_pr", [P, 2, DH], F32)
    lines_dram = nc.dram_tensor("bias_lines", [BIAS_HEADS, LINE + 1], F32, kind="Internal").ap()
    line_rows = nc.dram_tensor("bias_line_rows", [BIAS_HEADS, P, LINE + 1], F32, kind="Internal").ap()

    bank = [nc.alloc_psum_tensor(f"bank{b}", [P, 512], F32) for b in range(8)]
    B_STAT, B_RT = 4, 5
    B_T, B_O = (6, 7), (3, 4)
    B_S = [(0, 1, 2) if n == 3 else (0, 1, 2, 5) for n in range(5)]

    sems = {}

    def sem(name):
        sems.setdefault(name, nc.alloc_semaphore(name))
        return sems[name]

    raw_loaded = [sem(f"raw_loaded{j}") for j in range(R)]
    slot_taken = sem("slot_taken")
    hi_split = sem("hi_split")
    split_done = sem("split_done")
    unit_done = sem("unit_done")
    chunk_out = sem("chunk_out")
    silu_done = sem("silu_done")
    prod_done = sem("prod_done")
    act_hi_done = sem("act_hi_done")
    act_done = sem("act_done")
    sq_done = sem("sq_done")
    sq_added = sem("sq_added")
    pre_added = sem("pre_added")
    stat_done = sem("stat_done")
    rsqrt_done = sem("rsqrt_done")
    r_turned = sem("r_turned")
    r_copied = sem("r_copied")
    x_done = sem("x_done")
    hi_done = sem("hi_done")
    lo_done = sem("lo_done")
    dve_done = sem("dve_done")
    turned = sem("turned")
    rows_done = sem("rows_done")
    mask_done = sem("mask_done")
    krope_done = sem("krope_done")
    k_hi_done = sem("k_hi_done")
    k_lo_pool = sem("k_lo_pool")
    k_lo_done = sem("k_lo_done")
    q_hi_done = sem("q_hi_done")
    q_lo_done = sem("q_lo_done")
    cmp_x_done = sem("cmp_x_done")
    qk_done = sem("qk_done")
    logit_done = sem("logit_done")
    exp_done = sem("exp_done")
    probT_done = sem("probT_done")
    probT_copied = sem("probT_copied")
    pv_done = sem("pv_done")
    coef_done = sem("coef_done")
    scaled = sem("scaled")
    idx_done = sem("idx_done")
    relu_done = sem("relu_done")
    idx_added = sem("idx_added")
    cmp_zero = sem("cmp_zero")
    cmp_done = sem("cmp_done")
    gate_exp = sem("gate_exp")
    lam_exp = sem("lam_exp")
    q_nope = sem("q_nope")
    mla_chunk = sem("mla_chunk")
    pool_rope = sem("pool_rope")
    rope_added = sem("rope_added")
    mla_ready = sem("mla_ready")
    diff_out = sem("diff_out")
    sub_sq = sem("sub_sq")
    sub_turned = sem("sub_turned")
    sub_normed = sem("sub_normed")
    sub_hi = sem("sub_hi")
    sub_lo = sem("sub_lo")
    const_in = sem("const_in")
    x_in = [sem(f"x_in{c}") for c in range(KC)]
    start_in = sem("start_in")
    lines_out = sem("lines_out")
    aux_in = sem("aux_in")
    out_done = sem("out_done")
    ones_set = sem("ones_set")

    AUX = {"ev": 48, "mem0": 64, "od": 96, "mem1": 112}

    SQ = {}
    n_sq = n_stat = n_rs = n_rt = n_cp = 0
    for kind, k in [("pre", 0), ("post", 1), ("pre", 1), ("mem", 0), ("post", 2), ("pre", 2), ("post", 3), ("pre", 3),
                    ("post", 4), ("pre", 4), ("post", 5), ("pre", 5), ("cq", 0), ("ckv", 0), ("sub", 0), ("mem", 1),
                    ("post", 6), ("pre", 6), ("post", 7), ("pre", 7), ("post", 8)]:
        SQ[kind, k] = dict(sq=n_sq, stat=n_stat, rs=n_rs, rt=n_rt, cp=n_cp)
        n_sq += {"cq": 2, "ckv": 1, "sub": 0}.get(kind, 8)
        n_stat += 1
        n_rs += 1
        n_rt += kind != "sub"
        n_cp += kind in ("pre", "mem")
    ADD = {("post", k): 6 * (k - 1) + 7 * (k >= 2) + 7 * (k >= 6) for k in range(1, 9)}
    ADD["mem", 0], ADD["mem", 1] = 6, 6 * 5 + 7

    X0 = {s: KC * max(s - 1, 0) for s in range(9)}
    SPLIT, n_split = {}, 0
    for name, k in [("pre0", 8), ("pre1", 8), ("ev_o", 8), ("mem0", 8), ("pre2", 8), ("xo0", 4), ("pre3", 8),
                    ("pre4", 8), ("pre5", 8), ("cq", 2), ("ckv", 1), ("od_o", 4), ("mem1", 8), ("pre6", 8),
                    ("xo1", 4), ("pre7", 8)]:
        SPLIT[name] = n_split
        n_split += k
    TURN, n_turn = {}, 1
    for name, k in [("vg", 1), ("ev_v", 2), ("xv0", 4), ("dv", 4), ("xv1", 4)]:
        TURN[name] = n_turn
        n_turn += k
    V_ROWS = {"vg": 2, "ev_v": 3, "xv0": 10, "dv": 14, "xv1": 18}

    ev_heads = [h for f in range(A_HEADS // 2) for h in (f, f + 4)] + list(range(A_HEADS, A_HEADS + B_HEADS))
    STRIPS = {0: (ev_heads, ev_strip, [sem(f"ev_strip_in{j}") for j in range(4)], 2),
              2: (list(range(A_HEADS + B_HEADS, BIAS_HEADS)), od_strip, [sem(f"od_strip_in{j}") for j in range(3)], 1)}
    EV_POS = {h: k for k, h in enumerate(ev_heads)}

    def kind_of(job):
        phase, (kind, h, i) = job
        w = P * (i + 1)
        q = slice(P * i, P * i + P)
        off = T - P - P * i
        e = DH * (h % 2)
        s = dict(blocks=i + 1, rows=P, w=w, mask=None, k_lo=None, scale=-DH ** -0.5,
                 out=(h // 2, slice(e, e + DH), q))
        s.update(opens=True, closes=True, turns=True)
        if kind == "cmp":
            n = 8 * i + 7
            bias = lambda k: ev_strip[k % 4][:, off + CMP_LEN - 1:off + CMP_LEN + CMP_STRIDE * (n - 1):CMP_STRIDE]
            s.update(w=2 * GC, blocks=1, rows=2 * GC, q=ev[:, QA + h, q], k=kc[:], v=[vc[0:2 * GC, :]],
                     out=(h, slice(0, P), q), closes=False, strip=2 * h + 1,
                     parts=[(GC * g, n, bias(2 * h + g), gates[:, i, 3 * (h + 4 * g):3 * (h + 4 * g) + 1]) for g in range(2)])
            return s
        if kind in ("slc", "win"):
            g, k = h // 4, EV_POS[h]
            b = ("slc", "win").index(kind)
            n = 2 * b + g
            s.update(q=q_st[k % 4][:, q], k=k_st[n][0][:, 0:w], k_lo=k_st[n][1][:, 0:w], strip=k,
                     v=[ev_v[:, b, j, DH * g:DH * g + DH] for j in range(i + 1)],
                     out=(h % 4, slice(DH * g, DH * g + DH), q), opens=False, closes=b > 0,
                     parts=[(0, w, ev_strip[k % 4][:, off:off + w], gates[:, i, 3 * h + b + 1:3 * h + b + 2])])
        elif kind == "dsa":
            e = DH * (h % 2)
            g = A_HEADS + h
            s.update(q=q_st[g % 4][:, q], k=k_st[4][0][:, 0:w], k_lo=k_st[4][1][:, 0:w], strip=g,
                     v=[ev_v[:, 2, j, 0:DH] for j in range(i + 1)], parts=[(0, w, ev_strip[g % 4][:, off:off + w], None)],
                     out=(4 + h // 2, slice(e, e + DH), q), mask=taken_mask[:, i - 1, 0:w] if i else None)
        elif kind.startswith("diff"):
            e = int(kind[-1])
            s.update(q=od[64 * e:64 * e + DH, DQ + h, q], k=od[64 * e:64 * e + DH, DK + h, 0:w], strip=h,
                     v=[dv[:, h, j, :] for j in range(i + 1)], parts=[(0, w, od_strip[h % 3][:, off:off + w], None)],
                     out=(h, slice(0, P), q), turns=e > 0)
        elif kind == "mla":
            s.update(q=mla_q[0:DN + DR, h, q], k=mla_k[0:DN + DR, h, 0:w], scale=-(DN + DR) ** -0.5,
                     v=[mla_v[:, j, DH * h:DH * h + DH] for j in range(i + 1)],
                     parts=[(0, w, od_causal[:, off:off + w], None)], strip=None)
        else:
            s.update(q=xq[:, h, q], k=xkv[:, h, :], scale=-P ** -0.5, w=MEM, blocks=MT,
                     v=[xv[:, h, j, :] for j in range(MT)], parts=[(0, MEM, zero[:, 0:1].to_broadcast([P, MEM]), None)],
                     out=(h, slice(0, P), q), strip=None)
        return s

    MEM_SHARES = (range(0, 1), range(1, 3), range(3, 8))
    LAST_UNITS = {"down": 3 * KC, "ev_out": KC, "od_out": KC, "xo": KC // 2}
    OUT_KEY = ["ev_o", "xo0", None, "od_o", "xo1"]
    SUB_AT = 5
    BUFS = [ev_bufs, x_bufs, od_bufs, od_bufs, x_bufs]
    INFO = [[kind_of((p, job)) for job in jobs] for p, jobs in enumerate(JOBS)]

    n_turns = 0
    for infos in INFO:
        for n, info in enumerate(infos):
            info["turn"] = n_turns
            n_turns += info["turns"]
            after = infos[n + 1]["out"][0] if n + 1 < len(infos) else None
            info["ends"] = after != info["out"][0]

    def probs_of(phase, s):
        kind, f, i = JOBS[phase][s]
        return cmp_prob[:, f % 2, i, :] if kind == "cmp" else BUFS[phase][1][s % N_PROB]

    def strip_group(phase, s, size):
        return max(info["strip"] // size for info in INFO[phase][:s + 1])

    def first_of(phase, s, size):
        group = strip_group(phase, s, size)
        return group if s == 0 or strip_group(phase, s - 1, size) < group else None

    def q_chunk(g):
        return QA + g // 2 if g < A_HEADS else QB + (g - A_HEADS) // 2

    def up_ready(engine, unit, k):
        if k < 3:
            engine.wait_ge(mla_chunk, 3 * unit + k + 1)
        else:
            engine.wait_ge(unit_done, UNIT["uq"] + unit + 1)

    def k_rows(n):
        e = DH * (n % 2)
        return ev[e:e + DH, (KS, KW)[n // 2], :]

    def q_head(g):
        chunk, e = q_chunk(g), DH * (g % 2)
        other = DH - e
        return ev[e:e + DH, chunk, :], q_st[g % 4][e:e + DH, :], q_st[g % 4][other:other + DH, :]

    with nc.Block() as block:

        @block.sync
        def _(sp):
            sp.dma_start(ident[:], a["consts"][:, C_ID:C_ID + P]).then_inc(const_in, 16)
            sp.dma_start(gains[:], a["gains"]).then_inc(const_in, 16)
            sp.dma_start(row_ok[:], a["row_ok"]).then_inc(const_in, 16)
            def load(j, src, cols):
                sp.dma_start(raw[j][:, 0:cols], src).then_inc(raw_loaded[j], 16)

            def load_x(c):
                sp.dma_start(x[:, c, :], a["x"][:, c, :]).then_inc(x_in[c], 16)

            def stream(u0, n, source, first=0, cols=KC * P):
                for k in range(first, n):
                    if (n - k) % R == 0:
                        break
                    if u0 + k >= R:
                        sp.wait_ge(split_done, u0 + k - R + 1)
                    load((u0 + k) % R, source(k), cols)
                else:
                    return
                loops = (n - k) // R
                with sp.Fori(0, loops) as i:
                    for b in range(R):
                        sp.wait_ge(split_done, R * i + u0 + k + b - R + 1)
                        load((u0 + k + b) % R, source(R * i + k + b), cols)

            def ffn(f):
                first = 0
                if f == 0:
                    for k in range(R):
                        load(k, a["w_up"][0, k], KC * P)
                        for c in range(4 * k, 4 * k + 4) if k < 2 else ():
                            load_x(c)
                    first = R
                stream(UNIT[f"up{f}"], 2 * FC, lambda k: a["w_up"][f, k], first)
                u0 = UNIT[f"down{f}"]
                with sp.Fori(0, KC // R) as i:
                    for b in range(3 * R):
                        n, part = b // 3, b % 3
                        at, t = P * sum(DOWN_TILES[:part]), P * DOWN_TILES[part]
                        sp.wait_ge(split_done, 3 * R * i + u0 + b - R + 1)
                        load((u0 + b) % R, a["w_down"][f, R * i + n][:, at:at + t], t)

            ffn(0)
            stream(UNIT["ev_in"], EV_IN, lambda k: a["w_ev_in"][k])
            stream(UNIT["ev_out"], KC, lambda k: a["w_ev_out"][k])
            for n in range(2):
                if n == 1:
                    ffn(1)
                    ffn(2)
                    stream(UNIT["od_in"], OD_IN, lambda k: a["w_od_in"][k])
                    stream(UNIT["uq"], 2, lambda k: a["w_uq"][k])
                    stream(UNIT["ukv"], 1, lambda k: a["w_ukv"][k])
                    stream(UNIT["od_out"], KC, lambda k: a["w_od_out"][k])
                stream(UNIT[f"xkv{n}"], 2 * X_HEADS, lambda k: a["w_xkv"][n, k])
                stream(UNIT[f"xq{n}"], X_HEADS, lambda k: a["w_xq"][n, k])
                stream(UNIT[f"xo{n}"], KC // 2, lambda k: a["w_xo"][n, k])
            ffn(3)
            for c in range(KC):
                sp.wait_ge(x_done, X0[8] + c + 1)
                sp.dma_start(a["out"][:, c, :], x[:, c, :]).then_inc(out_done, 16)
            sp.wait_ge(out_done, 16 * KC)
            sp.wait_ge(lines_out, 32)

        @block.gpsimd
        def _(pool):
            pool.memset(ones[:], 1.0).then_inc(ones_set, 1)
            pool.memset(zero[:], 0.0).then_inc(ones_set, 1)
            pool.memset(table[:], NEG).then_inc(ones_set, 1)

            def split(j, cols, u, loaded, free):
                pool.wait_ge(raw_loaded[j], loaded)
                if free is not None:
                    pool.wait_ge(unit_done, free)
                pool.sem_inc(slot_taken, 1)
                pool.tensor_scalar(w_hi[j][:, 0:cols], raw[j][:, 0:cols], 1.0, 0.0, ALU.mult, ALU.add).then_inc(hi_split, 1)
                pool.wait_ge(hi_split, u + 1)
                pool.tensor_tensor(w_lo[j][:, 0:cols], raw[j][:, 0:cols], w_hi[j][:, 0:cols].bitcast(F32),
                                   ALU.subtract).then_inc(split_done, 1)

            def straight(u, cols=KC * P):
                split(u % R, cols, u, 16 * (u // R + 1), u - R + 1 if u >= R else None)

            def units(u0, n, first=0):
                for k in range(first, n):
                    if (n - k) % R == 0:
                        break
                    straight(u0 + k)
                else:
                    return
                with pool.Fori(0, (n - k) // R) as i:
                    for b in range(R):
                        u = u0 + k + b
                        split(u % R, KC * P, R * i + u, 16 * i + 16 * (u // R + 1), R * i + u - R + 1)

            def pre_norm(s):
                for c in range(1, KC):
                    pool.wait_ge(sq_done, SQ["pre", s]["sq"] + c + 1)
                    if c > 1:
                        pool.wait_ge(pre_added, 7 * s + c - 1)
                    pool.tensor_tensor(sq_sum[:], sq_sum[:], sq[c % 2][:], ALU.add).then_inc(pre_added, 1)

            def projection(name, n, s):
                for k in range(R):
                    straight(UNIT[name] + k)
                if s:
                    pre_norm(s)
                units(UNIT[name], n, R)

            def ffn(s, f):
                projection(f"up{f}", 2 * FC, s)
                u0 = UNIT[f"down{f}"]
                with pool.Fori(0, KC // R) as i:
                    for b in range(3 * R):
                        u = u0 + b
                        split(u % R, P * DOWN_TILES[b % 3], 3 * R * i + u, 48 * i + 16 * (u // R + 1), 3 * R * i + u - R + 1)

            def q_parts():
                pool.wait_ge(relu_done, (NT - 1) * IDX_HEADS)
                pool.wait_ge(rows_done, V_ROWS["vg"] + 1)
                for k in range(A_HEADS + B_HEADS):
                    src, hi, lo = q_head(k)
                    if k >= 4:
                        last = max(n for n, info in enumerate(INFO[0]) if info["strip"] == k - 4 and info["k_lo"] is not None)
                        pool.wait_ge(qk_done, last + 1)
                    pool.wait_ge(chunk_out, CHUNK["ev_in"] + q_chunk(k) + 1)
                    pool.tensor_scalar(hi, src, 1.0, 0.0, ALU.mult, ALU.add).then_inc(q_hi_done, 1)
                    pool.wait_ge(q_hi_done, k + 1)
                    pool.tensor_tensor(lo, src, hi.bitcast(F32), ALU.subtract).then_inc(q_lo_done, 1)
                    pool.wait_ge(q_lo_done, k + 1)

            def cmp_tokens():
                pool.wait_ge(chunk_out, CHUNK["ev_in"] + VCMP + 1)
                pool.wait_ge(aux_in, AUX["ev"])
                n = 0
                for kv, src in enumerate((KCMP, VCMP)):
                    for g in range(2):
                        e = slice(DH * g, DH * g + DH)
                        proj = ev[e, src, :]
                        for odd in range(2):
                            blocks = bass.AP(proj.tensor, proj.offset + odd,
                                             [list(proj.ap[0]), [2, CMP_LEN // 2], [CMP_STRIDE, N_CMP]])
                            pe_ = cmp_pe[e, kv, odd:CMP_LEN:2].unsqueeze(2).to_broadcast([DH, CMP_LEN // 2, N_CMP])
                            pool.tensor_tensor(cmp_x[DH * odd:DH * odd + DH, kv, :, g, :], blocks, pe_,
                                               ALU.add).then_inc(cmp_x_done, 1)
                            n += 1
                            pool.wait_ge(cmp_x_done, n)

            def k_low():
                pool.wait_ge(k_hi_done, 2)
                for half in range(2):
                    pool.tensor_tensor(k_st[0][1][DH * half:DH * half + DH, :], k_rows(0), k_st[0][0][0:DH, :].bitcast(F32),
                                       ALU.subtract).then_inc(k_lo_pool, 1)
                    pool.wait_ge(k_lo_pool, half + 1)

            ffn(0, 0)
            projection("ev_in", EV_IN, 1)
            cmp_tokens()
            k_low()
            q_parts()
            units(UNIT["ev_out"], KC)
            for n in range(2):
                if n == 1:
                    ffn(3, 1)
                    ffn(4, 2)
                    projection("od_in", OD_IN, 5)
                    units(UNIT["uq"], 2)
                    units(UNIT["ukv"], 1)
                    pool.wait_ge(split_done, UNIT["ukv"] + 1)
                    pool.wait_ge(chunk_out, CHUNK["uq"] + 2)
                    for k in range(4):
                        rows = slice(DR * k, DR * k + DR)
                        pool.tensor_tensor(mla_q[DN:DN + DR, k, :], rope_x[0][rows, :], rope_x[1][rows, :],
                                           ALU.add).then_inc(pool_rope, 1)
                        pool.wait_ge(pool_rope, k + 1)
                    units(UNIT["od_out"], KC)
                units(UNIT[f"xkv{n}"], 2 * X_HEADS)
                projection(f"xq{n}", X_HEADS, 2 + 4 * n)
                units(UNIT[f"xo{n}"], KC // 2)
            ffn(7, 3)

        @block.tensor
        def _(pe):
            def product(b, j, tile, hi, lo, first, last, n=T):
                w = slice(P * tile, P * tile + P)
                pe.matmul(bank[b][:, 0:n], w_hi[j][:, w], hi, start=first, stop=False)
                pe.matmul(bank[b][:, 0:n], w_hi[j][:, w], lo, start=False, stop=False)
                return pe.matmul(bank[b][:, 0:n], w_lo[j][:, w], hi, start=False, stop=last)

            def chunk_of_unit(u, c, j, b, hi, lo, n=T):
                pe.wait_ge(split_done, u + 1)
                pe.wait_ge(chunk_out, c - R + 1)
                for k in range(KC):
                    mm = product(b, j, k, hi[:, k, 0:n], lo[:, k, 0:n], k == 0, k == KC - 1, n)
                mm.then_inc(unit_done, 1)

            def chunks(name, n, first, hi, lo, cols=T):
                u0, c0 = UNIT[name], CHUNK[name]
                for k in range(first, n):
                    if (n - k) % R == 0:
                        break
                    chunk_of_unit(u0 + k, c0 + k, (u0 + k) % R, (c0 + k) % R, hi, lo, cols)
                else:
                    return
                with pe.Fori(0, (n - k) // R) as i:
                    for b in range(R):
                        chunk_of_unit(R * i + u0 + k + b, R * i + c0 + k + b, (u0 + k + b) % R, (c0 + k + b) % R,
                                      hi, lo, cols)

            def sums(src, tiles, first, last):
                for i in range(tiles):
                    mm = pe.matmul(bank[B_STAT][:, i:i + 1], src[:, P * i:P * i + P], ones[:],
                                   start=first and i == 0, stop=last, skip_group_check=True)
                return mm

            def turn_r(key, tiles):
                pe.wait_ge(rsqrt_done, SQ[key]["rs"] + 1)
                for i in range(tiles):
                    mm = pe.transpose(bank[B_RT][:, P * i:P * i + P], rs[:, 3, i:i + 1].to_broadcast([P, P]), ident[:])
                mm.then_inc(r_turned, 1)

            def post_norm(s, fill=None):
                key = ("post", s)
                if fill:
                    fill(0)
                pe.wait_ge(sq_added, ADD[key] + 6)
                sums(sq_sum, NT, True, False)
                pe.wait_ge(sq_done, SQ[key]["sq"] + KC)
                sums(sq[1], NT, False, True).then_inc(stat_done, 1)
                if fill:
                    fill(1)
                turn_r(key, NT)

            def pre_norm(s, name):
                key, u0, c0 = ("pre", s), UNIT[name], CHUNK[name]
                pe.wait_ge(split_done, u0 + R)
                if c0:
                    pe.wait_ge(chunk_out, c0)
                for c in range(KC - 2):
                    pe.wait_ge(lo_done, SPLIT[f"pre{s}"] + c + 1)
                    for k in range(R):
                        product((c0 + k) % R, (u0 + k) % R, c, h_hi[:, c, :], h_lo[:, c, :], c == 0, False)
                pe.wait_ge(pre_added, 7 * (s + 1))
                sums(sq_sum, NT, True, True).then_inc(stat_done, 1)
                pe.wait_ge(lo_done, SPLIT[f"pre{s}"] + KC)
                for k in range(R):
                    for c in range(KC - 2, KC):
                        mm = product((c0 + k) % R, (u0 + k) % R, c, h_hi[:, c, :], h_lo[:, c, :], False, c == KC - 1)
                    mm.then_inc(unit_done, 1)
                    if k == 2:
                        turn_r(key, NT)

            def pre_norm_by_halves(s, name):
                key, u0, c0 = ("pre", s), UNIT[name], CHUNK[name]
                for half in range(2):
                    for k in range(R):
                        if half == 0:
                            pe.wait_ge(split_done, u0 + k + 1)
                            pe.wait_ge(chunk_out, c0 + k - R + 1)
                        for c in range(4 * half, 4 * half + 4):
                            pe.wait_ge(lo_done, SPLIT[f"pre{s}"] + c + 1)
                            mm = product((c0 + k) % R, (u0 + k) % R, c, h_hi[:, c, :], h_lo[:, c, :], c == 0, c == KC - 1)
                        if half:
                            mm.then_inc(unit_done, 1)
                            if k == 1:
                                pe.wait_ge(pre_added, 7 * (s + 1))
                                sums(sq_sum, NT, True, True).then_inc(stat_done, 1)
                            if k == 2:
                                turn_r(key, NT)

            def first_pre_norm():
                pe.wait_ge(split_done, 1)
                for c in range(KC):
                    pe.wait_ge(lo_done, c + 1)
                    mm = product(0, 0, c, h_hi[:, c, :], h_lo[:, c, :], c == 0, c == KC - 1)
                mm.then_inc(unit_done, 1)
                for k in range(1, R):
                    if k == 2:
                        pe.wait_ge(pre_added, 7)
                        sums(sq_sum, NT, True, True).then_inc(stat_done, 1)
                    pe.wait_ge(split_done, k + 1)
                    for c in range(KC):
                        mm = product(k, k, c, h_hi[:, c, :], h_lo[:, c, :], c == 0, c == KC - 1)
                    mm.then_inc(unit_done, 1)
                    if k == 2:
                        pe.wait_ge(const_in, 48)
                        turn_r(("pre", 0), NT)

            def ffn(s, f):
                if s:
                    pre_norm(s, f"up{f}")
                else:
                    first_pre_norm()
                chunks(f"up{f}", 2 * FC, R, h_hi, h_lo)
                u0, c0 = UNIT[f"down{f}"], CHUNK[f"down{f}"]
                with pe.Fori(0, KC // R) as i:
                    for b in range(3 * R):
                        n, part, j = b // 3, b % 3, (u0 + b) % R
                        k0, tiles = sum(DOWN_TILES[:part]), DOWN_TILES[part]
                        pe.wait_ge(split_done, 3 * R * i + u0 + b + 1)
                        if part == 0:
                            pe.wait_ge(chunk_out, R * i + c0 + n - R + 1)
                        pe.wait_ge(act_done, FC * f + k0 + tiles)
                        for k in range(tiles):
                            mm = product((c0 + n) % R, j, k, act_hi[:, k0 + k, :], act_lo[:, k0 + k, :],
                                         k0 + k == 0, k0 + k == FC - 1)
                        mm.then_inc(unit_done, 1)
                post_norm(s + 1)

            def turn_rows(key, k, src, tiles):
                n = TURN[key] + k
                for i in range(tiles):
                    mm = pe.transpose(bank[B_T[n % 2]][:, P * i:P * i + P], src[:, P * i:P * i + P], ident[:])
                mm.then_inc(turned, 1)

            def attention(phase, hooks={}):
                infos, j0 = INFO[phase], JOB0[phase]
                probTs = BUFS[phase][2]
                n = len(infos)

                def logit(s):
                    j, info = j0 + s, infos[s]
                    banks = B_S[phase]
                    if s >= len(banks):
                        pe.wait_ge(logit_done, j - len(banks) + 1)
                    if info["mask"] is not None and JOBS[phase][s][1] == 0:
                        pe.wait_ge(mask_done, JOBS[phase][s][2])
                    if phase == 2 and s == 3:
                        pe.wait_ge(lo_done, SPLIT["ckv"] + 1)
                    out = bank[banks[s % len(banks)]][:, 0:info["w"]]
                    if phase == 0 and JOBS[0][s][2] == 0 and JOBS[0][s][0] in ("slc", "dsa"):
                        pe.wait_ge(q_lo_done, info["strip"] + 1)
                    if phase == 0 and s in (2, 3, 4):
                        pe.wait_ge(k_lo_done, 2 * (s - 1))
                    if phase == 0 and JOBS[0][s] == ("dsa", 0, 0):
                        pe.wait_ge(k_lo_done, 7)
                    more = info["mask"] is not None
                    if info["k_lo"] is not None:
                        pe.matmul(out, info["q"], info["k"], start=True, stop=False)
                        mm = pe.matmul(out, info["q"], info["k_lo"], start=False, stop=not more)
                    else:
                        mm = pe.matmul(out, info["q"], info["k"], start=True, stop=not more)
                    if info["mask"] is not None:
                        mm = pe.matmul(out, ident_bf[:], info["mask"], start=False, stop=True)
                    mm.then_inc(qk_done, 1)

                def turn(s):
                    j, info = j0 + s, infos[s]
                    if not info["turns"]:
                        return
                    t, prob = info["turn"], probs_of(phase, s)
                    pe.wait_ge(scaled, j + 1)
                    if t >= infos[0]["turn"] + 2:
                        pe.wait_ge(probT_copied, t - 1)
                    for b in range(info["blocks"]):
                        mm = pe.transpose(bank[B_T[t % 2]][0:info["rows"], P * b:P * b + P],
                                          prob[:, P * b:P * b + info["rows"]], ident[:])
                    mm.then_inc(probT_done, 1)

                def output(s):
                    info = infos[s]
                    if not info["turns"]:
                        return
                    t = info["turn"]
                    chunk, features, tokens = info["out"]
                    pe.wait_ge(probT_copied, t + 1)
                    if chunk >= 2 and info["opens"] and tokens.start == 0 and features.start == 0:
                        if phase == 2:
                            pe.wait_ge(sub_sq, chunk - 1)
                        else:
                            pe.wait_ge(lo_done, SPLIT[OUT_KEY[phase]] + chunk - 1)
                    for b, v in enumerate(info["v"]):
                        mm = pe.matmul(bank[B_O[chunk % 2]][features, tokens], v,
                                       probTs[t % N_PROBT][0:info["rows"], P * b:P * b + P],
                                       start=info["opens"] and b == 0, stop=info["closes"] and b == info["blocks"] - 1,
                                       skip_group_check=phase == 0)
                    mm.then_inc(pv_done, 1)

                for s in range(n + OUT_AT):
                    if s < n:
                        logit(s)
                    if TURN_AT <= s < n + TURN_AT:
                        turn(s - TURN_AT)
                    if s >= OUT_AT:
                        output(s - OUT_AT)
                    if s in hooks:
                        hooks[s]()

            def out_projection(name, s, mem):
                u0, c0 = UNIT[name], CHUNK[name]
                for k in range(KC):
                    if k == R:
                        key = ("mem", mem)
                        pe.wait_ge(sq_added, ADD[key] + 7)
                        sums(mem_sum, MT, True, True).then_inc(stat_done, 1)
                    if k == R + 1:
                        turn_r(("mem", mem), MT)
                    chunk_of_unit(u0 + k, c0 + k, (u0 + k) % R, (c0 + k) % R, h_hi, h_lo)

                def fill(share):
                    if share == 0:
                        pe.wait_ge(lo_done, SPLIT[f"mem{mem}"] + KC)
                    for k in MEM_SHARES[share]:
                        u, c = UNIT[f"xkv{mem}"] + k, CHUNK[f"xkv{mem}"] + k
                        chunk_of_unit(u, c, u % R, c % R, mem_hi, mem_lo, MEM)

                post_norm(s + 1, fill)
                fill(2)

            def even_mixer(s):
                pre_norm(s, "ev_in")
                c0 = CHUNK["ev_in"]
                pe.wait_ge(chunk_out, c0 + 4)
                turn_rows("vg", 0, ev[:, VG, :], NT)
                banks = (B_STAT, B_RT, B_T[(TURN["vg"] + 1) % 2])
                for k in range((NT - 1) * IDX_HEADS):
                    i, h = 1 + k // IDX_HEADS, k % IDX_HEADS
                    e = IDX_DH * (h % 4)
                    if k >= 3:
                        pe.wait_ge(relu_done, k - 2)
                    pe.matmul(bank[banks[k % 3]][:, 0:P * (i + 1)], ev[e:e + IDX_DH, IQ + h // 4, P * i:P * i + P],
                              ev[e:e + IDX_DH, IK, 0:P * (i + 1)], start=True, stop=True).then_inc(idx_done, 1)
                chunks("ev_in", EV_IN - 2, R, h_hi, h_lo)
                pe.wait_ge(relu_done, (NT - 1) * IDX_HEADS)
                pe.wait_ge(rows_done, V_ROWS["vg"] + 1)
                for k, src in enumerate((VS, VW)):
                    pe.wait_ge(chunk_out, c0 + src + 1)
                    turn_rows("ev_v", k, ev[:, src, :], NT)
                pe.wait_ge(aux_in, AUX["ev"])
                for kv in range(2):
                    pe.wait_ge(cmp_x_done, 4 * kv + 4)
                    for l in range(CMP_LEN // 2):
                        mm = pe.matmul(bank[4 + kv][0:DH, 0:2 * N_CMP], cmp_w[:, kv, l, :], cmp_x[:, kv, l, :, :],
                                       start=l == 0, stop=l == CMP_LEN // 2 - 1)
                    mm.then_inc(cmp_done, 1)
                pe.wait_ge(rows_done, V_ROWS["ev_v"] + 5)
                for g in range(2):
                    mm = pe.transpose(bank[4][0:N_CMP, P + DH * g:P + DH * g + DH], vcT[:, g, :], ident[0:DH, 0:DH])
                mm.then_inc(cmp_done, 1)
                chunks("ev_in", EV_IN, EV_IN - 2, h_hi, h_lo)
                pe.wait_ge(chunk_out, c0 + EV_IN)
                pe.wait_ge(rows_done, V_ROWS["ev_v"] + 2 + 5)
                pe.wait_ge(k_lo_pool, 2)
                attention(0)
                pe.wait_ge(lo_done, SPLIT["ev_o"] + KC)
                out_projection("ev_out", s, 0)

            def cross(s, n):
                pre_norm_by_halves(s, f"xq{n}")
                for h in range(X_HEADS):
                    if h >= 2:
                        pe.wait_ge(rows_done, V_ROWS[f"xv{n}"] + h - 1)
                    pe.wait_ge(chunk_out, CHUNK[f"xkv{n}"] + X_HEADS + h + 1)
                    turn_rows(f"xv{n}", h, xkv[:, X_HEADS + h, :], MT)
                pe.wait_ge(rows_done, V_ROWS[f"xv{n}"] + X_HEADS)
                pe.wait_ge(chunk_out, CHUNK[f"xq{n}"] + X_HEADS)
                attention(1 if n == 0 else 4)
                u0, c0 = UNIT[f"xo{n}"], CHUNK[f"xo{n}"]
                pe.wait_ge(lo_done, SPLIT[f"xo{n}"] + X_HEADS)
                for c in range(KC):
                    if c % 2 == 0:
                        pe.wait_ge(split_done, u0 + c // 2 + 1)
                    pe.wait_ge(chunk_out, c0 + c - R + 1)
                    for k in range(X_HEADS):
                        mm = product((c0 + c) % R, (u0 + c // 2) % R, X_HEADS * (c % 2) + k, h_hi[:, k, :],
                                     h_lo[:, k, :], k == 0, k == X_HEADS - 1)
                    if c % 2:
                        mm.then_inc(unit_done, 1)
                post_norm(s + 1)

            def odd_mixer(s):
                pre_norm(s, "od_in")
                c0 = CHUNK["od_in"]
                chunks("od_in", 8, R, h_hi, h_lo)
                pe.wait_ge(sq_done, SQ["cq", 0]["sq"] + 2)
                sums(sq[0], NT, True, False)
                sums(sq[1], NT, False, True).then_inc(stat_done, 1)
                chunks("od_in", 12, 8, h_hi, h_lo)
                turn_r(("cq", 0), NT)
                pe.wait_ge(sq_done, SQ["ckv", 0]["sq"] + 1)
                sums(sq[0], NT, True, True).then_inc(stat_done, 1)
                chunks("od_in", OD_IN, 12, h_hi, h_lo)
                pe.wait_ge(mla_ready, 2)
                turn_r(("ckv", 0), NT)
                for h in range(D_HEADS):
                    if h >= 2:
                        pe.wait_ge(rows_done, V_ROWS["dv"] + h - 1)
                    pe.wait_ge(chunk_out, c0 + DVT + h + 1)
                    turn_rows("dv", h, od[:, DVT + h, :], NT)
                pe.wait_ge(rows_done, V_ROWS["dv"] + D_HEADS)
                attention(2)
                pe.wait_ge(sub_sq, D_HEADS)
                for h in range(D_HEADS):
                    for i in range(NT):
                        n = NT * h + i
                        mm = pe.matmul(bank[B_STAT][:, n:n + 1], diff_sq[:, h, P * i:P * i + P], ones[:],
                                       start=n == 0, stop=n == NT * D_HEADS - 1, skip_group_check=True)
                mm.then_inc(stat_done, 1)
                uq, ukv, c0 = UNIT["uq"], UNIT["ukv"], CHUNK["uq"]
                jv = ukv % R
                pe.wait_ge(lo_done, SPLIT["ckv"] + 1)

                def up_queries(unit):
                    pe.wait_ge(split_done, uq + unit + 1)
                    for m_ in range(4):
                        for k in range(2):
                            mm = product((c0 + m_) % R, (uq + unit) % R, 2 * m_ + k, cq_hi[:, k, :], cq_lo[:, k, :],
                                         k == 0, k == 1)
                        mm.then_inc(*((mla_chunk, 1) if m_ < 3 else (unit_done, 1)))

                up_queries(0)
                pe.wait_ge(split_done, ukv + 1)
                pe.wait_ge(rsqrt_done, SQ["sub", 0]["rs"] + 1)
                for i in range(NT):
                    tok = slice(P * i, P * i + P)
                    out = bank[4 + i][:]
                    pe.matmul(out, ckv_hi[:, tok], w_hi[jv][:, T:2 * T], start=True, stop=False)
                    pe.matmul(out, ckv_hi[:, tok], w_lo[jv][:, T:2 * T], start=False, stop=False)
                    pe.matmul(out, ckv_lo[:, tok], w_hi[jv][:, T:2 * T], start=False, stop=True)
                pe.wait_ge(chunk_out, c0 + 4)
                up_queries(1)
                pe.wait_ge(q_nope, 4)
                pe.wait_ge(chunk_out, c0 + 8)
                for m_ in range(4):
                    mm = product((c0 + m_) % R, jv, m_, ckv_hi[:], ckv_lo[:], True, True)
                    mm.then_inc(*((mla_chunk, 1) if m_ < 3 else (unit_done, 1)))
                pe.wait_ge(chunk_out, c0 + 12)
                pe.wait_ge(q_nope, 4 + 4 + NT)
                pe.wait_ge(mla_ready, 4)
                pe.wait_ge(pool_rope, 4)
                pe.wait_ge(rope_added, 4)

                def turn_sub(h):
                    if h:
                        pe.wait_ge(sub_normed, h)
                    for i in range(NT):
                        r = rs[:, 3, NT * h + i:NT * h + i + 1].to_broadcast([P, P])
                        mm = pe.transpose(bank[B_RT][:, P * i:P * i + P], r, ident[:])
                    mm.then_inc(sub_turned, 1)

                attention(3, {SUB_AT * (h + 1): lambda h=h: turn_sub(h) for h in range(D_HEADS)})
                pe.wait_ge(lo_done, SPLIT["od_o"] + 4)
                pe.wait_ge(sub_lo, D_HEADS)
                out_projection("od_out", s, 1)

            pe.wait_ge(start_in, 16 * 3)
            pe.wait_ge(ones_set, 3)
            pe.matmul(bank[6][0:BIAS_HEADS, 0:512], table[:], onehot[:, 0:512], start=True, stop=True)
            pe.matmul(bank[7][0:BIAS_HEADS, 0:LINE + 1 - 512], table[:], onehot[:, 512:LINE + 1], start=True,
                      stop=True).then_inc(turned, 1)
            ffn(0, 0)
            even_mixer(1)
            cross(2, 0)
            ffn(3, 1)
            ffn(4, 2)
            odd_mixer(5)
            cross(6, 1)
            ffn(7, 3)

        @block.scalar
        def _(act):
            def pre_norm_parts(s):
                def square(c):
                    if c >= 3:
                        act.wait_ge(pre_added, 7 * s + c - 2)
                    act.activation((sq_sum if c == 0 else sq[c % 2])[:], x[:, c, :], ACT.Square).then_inc(sq_done, 1)

                late = s in (2, 6)
                for c in range(KC):
                    if s:
                        act.wait_ge(x_done, X0[s] + c + 1)
                    else:
                        act.wait_ge(x_in[c], 16)
                    g = G_PRE + KC * s + c
                    act.activation(h_hi[:, c, :], x[:, c, :], ACT.Copy, scale=gains[:, g:g + 1]).then_inc(hi_done, 1)
                    if not late:
                        square(c)
                for c in range(KC if late else 0):
                    square(c)

            def pre_norm_r(s):
                act.wait_ge(r_turned, SQ["pre", s]["rt"] + 1)
                act.activation(r_sb[:], bank[B_RT][:], ACT.Copy).then_inc(r_copied, 1)

            def pre_norm(s):
                pre_norm_parts(s)
                pre_norm_r(s)

            def squares(s, name, y, n0=0, n1=KC):
                key = ("post", s)
                last_unit = UNIT[name] + LAST_UNITS[name.rstrip("0123")]
                for c in range(n0, n1):
                    src = y[:, c, :]
                    if c == KC - 1:
                        act.wait_ge(unit_done, last_unit)
                        src = bank[(CHUNK[name] + c) % R][:]
                    else:
                        act.wait_ge(chunk_out, CHUNK[name] + c + 1)
                    if c >= 3:
                        act.wait_ge(sq_added, ADD[key] + c - 2)
                    act.activation((sq_sum if c == 0 else sq[c % 2])[:], src, ACT.Square).then_inc(sq_done, 1)

            def ffn(s, f):
                if s:
                    pre_norm(s)
                c0 = CHUNK[f"up{f}"]
                with act.Fori(0, FC // 2) as i:
                    for p in range(2):
                        act.wait_ge(chunk_out, 4 * i + c0 + 2 * p + 1)
                        act.activation(gate[p][:], gate[p][:], ACT.Silu).then_inc(silu_done, 1)
                squares(s + 1, f"down{f}", y_ffn)

            def copy_rows(key, k, dst, tiles):
                n = TURN[key] + k
                act.wait_ge(turned, n + 1)
                src = bank[B_T[n % 2]][:, 0:P * tiles].rearrange("p (i t) -> p i t", i=tiles)
                act.activation(dst, src, ACT.Copy).then_inc(rows_done, 1)

            def load_strip(phase, k):
                heads, bufs, strip_in, _ = STRIPS[phase]
                src = bass.AP(line_rows.tensor, P * (LINE + 1) * heads[k] + P - 1, [[LINE, P], [1, T]])
                act.dma_start(bufs[k % len(bufs)][:], src).then_inc(strip_in[k % len(bufs)], 16)

            def first_strips(phase):
                for k in range(len(STRIPS[phase][1])):
                    load_strip(phase, k)

            def attention(phase, hooks={}):
                infos, j0 = INFO[phase], JOB0[phase]
                logits, _, probTs = BUFS[phase]
                if phase in STRIPS:
                    heads, bufs, _, size = STRIPS[phase]

                def exp(s):
                    j, info = j0 + s, infos[s]
                    act.wait_ge(logit_done, j + 1)
                    group = first_of(phase, s, size) if phase in STRIPS else None
                    if group:
                        for k in range(size * (group - 1) + len(bufs), size * group + len(bufs)):
                            if k < len(heads):
                                load_strip(phase, k)
                    if s >= N_PROB:
                        act.wait_ge(probT_done, infos[s - N_PROB]["turn"] + 1)
                    prob = probs_of(phase, s)
                    for g, (at, w, _, _) in enumerate(info["parts"]):
                        ins = act.activation(prob[:, at:at + w], logits[s % N_LOGIT][:, at:at + w], ACT.Exp, scale=-1.0,
                                             bias=neg_max[:, j % 8, g:g + 1], accum_out=row_sum[:, j % 8, g:g + 1])
                    ins.then_inc(exp_done, 1)

                def copy(s):
                    info = infos[s]
                    if not info["turns"]:
                        return
                    t = info["turn"]
                    act.wait_ge(probT_done, t + 1)
                    if t >= infos[0]["turn"] + N_PROBT:
                        act.wait_ge(pv_done, t - N_PROBT + 1)
                    w = P * info["blocks"]
                    act.activation(probTs[t % N_PROBT][0:info["rows"], 0:w], bank[B_T[t % 2]][0:info["rows"], 0:w],
                                   ACT.Copy).then_inc(probT_copied, 1)

                def output_leaves(s):
                    f = infos[s]["out"][0]
                    act.wait_ge(pv_done, infos[s]["turn"] + 1)
                    src = bank[B_O[f % 2]][:]
                    if phase == 2:
                        act.activation(diff_o[:, f, :], src, ACT.Copy).then_inc(diff_out, 1)
                        act.activation(diff_sq[:, f, :], src, ACT.Square).then_inc(sub_sq, 1)
                    else:
                        act.activation(h_hi[:, f, :], src, ACT.Copy).then_inc(hi_done, 1)

                for s in range(len(infos) + OUT_AT + 1):
                    if TURN_AT <= s < len(infos) + TURN_AT:
                        copy(s - TURN_AT)
                    if s < len(infos):
                        exp(s)
                    if s > OUT_AT and infos[s - OUT_AT - 1]["ends"]:
                        output_leaves(s - OUT_AT - 1)
                    if s in hooks:
                        hooks[s]()

            def memory(n, split_key):
                act.wait_ge(lo_done, SPLIT[split_key] + (KC if n == 0 else 4))
                act.dma_start(mem_sb[:], a["mem"]).then_inc(aux_in, 16)
                act.wait_ge(aux_in, AUX[f"mem{n}"])
                for c in range(KC):
                    g = G_MEM + KC * n + c
                    act.activation(mem_hi[:, c, :], mem_sb[:, c, :], ACT.Copy, scale=gains[:, g:g + 1]).then_inc(hi_done, 1)
                    if c >= 3:
                        act.wait_ge(sq_added, ADD["mem", n] + c - 2)
                    act.activation((mem_sum if c == 0 else mem_sq[c % 2])[:], mem_sb[:, c, :],
                                   ACT.Square).then_inc(sq_done, 1)

            def memory_r(n):
                act.wait_ge(r_turned, SQ["mem", n]["rt"] + 1)
                act.activation(r_mem[:], bank[B_RT][:, 0:MEM], ACT.Copy).then_inc(r_copied, 1)

            def even_mixer(s):
                pre_norm(s)
                act.dma_start(cmp_w[:], a["cmp_w"]).then_inc(aux_in, 16)
                act.dma_start(cmp_pe[:], a["cmp_pe"]).then_inc(aux_in, 16)
                act.dma_start(ev_causal[:], a["consts"][:, C_CAUSAL:C_CAUSAL + T]).then_inc(aux_in, 16)
                act.wait_ge(lines_out, 32)
                first_strips(0)
                copy_rows("vg", 0, ev_v[:, 2, :, :], NT)
                act.wait_ge(rows_done, V_ROWS["vg"] + 1)
                act.activation(gates[:], ev_v[:, 2, :, DH:DH + 3 * A_HEADS], ACT.Exp, scale=-1.0).then_inc(gate_exp, 1)
                banks = (B_STAT, B_RT, B_T[(TURN["vg"] + 1) % 2])
                for k in range((NT - 1) * IDX_HEADS):
                    i = 1 + k // IDX_HEADS
                    act.wait_ge(idx_done, k + 1)
                    if k >= 2:
                        act.wait_ge(idx_added, k - 1)
                    act.activation(relu[k % 2][:, 0:P * (i + 1)], bank[banks[k % 3]][:, 0:P * (i + 1)],
                                   ACT.Relu).then_inc(relu_done, 1)
                c0 = CHUNK["ev_in"]

                def k_high(n):
                    for half in range(2):
                        act.activation(k_st[n][0][DH * half:DH * half + DH, :], k_rows(n), ACT.Copy).then_inc(k_hi_done, 1)

                act.wait_ge(chunk_out, c0 + KS + 1)
                k_high(0)
                act.wait_ge(idx_added, (NT - 1) * IDX_HEADS)
                k_high(1)
                copy_rows("ev_v", 0, ev_v[:, 0, :, :], NT)
                copy_rows("ev_v", 1, ev_v[:, 1, :, :], NT)
                act.wait_ge(cmp_x_done, 8)
                act.activation(k_st[4][0][:], ev[:, KB, :], ACT.Copy).then_inc(k_hi_done, 1)
                act.wait_ge(cmp_zero, 3)
                act.wait_ge(cmp_done, 1)
                for g in range(2):
                    act.activation(kc[DH * g:DH * g + DH, GC * g:GC * g + N_CMP], bank[4][0:DH, N_CMP * g:N_CMP * g + N_CMP],
                                   ACT.Copy).then_inc(rows_done, 1)
                act.wait_ge(cmp_done, 2)
                act.activation(vcT[:], bank[5][0:DH, 0:2 * N_CMP], ACT.Copy).then_inc(rows_done, 1)
                act.wait_ge(cmp_done, 3)
                for g in range(2):
                    cols = slice(DH * g, DH * g + DH)
                    act.activation(vc[GC * g:GC * g + N_CMP, cols], bank[4][0:N_CMP, P + DH * g:P + DH * g + DH],
                                   ACT.Copy).then_inc(rows_done, 1)
                act.wait_ge(mask_done, NT - 1)
                k_high(2)
                k_high(3)
                attention(0)
                memory(0, "ev_o")
                squares(s + 1, "ev_out", ev_y, 0, 5)
                memory_r(0)
                squares(s + 1, "ev_out", ev_y, 5, KC)

            def cross(s, n):
                pre_norm(s)
                for h in range(X_HEADS):
                    copy_rows(f"xv{n}", h, xv[:, h, :, :], MT)
                attention(1 if n == 0 else 4)
                squares(s + 1, f"xo{n}", x_y)

            def odd_mixer(s):
                pre_norm(s)
                first_strips(2)
                c0 = CHUNK["od_in"]
                for k in range(2):
                    act.wait_ge(chunk_out, c0 + CQ + k + 1)
                    act.activation(sq[k][:], od[:, CQ + k, :], ACT.Square).then_inc(sq_done, 1)
                act.wait_ge(stat_done, SQ["cq", 0]["stat"] + 1)
                act.activation(sq[0][:], od[:, CKV, :], ACT.Square).then_inc(sq_done, 1)
                for k in range(2):
                    act.wait_ge(mla_ready, k + 1)
                    act.activation(cq_hi[:, k, :], od[:, CQ + k, :], ACT.Copy).then_inc(hi_done, 1)
                for h in range(D_HEADS):
                    copy_rows("dv", h, dv[:, h, :, :], NT)
                act.wait_ge(mla_ready, 3)
                act.activation(ckv_hi[:], od[:, CKV, :], ACT.Copy).then_inc(hi_done, 1)
                attention(2)
                act.wait_ge(logit_done, JOB0[3])
                act.dma_start(rope_t[:], a["consts"][:, C_ROPE:C_END].rearrange("p (k t) -> p k t", k=2)).then_inc(aux_in, 16)
                act.dma_start(od_causal[:], a["consts"][:, C_CAUSAL:C_CAUSAL + T]).then_inc(aux_in, 16)
                b0 = CHUNK["uq"]
                for k in range(4):
                    up_ready(act, 1, k)
                    src = bank[(b0 + k) % R]
                    act.activation(mla_q[0:DN, 2 * k, :], src[0:DN, :], ACT.Copy).then_inc(q_nope, 1)
                    act.activation(mla_q[0:DN, 2 * k + 1, :], src[DN:P, :], ACT.Copy).then_inc(chunk_out, 1)
                act.wait_ge(krope_done, 1)
                for i in range(NT):
                    act.activation(mla_v[:, i, :], bank[4 + i][:], ACT.Copy).then_inc(q_nope, 1)
                for k in range(4):
                    up_ready(act, 2, k)
                    act.activation(mla_k[0:DN, 2 * k, :], bank[(b0 + k) % R][0:DN, :], ACT.Copy).then_inc(q_nope, 1)

                def sub_high(h):
                    act.wait_ge(sub_normed, h + 1)
                    act.activation(h_hi[:, 4 + h, :], diff_o[:, h, :], ACT.Copy).then_inc(sub_hi, 1)

                attention(3, hooks={SUB_AT * (h + 1) + 2: lambda h=h: sub_high(h) for h in range(D_HEADS)})
                act.wait_ge(sub_lo, D_HEADS)
                memory(1, "od_o")
                squares(s + 1, "od_out", od_y, 0, 5)
                memory_r(1)
                squares(s + 1, "od_out", od_y, 5, KC)

            act.wait_ge(ones_set, 3)
            act.dma_start(onehot[:], a["onehot"]).then_inc(start_in, 16)
            act.dma_start(table[0:BUCKETS, :], a["table"]).then_inc(start_in, 16)
            act.dma_start(lam_in[:], a["lam"].partition_broadcast(P)).then_inc(start_in, 16)
            act.wait_ge(const_in, 48)
            pre_norm_parts(0)
            act.wait_ge(turned, 1)
            act.activation(lines[:, 0:512], bank[6][0:BIAS_HEADS, :], ACT.Copy).then_inc(rows_done, 1)
            act.activation(lines[:, 512:LINE + 1], bank[7][0:BIAS_HEADS, 0:LINE + 1 - 512], ACT.Copy).then_inc(rows_done, 1)
            act.wait_ge(rows_done, 2)
            act.dma_start(lines_dram, lines[:]).then_inc(lines_out, 16)
            pre_norm_r(0)
            act.wait_ge(dve_done, 2)
            act.activation(lam[:, 3:5], lam[:, 1:3], ACT.Exp).then_inc(lam_exp, 1)
            act.activation(ident_bf[:], ident[:], ACT.Copy).then_inc(lam_exp, 1)
            act.wait_ge(lines_out, 16)
            rows = bass.AP(lines_dram.tensor, 0, [[LINE + 1, BIAS_HEADS], [0, P], [1, LINE + 1]])
            act.dma_start(line_rows, rows).then_inc(lines_out, 16)
            ffn(0, 0)
            even_mixer(1)
            cross(2, 0)
            ffn(3, 1)
            ffn(4, 2)
            odd_mixer(5)
            cross(6, 1)
            ffn(7, 3)

        @block.vector
        def _(dve):
            n_small = [0]

            def small(ins):
                n_small[0] += 1
                ins.then_inc(dve_done, 1)
                dve.wait_ge(dve_done, n_small[0])

            def rsqrt(key, w, d, stats=1, src=None):
                value, half, y = (rs[:, k, 0:w] for k in (0, 2, 3))
                square = rs[:, 1, 0:w]
                if src is None:
                    dve.wait_ge(stat_done, SQ[key]["stat"] + stats)
                    src = bank[B_STAT][:, 0:w]
                small(dve.tensor_scalar(value, src, 1.0 / d, EPS, ALU.mult, ALU.add))
                small(dve.tensor_scalar(y.bitcast(I32), value.bitcast(I32), -0.5, RSQRT_SEED, ALU.mult, ALU.add))
                for k in range(3):
                    small(dve.tensor_tensor(square, y, y, ALU.mult))
                    small(dve.scalar_tensor_tensor(half, square, -0.5, value, ALU.mult, ALU.mult))
                    last = dve.scalar_tensor_tensor(y, half, 1.5, y, ALU.add, ALU.mult)
                    if k < 2:
                        small(last)
                last.then_inc(rsqrt_done, 1)

            def pre_norm(s, c):
                g = G_PRE + KC * s + c
                dve.wait_ge(hi_done, SPLIT[f"pre{s}"] + c + 1)
                dve.scalar_tensor_tensor(h_lo[:, c, :], x[:, c, :], gains[:, g:g + 1], h_hi[:, c, :].bitcast(F32),
                                         ALU.mult, ALU.subtract).then_inc(lo_done, 1)

            def pre_norm_r(s):
                rsqrt(("pre", s), NT, D)
                dve.wait_ge(r_copied, SQ["pre", s]["cp"] + 1)

            def seam(s, y, mem=None):
                rsqrt(("post", s), NT, D)
                dve.wait_ge(r_turned, SQ["post", s]["rt"] + 1)

                def scaled(c):
                    g = G_POST + KC * (s - 1) + c
                    if c >= 2:
                        dve.wait_ge(x_done, X0[s] + c - 1)
                    dve.scalar_tensor_tensor(step[c % 2][:], y[:, c, :], gains[:, g:g + 1], bank[B_RT][:],
                                             ALU.mult, ALU.mult).then_inc(dve_done, 1)
                    n_small[0] += 1

                scaled(0)
                for c in range(KC):
                    dve.wait_ge(dve_done, n_small[0])
                    dve.tensor_tensor(x[:, c, :], x[:, c, :], step[c % 2][:], ALU.add).then_inc(x_done, 1)
                    if c + 1 < KC:
                        scaled(c + 1)
                    if s < 8:
                        pre_norm(s, c)
                    if mem is not None and c < R:
                        for k in range(c, c + 1) if c < R - 1 else range(c, 2 * X_HEADS):
                            leave(f"xkv{mem}", k, k + 1, xkv[:, k, :], r_mem[:])
                if s < 8:
                    pre_norm_r(s)

            def leave(name, c, unit, dst, r):
                dve.wait_ge(unit_done, UNIT[name] + unit)
                b = (CHUNK[name] + c) % R
                dve.tensor_tensor(dst, bank[b][:, 0:r.shape[-1]], r, ALU.mult).then_inc(chunk_out, 1)

            def output_chunks(s, name, y, unit_of, c0=0, c1=KC):
                key = ("post", s)

                def add(c):
                    dve.wait_ge(sq_done, SQ[key]["sq"] + c + 1)
                    if c > 1:
                        dve.wait_ge(sq_added, ADD[key] + c - 1)
                    dve.tensor_tensor(sq_sum[:], sq_sum[:], sq[c % 2][:], ALU.add).then_inc(sq_added, 1)

                for c in range(c0, c1):
                    if c >= 2:
                        add(c - 1)
                    dve.wait_ge(unit_done, UNIT[name] + unit_of(c))
                    if c == KC - 1:
                        dve.wait_ge(sq_done, SQ[key]["sq"] + KC)
                    dve.tensor_copy(y[:, c, :], bank[(CHUNK[name] + c) % R][:]).then_inc(chunk_out, 1)

            def ffn(s, f):
                u0, c0 = UNIT[f"up{f}"], CHUNK[f"up{f}"]
                with dve.Fori(0, FC // 2) as i:
                    for p in range(2):
                        k = 2 * p
                        dve.wait_ge(unit_done, 4 * i + u0 + k + 1)
                        dve.tensor_tensor(gate[p][:], bank[(c0 + k) % R][:], r_sb[:], ALU.mult).then_inc(chunk_out, 1)
                        dve.wait_ge(unit_done, 4 * i + u0 + k + 2)
                        dve.tensor_tensor(up[p][:], bank[(c0 + k + 1) % R][:], r_sb[:], ALU.mult).then_inc(chunk_out, 1)
                        dve.wait_ge(silu_done, 2 * i + FC * f + p + 1)
                        dve.wait_ge(chunk_out, 4 * i + c0 + k + 2)
                        dve.tensor_tensor(up[p][:], gate[p][:], up[p][:], ALU.mult).then_inc(prod_done, 1)
                        dve.wait_ge(prod_done, 2 * i + FC * f + p + 1)
                        dve.tensor_scalar(act_hi[:, 2 * i + p, :], up[p][:], 1.0, None, ALU.mult).then_inc(act_hi_done, 1)
                        dve.wait_ge(act_hi_done, 2 * i + FC * f + p + 1)
                        dve.tensor_tensor(act_lo[:, 2 * i + p, :], up[p][:], act_hi[:, 2 * i + p, :].bitcast(F32),
                                          ALU.subtract).then_inc(act_done, 1)
                output_chunks(s + 1, f"down{f}", y_ffn, lambda c: 3 * (c + 1))
                seam(s + 1, y_ffn)

            def memory(n):
                key = ("mem", n)
                for c in range(KC):
                    g = G_MEM + KC * n + c
                    dve.wait_ge(hi_done, SPLIT[f"mem{n}"] + c + 1)
                    dve.scalar_tensor_tensor(mem_lo[:, c, :], mem_sb[:, c, :], gains[:, g:g + 1],
                                             mem_hi[:, c, :].bitcast(F32), ALU.mult, ALU.subtract).then_inc(lo_done, 1)
                    if c:
                        dve.wait_ge(sq_done, SQ[key]["sq"] + c + 1)
                        if c > 1:
                            dve.wait_ge(sq_added, ADD[key] + c - 1)
                        dve.tensor_tensor(mem_sum[:], mem_sum[:], mem_sq[c % 2][:], ALU.add).then_inc(sq_added, 1)

            def attention(phase, hooks={}):
                infos, j0 = INFO[phase], JOB0[phase]
                logits = BUFS[phase][0]
                banks = B_S[phase]
                n, strips_seen = len(infos), [0]

                def logit(s):
                    j, info = j0 + s, infos[s]
                    if phase in STRIPS:
                        _, bufs, strip_in, _ = STRIPS[phase]
                        for k in range(strips_seen[0], info["strip"] + 1):
                            dve.wait_ge(strip_in[k % len(bufs)], 16 * (k // len(bufs) + 1))
                            strips_seen[0] = k + 1
                    dve.wait_ge(qk_done, j + 1)
                    if s >= N_LOGIT:
                        dve.wait_ge(exp_done, j - N_LOGIT + 1)
                    for g, (at, w, bias, _) in enumerate(info["parts"]):
                        ins = dve.tensor_tensor_reduce(
                            out=logits[s % N_LOGIT][:, at:at + w], in0=bank[banks[s % len(banks)]][:, at:at + w],
                            in1=bias, scale=info["scale"], scalar=3e38, op0=ALU.add, op1=ALU.min,
                            accum_out=neg_max[:, j % 8, g:g + 1])
                    ins.then_inc(logit_done, 1)

                def invert(s):
                    j, k = j0 + s, len(infos[s]["parts"])
                    dve.wait_ge(exp_done, j + 1)
                    dve.reciprocal(coef[:, j % 8, 0:k], row_sum[:, j % 8, 0:k]).then_inc(coef_done, 1)

                def scale(s):
                    j, info, prob = j0 + s, infos[s], probs_of(phase, s)
                    dve.wait_ge(coef_done, j + 1)
                    if phase == 2 and info["turns"]:
                        w = info["w"]
                        small(dve.tensor_tensor(coef[:, j % 8, 0:1], coef[:, j % 8, 0:1], lam[:, 0:1], ALU.mult))
                        dve.wait_ge(scaled, j)
                        dve.scalar_tensor_tensor(prob[:, 0:w], prob[:, 0:w], coef[:, j % 8, 0:1],
                                                 probs_of(phase, s - 1)[:, 0:w], ALU.mult, ALU.add).then_inc(scaled, 1)
                        return
                    for g, (at, w, _, gate_) in enumerate(info["parts"]):
                        out, r = prob[:, at:at + w], coef[:, j % 8, g:g + 1]
                        if gate_ is None:
                            ins = dve.tensor_scalar(out, out, r, None, ALU.mult)
                        else:
                            ins = dve.tensor_scalar(out, out, r, gate_, ALU.mult, ALU.mult)
                    ins.then_inc(scaled, 1)

                def low(s):
                    f = infos[s]["out"][0]
                    dve.wait_ge(hi_done, SPLIT[OUT_KEY[phase]] + f + 1)
                    dve.tensor_tensor(h_lo[:, f, :], bank[B_O[f % 2]][:], h_hi[:, f, :].bitcast(F32),
                                      ALU.subtract).then_inc(lo_done, 1)

                for s in range(n + OUT_AT + 2):
                    if SCALE_AT <= s < n + SCALE_AT:
                        invert(s - SCALE_AT)
                        scale(s - SCALE_AT)
                    if s < n:
                        logit(s)
                    if phase != 2 and s > OUT_AT + 1 and infos[s - OUT_AT - 2]["ends"]:
                        low(s - OUT_AT - 2)
                    if s in hooks:
                        hooks[s]()

            def even_mixer(s):
                out = [0]

                def leave_next():
                    c = out[0]
                    if c < EV_IN:
                        leave("ev_in", c, c + 1, ev[:, c, :], r_sb[:])
                        out[0] += 1

                for _ in range(4):
                    leave_next()
                dve.wait_ge(gate_exp, 1)
                small(dve.tensor_scalar(gates[:], gates[:], 1.0, None, ALU.add))
                small(dve.reciprocal(gates[:], gates[:]))
                first = gates[:, 0, 0:3 * A_HEADS:3]
                small(dve.tensor_scalar(first, first, row_ok[:], None, ALU.mult))
                dve.wait_ge(aux_in, AUX["ev"])
                for k in range((NT - 1) * IDX_HEADS):
                    i, h = 1 + k // IDX_HEADS, k % IDX_HEADS
                    w = P * (i + 1)
                    off = T - w
                    sc = score[i - 1][:, 0:w]
                    dve.wait_ge(relu_done, k + 1)
                    if h:
                        dve.wait_ge(idx_added, k)
                    dve.scalar_tensor_tensor(sc, relu[k % 2][:, 0:w], ev_v[:, 2, i, 88 + h:89 + h],
                                             sc if h else ev_causal[:, off:off + w], ALU.mult,
                                             ALU.add).then_inc(idx_added, 1)
                dve.wait_ge(idx_added, (NT - 1) * IDX_HEADS)
                dve.memset(kc[:], 0.0).then_inc(cmp_zero, 1)
                dve.memset(vc[:], 0.0).then_inc(cmp_zero, 1)
                dve.memset(cmp_prob[:], 0.0).then_inc(cmp_zero, 1)
                tiles_ = [(top8[:, i - 1, :], score[i - 1][:, 0:P * (i + 1)]) for i in range(1, NT)]
                for k in range(TOPK // 8):
                    at = n_small[0]
                    for i, (best, sc) in enumerate(tiles_):
                        if k:
                            dve.wait_ge(dve_done, at - NT + 2 + i)
                        dve.max(best, sc).then_inc(dve_done, 1)
                    for i, (best, sc) in enumerate(tiles_):
                        dve.wait_ge(dve_done, at + 1 + i)
                        dve.match_replace(sc, best, sc, TAKEN).then_inc(dve_done, 1)
                    n_small[0] += 2 * (NT - 1)
                    if k % 3 != 2:
                        leave_next()
                for i, (_, sc) in enumerate(tiles_):
                    dve.wait_ge(dve_done, n_small[0] - NT + 2 + i)
                    dve.tensor_scalar(taken_mask[:, i, 0:P * (i + 2)], sc, TAKEN / 2, NEG, ALU.is_gt,
                                      ALU.mult).then_inc(mask_done, 1)
                for _ in range(EV_IN):
                    leave_next()
                dve.wait_ge(chunk_out, CHUNK["ev_in"] + EV_IN)

                def k_low(n):
                    dve.wait_ge(k_hi_done, {1: 4, 2: 7, 3: 9}[n])
                    e = slice(DH * (n % 2), DH * (n % 2) + DH)
                    for half in range(2):
                        dve.tensor_tensor(k_st[n][1][DH * half:DH * half + DH, :], k_rows(n),
                                          k_st[n][0][e, :].bitcast(F32), ALU.subtract).then_inc(k_lo_done, 1)

                def kb_low():
                    dve.tensor_tensor(k_st[4][1][:], ev[:, KB, :], k_st[4][0][:].bitcast(F32), ALU.subtract).then_inc(k_lo_done, 1)

                attention(0, {0: lambda: k_low(2), 1: lambda: k_low(1), 2: lambda: k_low(3), 6: kb_low})
                memory(0)
                output_chunks(s + 1, "ev_out", ev_y, lambda c: c + 1, 0, R)
                rsqrt(("mem", 0), MT, D)
                output_chunks(s + 1, "ev_out", ev_y, lambda c: c + 1, R, KC)
                dve.wait_ge(r_copied, SQ["mem", 0]["cp"] + 1)
                seam(s + 1, ev_y, 0)

            def cross(s, n):
                for h in range(X_HEADS):
                    leave(f"xq{n}", h, h + 1, xq[:, h, :], r_sb[:])
                attention(1 if n == 0 else 4)
                output_chunks(s + 1, f"xo{n}", x_y, lambda c: c // 2 + 1)
                seam(s + 1, x_y)

            def odd_mixer(s):
                def leave_to(c0, c1):
                    for c in range(c0, c1):
                        leave("od_in", c, c + 1, od[:, c, :], r_sb[:])

                leave_to(0, 8)
                dve.wait_ge(chunk_out, CHUNK["od_in"] + 8)
                for key, d, cs, g0, lo in ((("cq", 0), 2 * P, (CQ, CQ + 1), G_Q, (cq_lo[:, 0, :], cq_lo[:, 1, :])),
                                           (("ckv", 0), P, (CKV,), G_KV, (ckv_lo[:],))):
                    rsqrt(key, NT, d)
                    leave_to(*((8, 12) if key[0] == "cq" else (12, OD_IN)))
                    dve.wait_ge(r_turned, SQ[key]["rt"] + 1)
                    for k, c in enumerate(cs):
                        dve.scalar_tensor_tensor(od[:, c, :], od[:, c, :], gains[:, g0 + k:g0 + k + 1], bank[B_RT][:],
                                                 ALU.mult, ALU.mult).then_inc(mla_ready, 1)
                    for k, c in enumerate(cs):
                        hi = cq_hi[:, k, :] if key[0] == "cq" else ckv_hi[:]
                        dve.wait_ge(hi_done, SPLIT[key[0]] + k + 1)
                        dve.tensor_tensor(lo[k], od[:, c, :], hi.bitcast(F32), ALU.subtract).then_inc(lo_done, 1)
                attention(2)
                rsqrt(("sub", 0), NT * D_HEADS, DV)
                dve.wait_ge(aux_in, AUX["od"])
                e = slice(DN, DN + DR)
                small(dve.tensor_tensor(step[1][e, :], od[0:DR, KR, :], rope_t[0:DR, 0, :], ALU.mult))
                small(dve.tensor_tensor(step[0][e, :], od[DR:2 * DR, KR, :], rope_t[DR:2 * DR, 1, :], ALU.mult))
                dve.tensor_tensor(step[1][e, :], step[1][e, :], step[0][e, :], ALU.add).then_inc(krope_done, 1)
                for k in range(4):
                    up_ready(dve, 0, k)
                    dve.tensor_tensor(rope_x[k][:], bank[(CHUNK["uq"] + k) % R][:], rope_t[:, k % 2, :],
                                      ALU.mult).then_inc(chunk_out, 1)
                dve.wait_ge(chunk_out, CHUNK["uq"] + 4)
                for k in range(4):
                    rows = slice(DR * k, DR * k + DR)
                    dve.tensor_tensor(mla_q[e, 4 + k, :], rope_x[2][rows, :], rope_x[3][rows, :], ALU.add).then_inc(rope_added, 1)
                dve.wait_ge(krope_done, 1)
                dve.tensor_copy(mla_k[e, :, :], step[1][e, :].unsqueeze(1).to_broadcast([DR, C_HEADS, T])).then_inc(mla_ready, 1)
                for k in range(4):
                    up_ready(dve, 2, k)
                    dve.tensor_copy(mla_k[0:DN, 2 * k + 1, :], bank[(CHUNK["uq"] + k) % R][DN:P, :]).then_inc(chunk_out, 1)

                def norm_sub(h):
                    dve.wait_ge(sub_turned, h + 1)
                    dve.wait_ge(diff_out, h + 1)
                    dve.scalar_tensor_tensor(diff_o[:, h, :], diff_o[:, h, :], lam[:, 5:6], bank[B_RT][:],
                                             ALU.mult, ALU.mult).then_inc(sub_normed, 1)

                def sub_low(h):
                    dve.wait_ge(sub_hi, h + 1)
                    dve.tensor_tensor(h_lo[:, 4 + h, :], diff_o[:, h, :], h_hi[:, 4 + h, :].bitcast(F32),
                                      ALU.subtract).then_inc(sub_lo, 1)

                hooks = {SUB_AT * (h + 1) + 1: lambda h=h: norm_sub(h) for h in range(D_HEADS)}
                hooks.update({SUB_AT * (h + 1) + 3: lambda h=h: sub_low(h) for h in range(D_HEADS)})
                attention(3, hooks=hooks)
                memory(1)
                output_chunks(s + 1, "od_out", od_y, lambda c: c + 1, 0, R)
                rsqrt(("mem", 1), MT, D)
                output_chunks(s + 1, "od_out", od_y, lambda c: c + 1, R, KC)
                dve.wait_ge(r_copied, SQ["mem", 1]["cp"] + 1)
                seam(s + 1, od_y, 1)

            dve.wait_ge(start_in, 16 * 3)
            for k in range(2):
                dve.tensor_tensor_reduce(out=lam_pr[:, k, :], in0=lam_in[:, 2 * k, :], in1=lam_in[:, 2 * k + 1, :],
                                         scale=1.0, scalar=0.0, op0=ALU.mult, op1=ALU.add,
                                         accum_out=lam[:, 1 + k:2 + k]).then_inc(dve_done, 1)
                n_small[0] += 1
            dve.wait_ge(const_in, 48)
            for c in range(KC):
                dve.wait_ge(x_in[c], 16)
                pre_norm(0, c)
                if c:
                    dve.wait_ge(sq_done, c + 1)
                    if c > 1:
                        dve.wait_ge(pre_added, c - 1)
                    dve.tensor_tensor(sq_sum[:], sq_sum[:], sq[c % 2][:], ALU.add).then_inc(pre_added, 1)
            pre_norm_r(0)
            dve.wait_ge(lam_exp, 1)
            small(dve.tensor_scalar(lam[:, 0:1], lam[:, 4:5], lam[:, 3:4], LAM_INIT, ALU.subtract, ALU.subtract))
            small(dve.tensor_scalar(lam[:, 5:6], gains[:, G_SUB:G_SUB + 1], 1.0 - LAM_INIT, None, ALU.mult))
            for at_, to in ((0, 1), (3, 5), (7, 8)):
                half = gains[:, G_POST + KC * at_:G_POST + KC * to]
                small(dve.tensor_scalar(half, half, 0.5, None, ALU.mult))
            dve.wait_ge(lines_out, 16)
            ffn(0, 0)
            even_mixer(1)
            cross(2, 0)
            ffn(3, 1)
            ffn(4, 2)
            odd_mixer(5)
            cross(6, 1)
            ffn(7, 3)


def constants():
    c = np.zeros((P, C_END), np.float32)
    c[:, C_ID:C_ID + P] = np.eye(P)
    dist = (T - P) + np.arange(P)[:, None] - np.arange(T)[None, :]
    c[:, C_CAUSAL:C_CAUSAL + T] = np.where(dist < 0, NEG, 0.0)
    half = DR // 2
    inv = np.float32(10000.0) ** (-np.arange(half, dtype=np.float32) / np.float32(half))
    ang = np.arange(T, dtype=np.float32)[None, :] * inv[:, None]
    cos, sin = np.cos(ang), np.sin(ang)
    c[:, C_ROPE:C_ROPE + T] = np.concatenate([cos] * 8)
    c[:, C_ROPE + T:C_END] = np.concatenate([-sin, sin] * 4)
    row_ok = (np.arange(P) >= CMP_LEN - 1).astype(np.float32).reshape(P, 1)
    d = T - 1 - np.arange(LINE + 1)
    near = BUCKETS // 2
    ratio = np.log(np.maximum(d, 1).astype(np.float32) / np.float32(near)) / np.float32(math.log(MAX_DIST / near))
    far = np.minimum(near + (ratio * np.float32(BUCKETS - near)).astype(np.int32), BUCKETS - 1)
    bucket = np.where(d < 0, BUCKETS, np.where(d < near, d, far))
    onehot = np.zeros((BUCKETS + 1, LINE + 1), np.float32)
    onehot[bucket, np.arange(LINE + 1)] = np.where(d < 0, 1.0, DH ** 0.5)
    return c, onehot, row_ok


def tiles(w, kt, cols):
    return w.reshape(kt, P, cols, P).transpose(2, 1, 0, 3).reshape(cols, P, kt * P)


def vectors(g):
    return g.reshape(-1, P).T


def kernel(x, mem, rel_bias_table, norm_pre, norm_post, mem_norm, ffn_wg, ffn_wu, ffn_wd,
           ev_w_in, ev_cmp_pe, ev_cmp_w, ev_w_out, od_w_in, od_q_norm, od_kv_norm, od_w_uq,
           od_w_ukv, od_lambda, od_subln, od_w_out, xa_wq, xa_wkv, xa_wo):
    import concourse.bacc as bacc
    from concourse.bass_utils import run_bass_kernel_spmd

    consts, onehot, row_ok = constants()
    ins = {"consts": consts, "onehot": onehot, "row_ok": row_ok}
    ins["x"] = x[0].T.reshape(KC, P, T).transpose(1, 0, 2)
    ins["mem"] = mem[0].T.reshape(KC, P, MEM).transpose(1, 0, 2)
    ins["table"] = rel_bias_table
    ins["lam"] = od_lambda[0]
    ins["gains"] = np.concatenate([vectors(norm_pre), vectors(norm_post), vectors(mem_norm), vectors(od_q_norm),
                                   vectors(od_kv_norm), vectors(od_subln)], 1)
    wg, wu, wd = (w.reshape((2 * DEPTH,) + w.shape[2:]) for w in (ffn_wg, ffn_wu, ffn_wd))
    ins["w_up"] = np.stack([np.stack([tiles(wg[f], KC, FC), tiles(wu[f], KC, FC)], 1).reshape(2 * FC, P, D)
                            for f in range(2 * DEPTH)])
    ins["w_down"] = np.stack([tiles(wd[f], FC, KC) for f in range(2 * DEPTH)])
    w = ev_w_in[0]
    sizes = (A_HEADS * DH, 12 * DH, 3 * A_HEADS, B_HEADS * DH, DH, DH, IDX_HEADS * IDX_DH, IDX_DH, IDX_HEADS)
    at = np.cumsum((0,) + sizes)
    qa, kva, ga, qb, kb, vb, iq, ik, iw = (w[:, at[n]:at[n + 1]] for n in range(9))
    pair = [qa[:, DH * h:DH * h + DH] for c in range(4) for h in (c, c + 4)]
    cols = [iq, ik, ik, ik, ik, vb, ga, iw, ik, kb, kb, qb, kva] + pair
    ins["w_ev_in"] = tiles(np.concatenate(cols, 1), KC, EV_IN)
    w = ev_w_out[0]
    rows = [w[DH * h:DH * h + DH] for c in range(4) for h in (c, c + 4)] + [w[A_HEADS * DH:]]
    ins["w_ev_out"] = tiles(np.concatenate(rows, 0), KC, KC)
    w = ev_cmp_w[0].reshape(2, CMP_LEN // 2, 2, DH, DH)
    ins["cmp_w"] = w.transpose(2, 3, 0, 1, 4).reshape(P, 2, CMP_LEN // 2, DH)
    ins["cmp_pe"] = np.concatenate([ev_cmp_pe[0].transpose(2, 0, 1)] * 2)
    w = od_w_in[0]
    cq, ckv, kr, rest = w[:, :256], w[:, 256:384], w[:, 384:416], w[:, 416:]
    cols = [cq, ckv, kr, kr[:, 16:], kr[:, :16], kr, kr, rest]
    ins["w_od_in"] = tiles(np.concatenate(cols, 1), KC, OD_IN)
    ins["w_od_out"] = tiles(od_w_out[0], KC, KC)
    q = od_w_uq[0].reshape(256, C_HEADS, DN + DR)
    rot, swapped = q[:, :, DN:], np.concatenate([q[:, :, DN + DR // 2:], q[:, :, DN:DN + DR // 2]], 2)
    q = np.concatenate([rot[:, :4], swapped[:, :4], rot[:, 4:], swapped[:, 4:]], 1).reshape(256, 4 * P), q[:, :, :DN].reshape(256, 4 * P)
    ins["w_uq"] = tiles(np.concatenate(q, 1), 2, C_HEADS).reshape(2, 4, P, 2 * P).transpose(0, 2, 1, 3).reshape(2, P, D)
    kv = od_w_ukv[0].reshape(P, C_HEADS, 2, DN).transpose(0, 2, 1, 3)
    ins["w_ukv"] = kv.reshape(1, P, D)
    ins["w_xq"] = np.stack([tiles(w, KC, X_HEADS) for w in xa_wq])
    ins["w_xkv"] = np.stack([tiles(w, KC, 2 * X_HEADS) for w in xa_wkv])
    wo = np.stack([tiles(w, X_HEADS, KC) for w in xa_wo])
    ins["w_xo"] = wo.reshape(DEPTH, KC // 2, 2, P, 512).transpose(0, 1, 3, 2, 4).reshape(DEPTH, KC // 2, P, D)

    nc = bacc.Bacc("TRN2", target_bir_lowering=False, num_devices=1)
    arrays, aps = {}, {}
    for name, value in ins.items():
        arrays[f"in_{name}"] = np.ascontiguousarray(value)
        aps[name] = nc.dram_tensor(f"in_{name}", value.shape, F32, kind="ExternalInput").ap()
    aps["out"] = nc.dram_tensor("out", (P, KC, T), F32, kind="ExternalOutput").ap()
    build(nc, aps)
    r = run_bass_kernel_spmd(nc, [arrays], core_ids=[0])
    out = np.asarray(r.results[0]["out"])
    return out.transpose(1, 0, 2).reshape(D, T).T[None]
```
